# Optimizing a Trainium2 kernel written in Bass

```python
import jax, jax.numpy as jnp
from jax import lax
import numpy as np
import math

D_MODEL = 1024
BATCH = 1
SEQ = 256
DEPTH = 1

GRID_W = 64
CTX_LEN = 256
ATTN_WIDTH = 512
N_HEADS = 8
N_KV_HEADS = 2
HEAD_DIM = ATTN_WIDTH // N_HEADS
KV_REP = N_HEADS // N_KV_HEADS
KV_WIDTH = N_KV_HEADS * HEAD_DIM
CONV_WIDTH = D_MODEL - ATTN_WIDTH
CONV_HEADS = 8
CONV_K = 3
MIX_WIDTH = ATTN_WIDTH + CONV_WIDTH
IN_COLS = ATTN_WIDTH + 2 * KV_WIDTH + 3 * CONV_WIDTH
ROPE_THETA = 10000.0
ROPE_AXIS_DIM = HEAD_DIM // 2
ROPE_FREQS = ROPE_AXIS_DIM // 2
Q_BLOCK = 128
N_GROUPS = 4
EXPERTS_PER_GROUP = 8
N_EXPERTS = N_GROUPS * EXPERTS_PER_GROUP
TOP_K = 2
D_EXPERT = 768
MOE_BLOCK = 128
N_MOD = 6
EPS = 1e-6


def rms_norm(x, g):
    xf = x.astype(jnp.float32)
    y = xf * lax.rsqrt(jnp.mean(xf * xf, axis=-1, keepdims=True) + EPS)
    return (y * g.astype(jnp.float32)).astype(x.dtype)

def head_rms(x, g, n_heads):
    xs = x.reshape(*x.shape[:-1], n_heads, -1)
    return rms_norm(xs, g.reshape(n_heads, -1)).reshape(x.shape)

def modulation(cond, w_mod, b_mod):
    mod = jax.nn.silu(cond) @ w_mod + b_mod
    return jnp.split(mod[..., None, :], N_MOD, axis=-1)

def axial_rope_tables(n_tokens, dtype):
    rows = n_tokens // GRID_W
    row_idx = jnp.repeat(jnp.arange(rows, dtype=jnp.float32), GRID_W)
    col_idx = jnp.tile(jnp.arange(GRID_W, dtype=jnp.float32), rows)
    inv_freq = ROPE_THETA ** (-jnp.arange(0, ROPE_AXIS_DIM, 2, dtype=jnp.float32) / ROPE_AXIS_DIM)
    ang = jnp.stack([row_idx[:, None] * inv_freq, col_idx[:, None] * inv_freq], axis=1)
    return jnp.cos(ang).astype(dtype), jnp.sin(ang).astype(dtype)

def apply_axial_rope(x, cos, sin):
    xs = x.reshape(*x.shape[:-1], 2, 2, ROPE_FREQS)
    x1, x2 = xs[..., 0, :], xs[..., 1, :]
    c, s = cos[:, None], sin[:, None]
    return jnp.stack([x1 * c - x2 * s, x1 * s + x2 * c], axis=-2).reshape(x.shape)

def in_proj(h, w_in, q_g, k_g):
    z = h @ w_in
    b, s = h.shape[:2]
    cuts = [ATTN_WIDTH, ATTN_WIDTH + KV_WIDTH, ATTN_WIDTH + 2 * KV_WIDTH,
            ATTN_WIDTH + 2 * KV_WIDTH + CONV_WIDTH, ATTN_WIDTH + 2 * KV_WIDTH + 2 * CONV_WIDTH]
    q, k, v, gb, gc, u = jnp.split(z, cuts, axis=-1)
    q = rms_norm(q.reshape(b, s, N_HEADS, HEAD_DIM), q_g)
    k = rms_norm(k.reshape(b, s, N_KV_HEADS, HEAD_DIM), k_g)
    v = v.reshape(b, s, N_KV_HEADS, HEAD_DIM)
    return q, k, v, gb, gc, u

def attend(q, k, v):
    s = jnp.einsum('bqgrd,bkgd->bgrqk', q, k, preferred_element_type=jnp.float32) * (HEAD_DIM ** -0.5)
    p = jax.nn.softmax(s, axis=-1).astype(v.dtype)
    return jnp.einsum('bgrqk,bkgd->bqgrd', p, v)

def latent_attention(q, k_all, v_all):
    b, s = q.shape[:2]
    nb = s // Q_BLOCK
    qb = q.reshape(b, nb, Q_BLOCK, N_KV_HEADS, KV_REP, HEAD_DIM).transpose(1, 0, 2, 3, 4, 5)
    ob = lax.map(lambda qi: attend(qi, k_all, v_all), qb)
    return ob.transpose(1, 0, 2, 3, 4, 5).reshape(b, s, ATTN_WIDTH)

def short_conv(gb, gc, u, conv_w):
    v = gc * u
    vp = jnp.pad(v, ((0, 0), (1, 1), (0, 0)))
    y = conv_w[0] * vp[:, :-2] + conv_w[1] * vp[:, 1:-1] + conv_w[2] * vp[:, 2:]
    return gb * y

def merge_out(a, cv, attn_g, conv_g, w_out):
    return jnp.concatenate([head_rms(a, attn_g, N_HEADS), head_rms(cv, conv_g, CONV_HEADS)], axis=-1) @ w_out

def hier_moe(h, w_group, w_router, w_gate, w_up, w_down):
    d = h.shape[-1]
    ht = h.reshape(-1, d)
    n = ht.shape[0]
    g_prob = jax.nn.softmax((ht @ w_group).astype(jnp.float32), axis=-1)
    g_sel = jnp.argmax(g_prob, axis=-1)
    g_w = jnp.take_along_axis(g_prob, g_sel[:, None], axis=1)[:, 0]
    e_logits = (ht @ w_router).astype(jnp.float32).reshape(n, N_GROUPS, EXPERTS_PER_GROUP)
    e_logits = jnp.take_along_axis(e_logits, g_sel[:, None, None], axis=1)[:, 0]
    e_prob = jax.nn.softmax(e_logits, axis=-1)
    top_p, top_i = lax.top_k(e_prob, TOP_K)
    top_p = top_p / jnp.sum(top_p, axis=-1, keepdims=True)
    wts = (g_w[:, None] * top_p).reshape(-1)
    eid = (g_sel[:, None] * EXPERTS_PER_GROUP + top_i).reshape(-1).astype(jnp.int32)
    tok = jnp.repeat(jnp.arange(n, dtype=jnp.int32), TOP_K)
    m = eid.shape[0]
    order = jnp.argsort(eid)
    s_e, s_tok, s_w = eid[order], tok[order], wts[order]
    counts = jnp.bincount(eid, length=N_EXPERTS).astype(jnp.int32)
    starts = jnp.cumsum(counts) - counts
    padded = ((counts + MOE_BLOCK - 1) // MOE_BLOCK) * MOE_BLOCK
    pstarts = jnp.cumsum(padded) - padded
    pends = pstarts + padded
    dest = pstarts[s_e] + (jnp.arange(m, dtype=jnp.int32) - starts[s_e])
    p_rows = m + N_EXPERTS * MOE_BLOCK
    n_blk = p_rows // MOE_BLOCK
    xbuf = jnp.zeros((p_rows, d), h.dtype).at[dest].set(ht[s_tok])
    blk_start = jnp.arange(n_blk, dtype=jnp.int32) * MOE_BLOCK
    blk_e = jnp.minimum(jnp.searchsorted(pends, blk_start, side='right'), N_EXPERTS - 1)

    def expert_block(args):
        xb, e = args
        return (jax.nn.silu(xb @ w_gate[e]) * (xb @ w_up[e])) @ w_down[e]

    ybuf = lax.map(expert_block, (xbuf.reshape(n_blk, MOE_BLOCK, d), blk_e)).reshape(p_rows, d)
    y = ybuf[dest] * s_w[:, None].astype(h.dtype)
    return jax.ops.segment_sum(y, s_tok, num_segments=n).reshape(h.shape)

def trunk_layer(x, ctx, c, c_ctx, cos, sin, w_mod, b_mod, norm1_g, w_in, q_norm_g, k_norm_g,
                conv_w, attn_out_g, conv_out_g, w_out, norm2_g, w_group, w_router, w_gate, w_up,
                w_down, update_ctx):
    sh1, sc1, gt1, sh2, sc2, gt2 = modulation(c, w_mod, b_mod)
    csh1, csc1, cgt1, csh2, csc2, cgt2 = modulation(c_ctx, w_mod, b_mod)
    hx = rms_norm(x, norm1_g) * (1.0 + sc1) + sh1
    hc = rms_norm(ctx, norm1_g) * (1.0 + csc1) + csh1
    qx, kx, vx, bx, cx, ux = in_proj(hx, w_in, q_norm_g, k_norm_g)
    qc, kc, vc, bc, cc, uc = in_proj(hc, w_in, q_norm_g, k_norm_g)
    qx = apply_axial_rope(qx, cos, sin)
    kx = apply_axial_rope(kx, cos, sin)
    k_all = jnp.concatenate([kc, kx], axis=1)
    v_all = jnp.concatenate([vc, vx], axis=1)
    ax = latent_attention(qx, k_all, v_all)
    convx = short_conv(bx, cx, ux, conv_w)
    x_new = x + gt1 * merge_out(ax, convx, attn_out_g, conv_out_g, w_out)
    hx2 = rms_norm(x_new, norm2_g) * (1.0 + sc2) + sh2
    x_new = x_new + gt2 * hier_moe(hx2, w_group, w_router, w_gate, w_up, w_down)
    if update_ctx:
        b = ctx.shape[0]
        ac = attend(qc.reshape(b, -1, N_KV_HEADS, KV_REP, HEAD_DIM), kc, vc).reshape(b, -1, ATTN_WIDTH)
        convc = short_conv(bc, cc, uc, conv_w)
        ctx = ctx + cgt1 * merge_out(ac, convc, attn_out_g, conv_out_g, w_out)
        hc2 = rms_norm(ctx, norm2_g) * (1.0 + csc2) + csh2
        ctx = ctx + cgt2 * hier_moe(hc2, w_group, w_router, w_gate, w_up, w_down)
    return x_new, ctx

def first_inputs(seed: int = 0) -> dict:
    key = jax.random.key(seed)
    ks = jax.random.split(key, 21)
    f32 = jnp.float32
    L, D = DEPTH, D_MODEL

    def nrm(k, shape, scale):
        return jax.random.normal(k, shape, f32) * scale

    return {
        "x": nrm(ks[0], (BATCH, SEQ, D), 1.0),
        "c": nrm(ks[1], (BATCH, D), 1.0),
        "ctx": nrm(ks[2], (BATCH, CTX_LEN, D), 1.0),
        "c_ctx": nrm(ks[3], (D,), 1.0),
        "w_mod": nrm(ks[4], (L, D, N_MOD * D), 0.5 * D ** -0.5),
        "b_mod": nrm(ks[5], (L, N_MOD * D), 0.02),
        "norm1_g": 1.0 + nrm(ks[6], (L, D), 0.02),
        "w_in": nrm(ks[7], (L, D, IN_COLS), D ** -0.5),
        "q_norm_g": 1.0 + nrm(ks[8], (L, HEAD_DIM), 0.02),
        "k_norm_g": 1.0 + nrm(ks[9], (L, HEAD_DIM), 0.02),
        "conv_w": nrm(ks[10], (L, CONV_K, CONV_WIDTH), CONV_K ** -0.5),
        "attn_out_g": 1.0 + nrm(ks[11], (L, ATTN_WIDTH), 0.02),
        "conv_out_g": 1.0 + nrm(ks[12], (L, CONV_WIDTH), 0.02),
        "w_out": nrm(ks[13], (L, MIX_WIDTH, D), MIX_WIDTH ** -0.5),
        "norm2_g": 1.0 + nrm(ks[14], (L, D), 0.02),
        "w_group": nrm(ks[15], (L, D, N_GROUPS), D ** -0.5),
        "w_router": nrm(ks[16], (L, D, N_EXPERTS), D ** -0.5),
        "w_gate": nrm(ks[17], (L, N_EXPERTS, D, D_EXPERT), D ** -0.5),
        "w_up": nrm(ks[18], (L, N_EXPERTS, D, D_EXPERT), D ** -0.5),
        "w_down": nrm(ks[19], (L, N_EXPERTS, D_EXPERT, D), D_EXPERT ** -0.5),
        "final_g": 1.0 + nrm(ks[20], (D,), 0.02),
    }

def first_block(x, c, ctx, c_ctx, w_mod, b_mod, norm1_g, w_in, q_norm_g, k_norm_g, conv_w,
              attn_out_g, conv_out_g, w_out, norm2_g, w_group, w_router, w_gate, w_up, w_down,
              final_g):
    cos, sin = axial_rope_tables(x.shape[1], x.dtype)
    for i in range(DEPTH):
        x, ctx = trunk_layer(x, ctx, c, c_ctx, cos, sin, w_mod[i], b_mod[i], norm1_g[i], w_in[i],
                             q_norm_g[i], k_norm_g[i], conv_w[i], attn_out_g[i], conv_out_g[i],
                             w_out[i], norm2_g[i], w_group[i], w_router[i], w_gate[i], w_up[i],
                             w_down[i], update_ctx=(i < DEPTH - 1))
    return rms_norm(x, final_g)


CHUNK = 64
D_FF = 2816
FFN_RES_WEIGHT = 0.5
ADA_SUBLAYERS = 3
ADA_WIDTH = ADA_SUBLAYERS * 3 * D_MODEL
MLA_HEADS = 8
MLA_Q_RANK = 256
MLA_KV_RANK = 128
MLA_NOPE = 64
MLA_ROPE = 32
MLA_V = 64
CA_HEADS = 8
CA_HEAD_DIM = 64
CA_LEFT_CHUNKS = 8
CA_BAND = CA_LEFT_CHUNKS + 1
MAX_REL_DIST = 256
CA_WIDTH = CA_HEADS * CA_HEAD_DIM
MLA_OUT_WIDTH = MLA_HEADS * MLA_V
W_IN_COLS = MLA_Q_RANK + MLA_KV_RANK + MLA_ROPE + 3 * CA_WIDTH + 2 * D_MODEL
NEG_INF = -1e30


def rmsnorm(x, g):
    xf = x.astype(jnp.float32)
    y = xf * lax.rsqrt(jnp.mean(xf * xf, axis=-1, keepdims=True) + EPS)
    return (y * g.astype(jnp.float32)).astype(x.dtype)

def modulate(h, shift, scale):
    return h * (1 + scale[:, None, :]) + shift[:, None, :]

def swiglu(h, w_in, w_out):
    gu = h @ w_in
    g, u = jnp.split(gu, 2, axis=-1)
    return (jax.nn.silu(g) * u) @ w_out

def rope(x, cos, sin):
    half = x.shape[-1] // 2
    x1, x2 = x[..., :half], x[..., half:]
    return jnp.concatenate([x1 * cos - x2 * sin, x1 * sin + x2 * cos], axis=-1).astype(x.dtype)

def mla_attention(q_lat, kv_lat, k_pe_raw, positions, q_norm, w_uq, kv_norm, w_ukv):
    B, S = q_lat.shape[:2]
    cq = rmsnorm(q_lat, q_norm)
    q = (cq @ w_uq).reshape(B, S, MLA_HEADS, MLA_NOPE + MLA_ROPE)
    q_nope, q_pe = q[..., :MLA_NOPE], q[..., MLA_NOPE:]
    ckv = rmsnorm(kv_lat, kv_norm)
    kv = (ckv @ w_ukv).reshape(B, S, MLA_HEADS, MLA_NOPE + MLA_V)
    k_nope, v = kv[..., :MLA_NOPE], kv[..., MLA_NOPE:]

    inv_freq = ROPE_THETA ** (-jnp.arange(0, MLA_ROPE, 2, dtype=jnp.float32) / MLA_ROPE)
    ang = positions.astype(jnp.float32)[..., None] * inv_freq
    cos, sin = jnp.cos(ang), jnp.sin(ang)
    q_pe = rope(q_pe, cos[:, :, None, :], sin[:, :, None, :])
    k_pe = rope(k_pe_raw, cos, sin)

    scale = (MLA_NOPE + MLA_ROPE) ** -0.5
    key_chunk = jnp.arange(S) // CHUNK

    def block(qi):
        start = qi * Q_BLOCK
        qn = lax.dynamic_slice_in_dim(q_nope, start, Q_BLOCK, axis=1)
        qp = lax.dynamic_slice_in_dim(q_pe, start, Q_BLOCK, axis=1)
        s = (jnp.einsum('bqhd,bkhd->bhqk', qn, k_nope)
             + jnp.einsum('bqhd,bkd->bhqk', qp, k_pe)).astype(jnp.float32) * scale
        q_chunk = (start + jnp.arange(Q_BLOCK)) // CHUNK
        mask = key_chunk[None, :] <= q_chunk[:, None]
        s = jnp.where(mask[None, None], s, NEG_INF)
        p = jax.nn.softmax(s, axis=-1).astype(v.dtype)
        return jnp.einsum('bhqk,bkhd->bqhd', p, v)

    o = lax.map(block, jnp.arange(S // Q_BLOCK))
    return jnp.moveaxis(o, 0, 1).reshape(B, S, MLA_OUT_WIDTH)

def chunk_attention(q, k, v, rel_bias):
    B, S = q.shape[:2]
    NC = S // CHUNK
    KB = CA_BAND * CHUNK
    q = q.reshape(B, NC, CHUNK, CA_HEADS, CA_HEAD_DIM)
    pad = ((0, 0), (CA_LEFT_CHUNKS, 0), (0, 0), (0, 0), (0, 0))
    kpad = jnp.pad(k.reshape(B, NC, CHUNK, CA_HEADS, CA_HEAD_DIM), pad)
    vpad = jnp.pad(v.reshape(B, NC, CHUNK, CA_HEADS, CA_HEAD_DIM), pad)
    idx = jnp.arange(NC)[:, None] + jnp.arange(CA_BAND)[None, :]
    kb = kpad[:, idx].reshape(B, NC, KB, CA_HEADS, CA_HEAD_DIM)
    vb = vpad[:, idx].reshape(B, NC, KB, CA_HEADS, CA_HEAD_DIM)

    s = jnp.einsum('bnqhd,bnkhd->bnhqk', q, kb).astype(jnp.float32) * CA_HEAD_DIM ** -0.5
    rel = CA_LEFT_CHUNKS * CHUNK + jnp.arange(CHUNK)[:, None] - jnp.arange(KB)[None, :]
    rel = jnp.clip(rel, -MAX_REL_DIST, MAX_REL_DIST) + MAX_REL_DIST
    bias = jnp.transpose(rel_bias[rel], (2, 0, 1)).astype(jnp.float32)
    s = s + bias[None, None]
    key_chunk = jnp.arange(NC)[:, None] - CA_LEFT_CHUNKS + jnp.arange(KB)[None, :] // CHUNK
    valid = key_chunk >= 0
    s = jnp.where(valid[None, :, None, None, :], s, NEG_INF)
    p = jax.nn.softmax(s, axis=-1).astype(vb.dtype)
    o = jnp.einsum('bnhqk,bnkhd->bnqhd', p, vb)
    return o.reshape(B, S, CA_WIDTH)

def second_inputs(seed: int = 0) -> dict:
    key = jax.random.key(seed)
    ks = jax.random.split(key, 24)
    L, D = DEPTH, D_MODEL

    def w(k, shape, fan_in, mult=1.0):
        return jax.random.normal(k, shape, jnp.float32) * (mult * fan_in ** -0.5)

    def gain(k, shape):
        return 1.0 + 0.1 * jax.random.normal(k, shape, jnp.float32)

    offsets = jax.random.randint(ks[2], (BATCH, 1), 0, 64, dtype=jnp.int32) * CHUNK
    positions = offsets + jnp.arange(SEQ, dtype=jnp.int32)[None, :]
    return {
        "x": jax.random.normal(ks[0], (BATCH, SEQ, D), jnp.float32),
        "c": jax.random.normal(ks[1], (BATCH, D), jnp.float32),
        "positions": positions,
        "w_ada": w(ks[3], (L, D, ADA_WIDTH), D),
        "b_ada": 0.1 * jax.random.normal(ks[4], (L, ADA_WIDTH), jnp.float32),
        "ffn1_norm": gain(ks[5], (L, D)),
        "ffn1_w_in": w(ks[6], (L, D, 2 * D_FF), D),
        "ffn1_w_out": w(ks[7], (L, D_FF, D), D_FF),
        "mix_norm": gain(ks[8], (L, D)),
        "w_in": w(ks[9], (L, D, W_IN_COLS), D),
        "mla_q_norm": gain(ks[10], (L, MLA_Q_RANK)),
        "mla_w_uq": w(ks[11], (L, MLA_Q_RANK, MLA_HEADS * (MLA_NOPE + MLA_ROPE)), MLA_Q_RANK),
        "mla_kv_norm": gain(ks[12], (L, MLA_KV_RANK)),
        "mla_w_ukv": w(ks[13], (L, MLA_KV_RANK, MLA_HEADS * (MLA_NOPE + MLA_V)), MLA_KV_RANK),
        "rel_bias": 0.5 * jax.random.normal(ks[14], (L, 2 * MAX_REL_DIST + 1, CA_HEADS), jnp.float32),
        "w_branch_a": w(ks[15], (L, MLA_OUT_WIDTH, D), MLA_OUT_WIDTH),
        "w_branch_b": w(ks[16], (L, CA_WIDTH, D), CA_WIDTH),
        "w_out": w(ks[17], (L, D, D), D),
        "ffn2_norm": gain(ks[18], (L, D)),
        "ffn2_w_in": w(ks[19], (L, D, 2 * D_FF), D),
        "ffn2_w_out": w(ks[20], (L, D_FF, D), D_FF),
        "final_norm": gain(ks[21], (D,)),
    }

def second_block(x, c, positions, w_ada, b_ada, ffn1_norm, ffn1_w_in, ffn1_w_out,
              mix_norm, w_in, mla_q_norm, mla_w_uq, mla_kv_norm, mla_w_ukv, rel_bias,
              w_branch_a, w_branch_b, w_out, ffn2_norm, ffn2_w_in, ffn2_w_out, final_norm):
    c_act = jax.nn.silu(c)
    splits = []
    acc = 0
    for width in (MLA_Q_RANK, MLA_KV_RANK, MLA_ROPE, CA_WIDTH, CA_WIDTH, CA_WIDTH, D_MODEL):
        acc += width
        splits.append(acc)

    for l in range(DEPTH):
        ada = c_act @ w_ada[l] + b_ada[l]
        (sh1, sc1, g1, sh2, sc2, g2, sh3, sc3, g3) = jnp.split(ada, 3 * ADA_SUBLAYERS, axis=-1)

        h = modulate(rmsnorm(x, ffn1_norm[l]), sh1, sc1)
        x = x + FFN_RES_WEIGHT * g1[:, None, :] * swiglu(h, ffn1_w_in[l], ffn1_w_out[l])

        h = modulate(rmsnorm(x, mix_norm[l]), sh2, sc2)
        z = h @ w_in[l]
        q_lat, kv_lat, k_pe_raw, ca_q, ca_k, ca_v, gate_a, gate_b = jnp.split(z, splits, axis=-1)
        y_a = mla_attention(q_lat, kv_lat, k_pe_raw, positions, mla_q_norm[l], mla_w_uq[l],
                            mla_kv_norm[l], mla_w_ukv[l]) @ w_branch_a[l]
        B, S = ca_q.shape[:2]
        shp = (B, S, CA_HEADS, CA_HEAD_DIM)
        y_b = chunk_attention(ca_q.reshape(shp), ca_k.reshape(shp), ca_v.reshape(shp),
                              rel_bias[l]) @ w_branch_b[l]
        merged = jax.nn.sigmoid(gate_a) * y_a + jax.nn.sigmoid(gate_b) * y_b
        x = x + g2[:, None, :] * (merged @ w_out[l])

        h = modulate(rmsnorm(x, ffn2_norm[l]), sh3, sc3)
        x = x + FFN_RES_WEIGHT * g3[:, None, :] * swiglu(h, ffn2_w_in[l], ffn2_w_out[l])

    return rmsnorm(x, final_norm)


def setup_inputs(seed=0):
    out = dict(first_inputs(seed))
    for name, value in second_inputs(seed + 1).items():
        if name != "x":
            out[name + "_2"] = value
    return out


def reference(
    x, c, ctx, c_ctx, w_mod, b_mod, norm1_g, w_in, q_norm_g, k_norm_g, conv_w, attn_out_g,
    conv_out_g, w_out, norm2_g, w_group, w_router, w_gate, w_up, w_down, final_g, c_2,
    positions_2, w_ada_2, b_ada_2, ffn1_norm_2, ffn1_w_in_2, ffn1_w_out_2, mix_norm_2, w_in_2,
    mla_q_norm_2, mla_w_uq_2, mla_kv_norm_2, mla_w_ukv_2, rel_bias_2, w_branch_a_2,
    w_branch_b_2, w_out_2, ffn2_norm_2, ffn2_w_in_2, ffn2_w_out_2, final_norm_2,
):
    x = first_block(
        x, c, ctx, c_ctx, w_mod, b_mod, norm1_g, w_in, q_norm_g, k_norm_g, conv_w, attn_out_g,
        conv_out_g, w_out, norm2_g, w_group, w_router, w_gate, w_up, w_down, final_g,
    )
    return second_block(
        x, c_2, positions_2, w_ada_2, b_ada_2, ffn1_norm_2, ffn1_w_in_2, ffn1_w_out_2,
        mix_norm_2, w_in_2, mla_q_norm_2, mla_w_uq_2, mla_kv_norm_2, mla_w_ukv_2, rel_bias_2,
        w_branch_a_2, w_branch_b_2, w_out_2, ffn2_norm_2, ffn2_w_in_2, ffn2_w_out_2,
        final_norm_2,
    )


_drawn_inputs = setup_inputs


def setup_inputs(seed=0):
    import zlib

    import numpy as np

    out = dict(_drawn_inputs(seed))
    spreads = {}
    factors = {'norm1_g': 4.949,
     'q_norm_g': 8.0,
     'k_norm_g': 8.0,
     'attn_out_g': 6.32,
     'conv_out_g': 8.0,
     'norm2_g': 4.715,
     'final_g': 2.836,
     'mla_q_norm_2': 8.0,
     'mla_kv_norm_2': 2.829,
     'rel_bias_2': 4.384,
     'ffn2_norm_2': 3.848}
    for name, (base, spread) in spreads.items():
        noise = np.random.default_rng([zlib.crc32(name.encode()), seed]).standard_normal(out[name].shape)
        drawn = base * np.exp(spread * noise) if base else spread * noise
        out[name] = __import__('jax').numpy.asarray(drawn.astype(out[name].dtype))
    for name, factor in factors.items():
        out[name] = (out[name] * factor).astype(out[name].dtype)
    return out
```

```python
import concourse.bass as bass
from concourse import mybir
from contextlib import ExitStack

F32 = mybir.dt.float32
BF16 = mybir.dt.bfloat16
I32 = mybir.dt.int32
U32 = mybir.dt.uint32
ALU = mybir.AluOpType
ACT = mybir.ActivationFunctionType
AX_X = mybir.AxisListType.X

P = 128
T = 256
D = 1024
KD = D // P
EPS = 1e-6
N_GROUPS, GROUP_SIZE = 4, 8
N_EXPERTS = N_GROUPS * GROUP_SIZE
D_EXPERT = 768
HALF_E = D_EXPERT // 2
SLOTS = 64
PASSES = T // SLOTS
D_FF = 2816
FF_CHUNK = 256
FF_LOOPS = (D_FF // FF_CHUNK - 1) // 2
CHUNK = 64
NO_SLOT = 10000.0
NEG = -1e30
ROPE_SCALE_2 = 96 ** -0.5
TWO_PI = 6.283185307179586
PI_A, PI_B = 6.28125, 0.0019350051879882812
PI_C = TWO_PI - PI_A - PI_B

CONST_COLS = [("ident", 128), ("ones", 128), ("heads64", 128), ("rot_axial", 128), ("rot_half", 128),
              ("reverse", 128), ("before", 128), ("slot", 128), ("expert_id", 32), ("group_rank", 4),
              ("eps", 1), ("inv_freq", 1), ("pad", 2), ("axial_cos", 256), ("axial_sin", 256)]


def const_offsets():
    at, out = 0, {}
    for name, width in CONST_COLS:
        out[name] = (at, width)
        at += width
    return out, at


ROWS_A = {"b_mod": 0, "norm1_g": 48, "norm2_g": 56, "final_g": 64, "c": 72, "c_ctx": 80, "q_norm_g": 88,
          "k_norm_g": 89, "attn_out_g": 90, "conv_out_g": 94, "conv_w": 98}
N_ROWS_A = 110
ROWS_B = {"b_ada": 0, "ffn1_norm": 72, "mix_norm": 80, "ffn2_norm": 88, "final_norm": 96, "c": 104,
          "mla_q_norm": 112, "mla_kv_norm": 114}
N_ROWS_B = 115

JOBS = (["rows_a", "rows_b"] + [f"x_turn{i}" for i in range(4)] + [f"ctx_turn{i}" for i in range(4)]
        + ["sum_x", "sum_ctx"] + [f"mod{i}" for i in range(4)]
        + ["z_k", "z_v", "col_gt1a", "z_q0", "z_q1", "col_gt1b", "z_gb0", "z_gb1", "col_sh2a",
           "z_gc0", "z_gc1", "col_sh2b", "z_u0", "z_u1", "col_sc2a"]
        + [f"qk_sum{i}" for i in range(3)] + [f"qk_rot{i}" for i in range(3)] + ["col_sc2b", "col_gt2a"]
        + [f"attn_o{i}" for i in range(4)] + ["col_gt2b"] + [f"head_sum{i}" for i in range(4)]
        + [f"merge{i}" for i in range(4)] + ["sum_n2", "logits"] + [f"h2_turn{i}" for i in range(4)]
        + ["positions", "bias_turn"]
        + [f"col_ada{i}" for i in range(4)] + ["sum_final", "sum_ffn1"]
        + ["sum_mix", "z_lat", "z_kv", "z_caq0", "z_caq1", "col_ada14", "z_cak0", "z_cak1", "col_ada15", "z_cav0", "z_cav1",
           "lat_sum", "col_ada16", "z_ga0", "z_ga1", "z_ga2", "z_ga3", "col_ada17", "z_gb0_2", "z_gb1_2", "z_gb2_2", "z_gb3_2"]
        + [f"mla_q{i}" for i in range(4)] + [f"mla_k{i}" for i in range(4)] + ["mla_v0", "mla_v1"]
        + [f"pe_rot{i}" for i in range(4)] + ["kpe_rot"]
        + [f"mla_o{i}" for i in range(4)] + [f"ca_o{i}" for i in range(4)]
        + [f"branch_{ab}{i}" for i in range(4) for ab in "ab"] + [f"out2_{i}" for i in range(4)]
        + ["sum_ffn2", "sum_last"] + [f"y_turn{i}" for i in range(4)])
JOB = {name: j for j, name in enumerate(JOBS)}
assert len(JOB) == len(JOBS)

RING = 6
SLOT_W = 4096
PRE = ([(f"mod{i}", f"mod{i}") for i in range(4)]
       + [("w_kv", "z_v"), ("gt1a", 0), ("w_q", "z_q1"), ("gt1b", 1), ("w_gb", "z_gb1"), ("sh2a", 2), ("w_gc", "z_gc1"),
          ("sh2b", 3), ("w_u", "z_u1"), ("sc2a", 4), ("sc2b", 5), ("gt2a", 6), ("gt2b", 7), ("w_out0", "merge1"),
          ("w_out1", "merge3")])
MID = ([("ada14", 22), ("w2_lat", "z_kv"), ("w2_caq", "z_caq1"), ("w2_cak", "z_cak1"), ("ada15", 23), ("w2_cav", "z_cav1"),
        ("ada16", 24), ("w2_ga0", "z_ga1"), ("w2_ga1", "z_ga3"), ("ada17", 25), ("w2_gb0", "z_gb1_2"),
        ("w2_gb1", "z_gb3_2"), ("mla_up", "mla_v1"), ("w_branch_a", "branch_a3"), ("w_branch_b", "branch_b3"),
        ("w_out2_0", "out2_1"), ("w_out2_1", "out2_3")])


def ring_places():
    place, loads = {}, [0] * RING
    for part, items in (("pre", PRE), ("ada", [(f"ada{i}", 8 + i) for i in range(4)]), ("mid", MID)):
        for at, (name, _) in enumerate(items):
            s = at % RING
            if name == "w_out1":
                s = 4
            if name != "mla_up":
                loads[s] += 1
            place[(part, name)] = (s, loads[s])
    return place


def mixed_blocks_kernel(nc, ins, out):
    C, n_const = const_offsets()
    PLACE = ring_places()

    with ExitStack() as ctx:
        def sb(name, shape, dt=F32):
            return ctx.enter_context(nc.sbuf_tensor(name, shape, dt))

        sems = {}

        def sem(name):
            if name not in sems:
                sems[name] = ctx.enter_context(nc.semaphore(name))
            return sems[name]

        consts = sb("consts", [P, n_const])
        rows_a = sb("rows_a", [N_ROWS_A, P])
        rows_b = sb("rows_b", [N_ROWS_B, P])
        cols_a = sb("cols_a", [P, N_ROWS_A])
        cols_b = sb("cols_b", [P, N_ROWS_B])
        xT = sb("xT", [P, KD, T])
        hT = sb("hT", [P, KD, T])
        squares = sb("squares", [P, KD, T])
        mixT = sb("mixT", [P, KD, T])
        h_rows = sb("h_rows", [P, 2, D])
        rstd = sb("rstd", [P, 2 * T])
        small = sb("small", [P, 2048])
        cond = sb("cond", [P, KD, 2])
        cond2 = sb("cond2", [P, KD])
        mod = sb("mod", [P, 6 * KD])
        mod_ctx = sb("mod_ctx", [P, 2 * KD])
        ada = sb("ada", [P, 9 * KD])
        gains = sb("gains", [P, 3 * KD])
        mod_acc = sb("mod_acc", [P, 2, 512])
        stats = sb("stats", [P, 3, 3, 16])
        router = sb("router", [P, KD, 36])
        route = sb("route", [P, 2, 168])
        picked = sb("picked", [P, 2, 40])
        picked_i = sb("picked_i", [P, 2, 8], U32)
        busiest = sb("busiest", [1, 1], I32)
        zeros = sb("zeros", [P, 512], BF16)
        ARENA = 9 * SLOT_W
        arena = sb("arena", [P, ARENA])

        def ring(slot):
            return arena[:, slot * SLOT_W:(slot + 1) * SLOT_W]

        def ring_w(part, name):
            return ring(PLACE[(part, name)][0]).rearrange("p (k n) -> p k n", k=KD)

        EW = KD * D_EXPERT

        def expert_w(u):
            base = 3 * EW * u
            gate = arena[:, base:base + EW].rearrange("p (k n) -> p k n", k=KD)
            up = arena[:, base + EW:base + 2 * EW].rearrange("p (k n) -> p k n", k=KD)
            down = arena[:, base + 2 * EW:base + 3 * EW].rearrange("p (k n) -> p k n", k=6)
            return gate, up, down

        temp_at = [RING * SLOT_W]

        def temp(*shape):
            n = 1
            for s in shape:
                n *= s
            a = arena[:, temp_at[0]:temp_at[0] + n]
            temp_at[0] += n
            assert temp_at[0] <= ARENA
            if len(shape) == 1:
                return a
            names = "abc"[:len(shape)]
            spec = {names[i]: shape[i] for i in range(len(shape))}
            return a.rearrange(f"p ({' '.join(names)}) -> p {' '.join(names)}", **spec)

        logits, assigned = route[:, :, 0:36], route[:, :, 36:68]
        places, weights = route[:, :, 68:101], route[:, :, 101:134]
        route_tmp = route[:, :, 134:166]
        rel_bias_rows = sb("rel_bias_rows", [P, 4, 8])
        half_gate = sb("half_gate", [P, KD])
        x_rows, ctx_rows = temp(2, D), temp(2, D)
        ctxT = h_rows[:, :, :].rearrange("p b (k t) -> p (b k) t", t=T)
        ctx_squares = x_rows.rearrange("p b (k t) -> p (b k) t", t=T)
        gate_aT, gate_bT = ctxT, mixT[:, :, :]
        qk = temp(6, T)
        v1 = temp(4, P)
        gate_b = temp(4, T)
        conv_in = temp(4, T + 2)
        conv_out = temp(4, T)
        qk_tmp = temp(6, T)
        temp_at[0] = RING * SLOT_W
        mla_q, mla_k = temp(8, T), temp(8, T)
        mla_v = temp(2, 512)
        ca_q, ca_k, ca_v = temp(4, T), temp(4, T), temp(2, 512)
        ca_bias = temp(3072)
        bias_early = ca_bias[:, 0:8 * P].rearrange("p (h k) -> p h k", h=8)
        bias_late = ca_bias[:, 8 * P:24 * P].rearrange("p (h k) -> p h k", h=8)
        latT = small[:, 0:3 * T].rearrange("p (c t) -> p c t", c=3)
        pe_tmp = small[:, 768:768 + 512]
        angle = squares[:, 0:5, :]
        bias_rows = small[0:8, 1536:2048]
        rope_cs = sb("rope_cs", [P, 2, T])
        turns = squares[:, 5, :].bitcast(I32)
        probs = small[:, 0:1024].rearrange("p (b k) -> p b k", b=2)
        probsT = small[:, 1024:2048].rearrange("p (b n) -> p b n", b=2)
        pick = mixT[:, 0, 0:2 * SLOTS].rearrange("p (b s) -> p b s", b=2)
        pick_w = mixT[:, 1, :].rearrange("p (b s) -> p b s", b=2)
        xeT = mixT[:, 2:4, :].rearrange("p a t -> p (a t)").rearrange("p (k s) -> p k s", k=KD)
        gate_act = mixT[:, 4:6, :].rearrange("p a t -> p (a t)")[:, 0:HALF_E]
        hidden = mixT[:, 6:8, :].rearrange("p a t -> p (a t)")[:, 0:HALF_E]
        hiddenT = small[:, 0:HALF_E].rearrange("p (c s) -> p c s", c=3)
        y_e = small[:, 512:1024]
        pick_wT = small[:, 1024:1536].rearrange("p (b t) -> p b t", b=2)
        silu_g = small[:, 0:512].rearrange("p (b t) -> p b t", b=2)
        ff_act = small[:, 512:1024].rearrange("p (b t) -> p b t", b=2)

        bank = [ctx.enter_context(nc.psum_tensor(f"bank{i}", [P, 512], F32)) for i in range(8)]
        bias_scratch = nc.dram_tensor("bias_scratch", (8, 512), F32, kind="Internal").ap()

        def K(name):
            at, width = C[name]
            return consts[:, at:at + width]

        def col_a(name, i=0):
            return cols_a[:, ROWS_A[name] + i:ROWS_A[name] + i + 1]

        def col_b(name, i=0):
            return cols_b[:, ROWS_B[name] + i:ROWS_B[name] + i + 1]

        def job_bank(name):
            return bank[JOB[name] % 4]

        def job_wide(name):
            return job_bank(name)[:, :].rearrange("p (a t) -> p a t", a=2)

        SET = {"n1": 0, "c1": 1, "n2": 0, "ffn1": 1, "mix": 2, "ffn2": 0}

        def gain(key, k):
            return gains[:, SET[key] * KD + k:SET[key] * KD + k + 1]

        def attention_1():
            for h in range(8):
                g = 64 * (h // 4)
                for qb in range(2):
                    yield dict(job=f"attn_o{h // 2}", last=(h % 2 == 1 and qb == 1), col=64 * (h % 2), qb=qb, keys=512,
                               q=[qk[g:g + 64, h % 4, qb * P:qb * P + P]],
                               k=[qk[g:g + 64, 4:6, :].rearrange("p a t -> p (a t)")],
                               v=[v1[:, b, g:g + 64] for b in range(4)], mask=False)

        def attention_mla():
            for h in range(8):
                for qb in range(2):
                    n = (qb + 1) * P
                    yield dict(job=f"mla_o{h // 2}", last=(h % 2 == 1 and qb == 1), col=64 * (h % 2), qb=qb, keys=n,
                               q=[mla_q[0:96, h, qb * P:qb * P + P]], k=[mla_k[0:96, h, 0:n]],
                               v=[mla_v[:, b, 64 * h:64 * h + 64] for b in range(qb + 1)], mask=True)

        def attention_ca():
            for h in range(8):
                p = 64 * (h % 2)
                for qb in range(2):
                    n = (qb + 1) * P
                    bias = bias_late[:, h, :] if qb else bias_early[:, h, :]
                    yield dict(job=f"ca_o{h // 2}", last=(h % 2 == 1 and qb == 1), col=p, qb=qb, keys=n,
                               q=[ca_q[p:p + 64, h // 2, qb * P:qb * P + P], K("reverse")],
                               k=[ca_k[p:p + 64, h // 2, 0:n], bias],
                               v=[ca_v[:, b, 64 * h:64 * h + 64] for b in range(qb + 1)], mask=True)

        ATTENTIONS = {"at1": (0, list(attention_1()), 0.125), "mla": (1, list(attention_mla()), ROPE_SCALE_2),
                      "ca": (2, list(attention_ca()), 1.0)}
        ATT_OUT = {"at1": lambda c: mixT[:, c, :], "mla": lambda c: squares[:, c, :], "ca": lambda c: squares[:, 4 + c, :]}

        block = ctx.enter_context(nc.Block())

        def wait_item_read(eng, reader):
            if isinstance(reader, int):
                eng.wait_ge(sem("mod_acc_step"), 8 * (reader + 1))
            else:
                eng.wait_ge(sem("job_ready"), JOB[reader] + 1)

        def chunked(ap, lo, hi):
            return ap[:, lo:hi].rearrange("(k p) n -> p k n", p=P)

        @block.sync
        def _(sp):
            readers = {}

            def load(part, name, src, reader, width=512, k=KD):
                slot, use = PLACE[(part, name)]
                if slot in readers:
                    wait_item_read(sp, readers[slot])
                dst = ring(slot).rearrange("p (k n) -> p k n", k=k)[:, :, 0:width]
                sp.dma_start(dst, src).then_inc(sem(f"ring_full{slot}"), 16)
                readers[slot] = reader

            sp.dma_start(x_rows, ins["x"][0].rearrange("(b p) d -> p b d", p=P)).then_inc(sem("x_loaded"), 16)
            sp.dma_start(ctx_rows, ins["ctx"][0].rearrange("(b p) d -> p b d", p=P)).then_inc(sem("ctx_loaded"), 16)
            w_mod, w_in, w_out = ins["w_mod"][0], ins["w_in"][0], ins["w_out"][0]
            seg = {"gt1a": 2048, "gt1b": 2560, "sh2a": 3072, "sh2b": 3584, "sc2a": 4096, "sc2b": 4608, "gt2a": 5120, "gt2b": 5632}
            win = {"w_q": (0, 512), "w_kv": (512, 256), "w_gb": (768, 512), "w_gc": (1280, 512), "w_u": (1792, 512)}
            for name, reader in PRE:
                if name in win:
                    at, width = win[name]
                    load("pre", name, chunked(w_in, at, at + width), reader, width)
                elif name.startswith("w_out"):
                    at = 512 * int(name[-1])
                    load("pre", name, chunked(w_out, at, at + 512), reader)
                else:
                    at = seg[name] if name in seg else 512 * int(name[-1])
                    load("pre", name, chunked(w_mod, at, at + 512), reader)

            w_gate, w_up, w_down = ins["w_gate"][0], ins["w_up"][0], ins["w_down"][0]

            def load_gate_up(u, e):
                gate, up, _ = expert_w(u)
                sp.dma_start(gate, w_gate[bass.ds(e, 1)].rearrange("a (k p) n -> p (a k) n", p=P))\
                  .then_inc(sem(f"gate_full{u}"), 16)
                sp.dma_start(up, w_up[bass.ds(e, 1)].rearrange("a (k p) n -> p (a k) n", p=P))\
                  .then_inc(sem(f"up_full{u}"), 16)

            def load_down(u, e):
                _, _, down = expert_w(u)
                sp.dma_start(down, w_down[bass.ds(e, 1)].rearrange("a (k p) n -> p (a k) n", p=P))\
                  .then_inc(sem(f"down_full{u}"), 16)

            def load_expert(u, e, done):
                sp.wait_ge(sem("gate_up_done"), done)
                load_gate_up(u, e)
                sp.wait_ge(sem("down_done"), done)
                load_down(u, e)

            for s in range(3):
                wait_item_read(sp, readers[s])
            load_gate_up(0, 0)
            for s in range(3, RING):
                wait_item_read(sp, readers[s])
            readers.clear()
            load_down(0, 0)
            sp.wait_ge(sem("mg_ready"), 1)
            load_gate_up(1, 1)
            load_down(1, 1)
            with sp.Fori(1, N_EXPERTS // 2) as it:
                for u in range(2):
                    load_expert(u, it * 2 + u, it * 2 + u - 1)
            sp.wait_ge(sem("busiest_ready"), 1)
            most = sp.value_load(busiest[0:1, 0:1], min_val=0, max_val=T)
            with sp.If(most > SLOTS):
                with sp.Fori(1, PASSES) as ps:
                    with sp.Fori(0, N_EXPERTS // 2) as it:
                        for u in range(2):
                            load_expert(u, it * 2 + u, ps * N_EXPERTS + it * 2 + u - 1)
                sp.wait_ge(sem("gate_up_done"), PASSES * N_EXPERTS)
                sp.wait_ge(sem("down_done"), PASSES * N_EXPERTS)

            w_ada = ins["w_ada_2"][0]
            sp.wait_ge(sem("gate_up_done"), N_EXPERTS - 1)
            sp.wait_ge(sem("down_done"), N_EXPERTS - 1)
            for i in range(4):
                load("ada", f"ada{i}", chunked(w_ada, 512 * i, 512 * i + 512), 8 + i)

            def load_ff_in(slot, w, c, key):
                dst = ring(slot).rearrange("p (k g n) -> p k g n", k=KD, g=2)
                for g in range(2):
                    sp.dma_start(dst[:, :, g, :], w[:, bass.ds(c * FF_CHUNK + g * D_FF, FF_CHUNK)]
                                 .rearrange("(k p) n -> p k n", p=P)).then_inc(sem(f"{key}_in_full{slot}"), 16)

            def load_ff_out(slot, w, c, key):
                dst = ring(slot)[:, 0:2 * D].rearrange("p (k n) -> p k n", k=2)
                sp.dma_start(dst, w[bass.ds(c * FF_CHUNK, FF_CHUNK), :].rearrange("(k p) n -> p k n", p=P))\
                  .then_inc(sem(f"{key}_out_full{slot}"), 16)

            def feed_forward(key, w_in_ff, w_out_ff, with_ada):
                for s in (2, 3):
                    wait_item_read(sp, readers[s])
                load_ff_in(2, w_in_ff, 0, key)
                load_ff_out(3, w_out_ff, 0, key)
                for s in (0, 1):
                    wait_item_read(sp, readers[s])
                if with_ada:
                    sp.wait_ge(sem("experts_done"), 1)
                with sp.Fori(0, FF_LOOPS) as it:
                    sp.wait_ge(sem(f"{key}_gate_up_done"), it * 4 + 1)
                    load_ff_in(0, w_in_ff, it * 2 + 1, key)
                    sp.wait_ge(sem(f"{key}_down_done"), it * 4 + 1)
                    load_ff_out(1, w_out_ff, it * 2 + 1, key)
                    sp.wait_ge(sem(f"{key}_gate_up_done"), it * 4 + 2)
                    load_ff_in(2, w_in_ff, it * 2 + 2, key)
                    sp.wait_ge(sem(f"{key}_down_done"), it * 4 + 2)
                    load_ff_out(3, w_out_ff, it * 2 + 2, key)
                    if with_ada:
                        for u in range(2):
                            sp.wait_ge(sem("mod_acc_step"), it * 16 + 8 * (11 + u))
                            sp.dma_start(ring(4 + u).rearrange("p (k n) -> p k n", k=KD),
                                         w_ada[:, bass.ds(it * 1024 + (4 + u) * 512, 512)]
                                         .rearrange("(k p) n -> p k n", p=P)).then_inc(sem(f"ada_full{4 + u}"), 16)
                sp.wait_ge(sem(f"{key}_sum_done"), 1)
                readers.clear()

            feed_forward("ffn1", ins["ffn1_w_in_2"][0], ins["ffn1_w_out_2"][0], True)
            w_in2 = ins["w_in_2"][0]
            w2 = {"w2_lat": (0, 416), "w2_caq": (416, 512), "w2_cak": (928, 512), "w2_cav": (1440, 512),
                  "w2_ga0": (1952, 512), "w2_ga1": (2464, 512), "w2_gb0": (2976, 512), "w2_gb1": (3488, 512)}
            sp.wait_ge(sem("mod_acc_step"), 8 * 22)
            for name, reader in MID:
                if name.startswith("ada"):
                    i = int(name[3:])
                    load("mid", name, chunked(w_ada, 512 * i, 512 * i + 512), reader)
                elif name == "mla_up":
                    slot, _ = PLACE[("mid", name)]
                    wait_item_read(sp, readers[slot])
                    sp.dma_start(ring(slot)[:, 0:1536].rearrange("p (k n) -> p k n", k=2),
                                 ins["mla_w_uq_2"][0].rearrange("(k p) n -> p k n", p=P)).then_inc(sem("w_uq_full"), 16)
                    sp.dma_start(ring(slot)[:, 1536:2560], ins["mla_w_ukv_2"][0]).then_inc(sem("w_ukv_full"), 16)
                    readers[slot] = reader
                elif name.startswith("w_branch"):
                    load("mid", name, chunked(ins[name + "_2"][0], 0, D), reader, D, 4)
                elif name.startswith("w_out2"):
                    at = 512 * int(name[-1])
                    load("mid", name, chunked(ins["w_out_2"][0], at, at + 512), reader)
                else:
                    at, width = w2[name]
                    load("mid", name, chunked(w_in2, at, at + width), reader, width)
            feed_forward("ffn2", ins["ffn2_w_in_2"][0], ins["ffn2_w_out_2"][0], False)
            sp.wait_ge(sem("job_emptied"), len(JOBS))
            sp.dma_start(out[0].rearrange("(b p) d -> p b d", p=P), h_rows[:, :, :]).then_inc(sem("stored"), 16)
            sp.wait_ge(sem("stored"), 16)

        @block.gpsimd
        def _(pool):
            n_step = [0]

            def step(instruction):
                n_step[0] += 1
                instruction.then_inc(sem("pool_step"), 1)
                pool.wait_ge(sem("pool_step"), n_step[0])

            pool.wait_ge(sem("conv_in_ready"), 1)
            for tap in range(3):
                for c in range(4):
                    w = col_a("conv_w", 4 * tap + c)
                    dst = conv_out[:, c, :] if tap == 0 else mixT[:, 4 + c, :]
                    i = nc.gpsimd.tensor_scalar(dst, conv_in[:, c, tap:tap + T], w, 0.0, ALU.mult, ALU.add)
                step(i)
                if tap:
                    step(nc.gpsimd.tensor_tensor(conv_out, conv_out, mixT[:, 4:8, :], ALU.add))
            nc.gpsimd.tensor_tensor(mixT[:, 4:8, :], conv_out, gate_b, ALU.mult).then_inc(sem("conv_done"), 1)
            pool.wait_ge(sem("job_emptied"), JOB["bias_turn"] + 1)
            pool.dma_start(bias_scratch, bias_rows).then_inc(sem("bias_stored"), 16)
            pool.wait_ge(sem("bias_stored"), 16)
            pool.wait_ge(sem("experts_done"), 1)
            for tile, first in ((bias_early, 129), (bias_late, 1)):
                src = bass.AP(bias_scratch.tensor, first, [[1, P], [512, 8], [1, tile.shape[2]]])
                pool.dma_start(tile, src).then_inc(sem("bias_loaded"), 16)


        @block.scalar
        def _(act):
            n_step = [0]

            def step(instruction):
                n_step[0] += 1
                instruction.then_inc(sem("act_step"), 1)
                act.wait_ge(sem("act_step"), n_step[0])

            def vec_rows(ap):
                return ap.rearrange("(r n) -> r n", n=P)

            act.dma_start(consts[:, :], ins["shape_constants"]).then_inc(sem("consts_loaded"), 16)
            a_loads = [(rows_a[0:48, :], vec_rows(ins["b_mod"][0]))]
            for name, src in (("norm1_g", ins["norm1_g"][0]), ("norm2_g", ins["norm2_g"][0]), ("final_g", ins["final_g"]),
                              ("c", ins["c"][0]), ("c_ctx", ins["c_ctx"]), ("attn_out_g", ins["attn_out_g"][0]),
                              ("conv_out_g", ins["conv_out_g"][0])):
                r = ROWS_A[name]
                src = vec_rows(src)
                a_loads.append((rows_a[r:r + src.shape[0], :], src))
            for name in ("q_norm_g", "k_norm_g"):
                r = ROWS_A[name]
                for half in range(2):
                    a_loads.append((rows_a[r:r + 1, 64 * half:64 * half + 64], ins[name]))
            a_loads.append((rows_a[ROWS_A["conv_w"]:N_ROWS_A, :], ins["conv_w"][0].rearrange("k (c n) -> (k c) n", n=P)))
            for dst, src in a_loads:
                act.dma_start(dst, src).then_inc(sem("rows_a_loaded"), 16)
            b_loads = []
            for name, src in (("b_ada", "b_ada_2"), ("ffn1_norm", "ffn1_norm_2"), ("mix_norm", "mix_norm_2"),
                              ("ffn2_norm", "ffn2_norm_2"), ("c", "c_2"), ("mla_q_norm", "mla_q_norm_2"),
                              ("mla_kv_norm", "mla_kv_norm_2")):
                r = ROWS_B[name]
                src = vec_rows(ins[src][0])
                b_loads.append((rows_b[r:r + src.shape[0], :], src))
            b_loads.append((rows_b[96:104, :], vec_rows(ins["final_norm_2"])))
            for dst, src in b_loads:
                act.dma_start(dst, src).then_inc(sem("rows_b_loaded"), 16)
            act.dma_start(router[:, :, 0:4], ins["w_group"][0].rearrange("(k p) n -> p k n", p=P))\
               .then_inc(sem("router_loaded"), 16)
            act.dma_start(router[:, :, 4:36], ins["w_router"][0].rearrange("(k p) n -> p k n", p=P))\
               .then_inc(sem("router_loaded"), 16)
            act.dma_start(turns[64:96, :], ins["positions_2"][0].partition_broadcast(32)).then_inc(sem("positions_loaded"), 16)
            for b in range(4):
                act.dma_start(rel_bias_rows[:, b, :], ins["rel_bias_2"][0][385 - P * b:513 - P * b, :])\
                   .then_inc(sem("rel_bias_loaded"), 16)

            act.wait_ge(sem("job_emptied"), 1)
            for i, name in enumerate(("c", "c_ctx")):
                r = ROWS_A[name]
                ins_ = nc.scalar.activation(cond[:, :, i], cols_a[:, r:r + KD], ACT.Silu)
                ins_.then_inc(sem("cond_ready"), 1)
            act.wait_ge(sem("job_emptied"), 2)
            nc.scalar.activation(cond2[:, :], cols_b[:, ROWS_B["c"]:ROWS_B["c"] + KD], ACT.Silu).then_inc(sem("cond_ready"), 1)

            def norm_squares(key, src, dst, source, value=1):
                act.wait_ge(sem(source), value)
                nc.scalar.activation(dst, src, ACT.Square).then_inc(sem(f"{key}_squares"), 1)

            def norm_root(key, job, ap):
                act.wait_ge(sem("job_emptied"), JOB[job] + 1)
                nc.scalar.activation(ap, ap, ACT.Sqrt, bias=K("eps")[0:ap.shape[0], :]).then_inc(sem(f"{key}_root"), 1)

            act.wait_ge(sem("angles_ready"), 1)
            nc.scalar.activation(rope_cs[64:96, :, :], angle[64:96, 2:4, :], ACT.Sin).then_inc(sem("rope_ready"), 1)
            act.wait_ge(sem("rope_ready"), 1)

            def attention(key):
                index, instances, scale = ATTENTIONS[key]
                n = len(instances)
                for i in range(n + 1):
                    if i < n:
                        it = instances[i]
                        act.wait_ge(sem(f"{key}_negmax"), i + 1)
                        nc.scalar.activation(probs[:, i % 2, 0:it["keys"]], bank[4 + i % 2][:, 0:it["keys"]], ACT.Exp,
                                             bias=stats[:, index, 0, i:i + 1], scale=scale,
                                             accum_out=stats[:, index, 1, i:i + 1]).then_inc(sem(f"{key}_exp"), 1)
                    if i >= 1:
                        j = i - 1
                        act.wait_ge(sem(f"{key}_turned"), j + 1)
                        w = instances[j]["keys"]
                        nc.scalar.activation(probsT[:, j % 2, 0:w], bank[6 + j % 2][:, 0:w], ACT.Copy)\
                          .then_inc(sem(f"{key}_probsT"), 1)

            norm_squares("n1", xT[:, :, :], squares[:, :, :], "job_emptied", JOB["x_turn3"] + 1)
            norm_squares("c1", ctxT, ctx_squares, "job_emptied", JOB["ctx_turn3"] + 1)
            norm_root("n1", "sum_x", rstd[:, 0:T])
            norm_root("c1", "sum_ctx", rstd[:, T:2 * T])
            norm_squares("qk", qk, squares[:, 0:6, :], "job_emptied", JOB["z_q1"] + 1)
            norm_root("qk", "qk_sum2", qk_tmp)
            attention("at1")
            act.wait_ge(sem("conv_done"), 1)
            norm_squares("mg", mixT[:, :, :], squares[:, :, :], "job_emptied", JOB["attn_o3"] + 1)
            norm_root("mg", "head_sum3", h_rows[:, :, :])
            norm_squares("n2", xT[:, :, :], squares[:, :, :], "job_emptied", JOB["merge3"] + 1)
            norm_root("n2", "sum_n2", rstd[:, 0:T])
            act.wait_ge(sem("router_max"), 2)
            for b in range(2):
                nc.scalar.activation(picked[:, b, 4:8], route[:, b, 0:4], ACT.Exp, bias=picked[:, b, 0:1],
                                     accum_out=picked[:, b, 1:2]).then_inc(sem("group_exp"), 1)
            act.wait_ge(sem("router_top"), 2)
            for b in range(2):
                nc.scalar.activation(picked[:, b, 2:3], picked[:, b, 17:18], ACT.Exp, bias=picked[:, b, 3:4])\
                  .then_inc(sem("second_exp"), 1)

            def expert_in(count):
                act.wait_ge(sem("gathered"), count)
                nc.scalar.activation(xeT, bank[6][:, :].rearrange("p (k s) -> p k s", k=KD), ACT.Copy)\
                  .then_inc(sem("xe_ready"), 1)

            def expert_steps(n, prep):
                act.wait_ge(sem("gate_up_done"), n)
                nc.scalar.activation(gate_act, bank[4][:, 0:HALF_E], ACT.Silu).then_inc(sem("gate_act_ready"), 1)
                expert_in(prep)
                act.wait_ge(sem("hidden_turned"), n)
                nc.scalar.activation(hiddenT, bank[5][:, 0:HALF_E].rearrange("p (c s) -> p c s", c=3), ACT.Copy)\
                  .then_inc(sem("hiddenT_ready"), 1)
                act.wait_ge(sem("down_done"), n)
                nc.scalar.activation(y_e, bank[6][:, :], ACT.Copy).then_inc(sem("y_ready"), 1)

            expert_in(1)
            with act.Fori(0, N_EXPERTS // 2) as it:
                for u in range(2):
                    expert_steps(it * 2 + u + 1, it * 2 + u + 2)
            act.wait_ge(sem("busiest_ready"), 1)
            most = act.value_load(busiest[0:1, 0:1], min_val=0, max_val=T)
            with act.If(most > SLOTS):
                with act.Fori(1, PASSES) as ps:
                    expert_in(ps * (N_EXPERTS + 1) + 1)
                    with act.Fori(0, N_EXPERTS // 2) as it:
                        for u in range(2):
                            expert_steps(ps * N_EXPERTS + it * 2 + u + 1, ps * (N_EXPERTS + 1) + it * 2 + u + 2)

            norm_squares("fin1", xT[:, :, :], squares[:, :, :], "y_moe_read")
            norm_root("fin1", "sum_final", rstd[:, 0:T])

            def feed_forward(key):
                def one(s, parity):
                    act.wait_ge(sem(f"{key}_gate_up_done"), s)
                    nc.scalar.activation(silu_g[:, parity, :], bank[4 + parity][:, 0:T], ACT.Silu)\
                      .then_inc(sem(f"{key}_silu"), 1)
                one(1, 0)
                one(2, 1)
                with act.Fori(0, FF_LOOPS) as it:
                    for j in range(4):
                        one(it * 4 + j + 3, j % 2)

            norm_squares("ffn1", xT[:, :, :], squares[:, :, :], "fin1_ready")
            norm_root("ffn1", "sum_ffn1", rstd[:, 0:T])
            feed_forward("ffn1")
            norm_squares("mix", xT[:, :, :], squares[:, :, :], "ffn1_sum_read")
            norm_root("mix", "sum_mix", rstd[:, 0:T])
            norm_squares("lat", latT, squares[:, 0:3, :], "job_emptied", JOB["z_kv"] + 1)
            norm_root("lat", "lat_sum", rstd[:, :])
            for gate, job in ((gate_aT, "z_ga3"), (gate_bT, "z_gb3_2")):
                act.wait_ge(sem("job_emptied"), JOB[job] + 1)
                nc.scalar.activation(gate, gate, ACT.Sigmoid).then_inc(sem("gates_ready"), 1)
            act.wait_ge(sem("bias_stored"), 16)
            attention("mla")
            attention("ca")
            norm_squares("ffn2", xT[:, :, :], squares[:, :, :], "job_emptied", JOB["out2_3"] + 1)
            norm_root("ffn2", "sum_ffn2", rstd[:, 0:T])
            feed_forward("ffn2")
            norm_squares("last", xT[:, :, :], squares[:, :, :], "ffn2_sum_read")
            norm_root("last", "sum_last", rstd[:, 0:T])

        @block.tensor
        def _(pe):
            ident = K("ident")
            done_jobs = [0]

            def ring_arrived(part, name):
                slot, loads = PLACE[(part, name)]
                pe.wait_ge(sem(f"ring_full{slot}"), 16 * loads)

            def open_job(name):
                j = JOB[name]
                assert j == done_jobs[0], (name, JOBS[done_jobs[0]])
                if j >= 4:
                    pe.wait_ge(sem("job_emptied"), j - 3)
                return bank[j % 4]

            def close_job(last):
                last.then_inc(sem("job_ready"), 1)
                done_jobs[0] += 1

            def product(dst, lhs, rhs):
                n = len(lhs)
                for i in range(n):
                    last = pe.matmul(dst, lhsT=lhs[i], rhs=rhs[i], start=(i == 0), stop=(i == n - 1))
                return last

            def turn_job(name, pieces):
                b = open_job(name)
                for i, piece in enumerate(pieces):
                    last = pe.transpose(b[:, i * P:(i + 1) * P], piece, ident)
                close_job(last)

            def sum_job(name, key, src, chunks, weights="ones", out_w=T):
                b = open_job(name)
                pe.wait_ge(sem(f"{key}_squares"), 1)
                last = product(b[:, 0:T], [K(weights)] * chunks, [src[:, k, :] for k in range(chunks)])
                close_job(last)

            def col_job(name, item):
                b = open_job(name)
                pe.wait_ge(sem("mod_acc_step"), 8 * (item + 1))
                for m in range(4):
                    last = pe.matmul(b[:, m:m + 1], lhsT=mod_acc[:, item % 2, m * P:(m + 1) * P],
                                     rhs=K("ones")[:, 0:1], start=True, stop=True)
                close_job(last)

            def linear_job(name, w, cols, src, n_wait=None):
                b = open_job(name)
                for i, (lo, n) in enumerate(cols):
                    k_n = w.shape[1]
                    last = product(b[0:n, i * T:(i + 1) * T], [w[:, k, lo:lo + n] for k in range(k_n)],
                                   [src[:, k, :] for k in range(k_n)])
                close_job(last)

            pe.wait_ge(sem("consts_loaded"), 16)
            for name, rows in (("rows_a", rows_a), ("rows_b", rows_b)):
                b = open_job(name)
                pe.wait_ge(sem(f"{name}_loaded"), 16 * {"rows_a": 13, "rows_b": 8}[name])
                n = rows.shape[0]
                close_job(pe.transpose(b[:, 0:n], rows[:, :], ident[0:n, 0:n]))
            for what, rows in (("x", x_rows), ("ctx", ctx_rows)):
                pe.wait_ge(sem(f"{what}_loaded"), 16)
                for i in range(4):
                    turn_job(f"{what}_turn{i}", [rows[:, b, (2 * i + c) * P:(2 * i + c + 1) * P]
                                                 for c in range(2) for b in range(2)])
            sum_job("sum_x", "n1", squares, KD)
            sum_job("sum_ctx", "c1", ctx_squares, KD)
            pe.wait_ge(sem("cond_ready"), 2)
            for i in range(4):
                ring_arrived("pre", f"mod{i}")
                w = ring_w("pre", f"mod{i}")
                b = open_job(f"mod{i}")
                for m in range(4):
                    last = product(b[:, 2 * m:2 * m + 2], [w[:, k, m * P:(m + 1) * P] for k in range(KD)],
                                   [cond[:, k, :] for k in range(KD)])
                close_job(last)
            ring_arrived("pre", "w_kv")
            w = ring_w("pre", "w_kv")
            b = open_job("z_k")
            pe.wait_ge(sem("c1_ready"), 1)
            product(b[:, 0:T], [w[:, k, 0:P] for k in range(KD)], [mixT[:, k, :] for k in range(KD)])
            pe.wait_ge(sem("n1_ready"), 1)
            close_job(product(b[:, T:2 * T], [w[:, k, 0:P] for k in range(KD)], [hT[:, k, :] for k in range(KD)]))
            b = open_job("z_v")
            for kb in range(4):
                src = mixT if kb < 2 else hT
                last = product(b[:, kb * P:(kb + 1) * P], [src[:, k, (kb % 2) * P:(kb % 2) * P + P] for k in range(KD)],
                               [w[:, k, P:2 * P] for k in range(KD)])
            close_job(last)
            col_job("col_gt1a", 0)
            ring_arrived("pre", "w_q")
            w = ring_w("pre", "w_q")
            for i in range(2):
                b = open_job(f"z_q{i}")
                for c in range(2):
                    for k in range(KD):
                        for a in range(2):
                            head = 2 * i + c + 4 * a
                            last = pe.matmul(b[64 * a:64 * a + 64, c * T:(c + 1) * T], lhsT=w[:, k, 64 * head:64 * head + 64],
                                             rhs=hT[:, k, :], start=(k == 0), stop=(k == KD - 1))
                close_job(last)
            col_job("col_gt1b", 1)
            for item, (name, col) in enumerate((("gb", "col_sh2a"), ("gc", "col_sh2b"), ("u", "col_sc2a"))):
                ring_arrived("pre", f"w_{name}")
                for i in range(2):
                    linear_job(f"z_{name}{i}", ring_w("pre", f"w_{name}"), [(256 * i, P), (256 * i + P, P)], hT)
                col_job(col, 2 + item)
            pe.wait_ge(sem("qk_squares"), 1)
            for i in range(3):
                b = open_job(f"qk_sum{i}")
                close_job(pe.matmul(b[:, :], lhsT=K("heads64"), rhs=squares[:, 2 * i:2 * i + 2, :], start=True, stop=True))
            pe.wait_ge(sem("qk_ready"), 1)
            for i, chunks in enumerate(((0, 2), (2, 4), (5, 6))):
                b = open_job(f"qk_rot{i}")
                w = (chunks[1] - chunks[0]) * T
                close_job(pe.matmul(b[:, 0:w], lhsT=K("rot_axial"), rhs=qk[:, chunks[0]:chunks[1], :], start=True, stop=True))
            col_job("col_sc2b", 5)
            col_job("col_gt2a", 6)

            def attention(key):
                _, instances, _ = ATTENTIONS[key]
                n = len(instances)
                job = None
                for i in range(n + 2):
                    if i < n:
                        it = instances[i]
                        if i >= 2:
                            pe.wait_ge(sem(f"{key}_exp"), i - 1)
                        product(bank[4 + i % 2][:, 0:it["keys"]], it["q"], it["k"]).then_inc(sem(f"{key}_scores"), 1)
                    if 1 <= i <= n:
                        j = i - 1
                        pe.wait_ge(sem(f"{key}_probs"), j + 1)
                        if j >= 2:
                            pe.wait_ge(sem(f"{key}_probsT"), j - 1)
                        for b in range(instances[j]["keys"] // P):
                            last = pe.transpose(bank[6 + j % 2][:, b * P:(b + 1) * P], probs[:, j % 2, b * P:(b + 1) * P], ident)
                        last.then_inc(sem(f"{key}_turned"), 1)
                    if i >= 2:
                        j = i - 2
                        it = instances[j]
                        if it["job"] != job:
                            job = it["job"]
                            open_job(job)
                        pe.wait_ge(sem(f"{key}_probsT"), j + 1)
                        nk = it["keys"] // P
                        last = product(job_bank(job)[it["col"]:it["col"] + 64, it["qb"] * P:(it["qb"] + 1) * P], it["v"],
                                       [probsT[:, j % 2, b * P:(b + 1) * P] for b in range(nk)])
                        if it["last"]:
                            close_job(last)

            pe.wait_ge(sem("rope1_ready"), 1)
            attention("at1")
            col_job("col_gt2b", 7)
            pe.wait_ge(sem("mg_squares"), 1)
            for i in range(4):
                b = open_job(f"head_sum{i}")
                close_job(pe.matmul(b[:, :], lhsT=K("heads64"), rhs=squares[:, 2 * i:2 * i + 2, :], start=True, stop=True))
            pe.wait_ge(sem("mg_ready"), 1)
            for i in range(4):
                if i % 2 == 0:
                    ring_arrived("pre", f"w_out{i // 2}")
                linear_job(f"merge{i}", ring_w("pre", f"w_out{i // 2}"), [(256 * (i % 2), P), (256 * (i % 2) + P, P)], mixT)
            sum_job("sum_n2", "n2", squares, KD)
            pe.wait_ge(sem("n2_ready"), 1)
            pe.wait_ge(sem("router_loaded"), 32)
            b = open_job("logits")
            for tb in range(2):
                last = product(b[:, 64 * tb:64 * tb + 36], [hT[:, k, tb * P:(tb + 1) * P] for k in range(KD)],
                               [router[:, k, :] for k in range(KD)])
            close_job(last)
            for i in range(4):
                turn_job(f"h2_turn{i}", [hT[:, 4 * (i % 2) + c, (i // 2) * P:(i // 2 + 1) * P] for c in range(4)])
            b = open_job("positions")
            pe.wait_ge(sem("assigned"), 1)
            a0, a1 = assigned[:, 0, :], assigned[:, 1, :]
            product(b[:, 0:32], [K("before")], [a0])
            product(b[:, 32:64], [K("ones"), K("before")], [a0, a1])
            close_job(product(b[:, 64:96], [K("ones"), K("ones")], [a0, a1]))
            b = open_job("bias_turn")
            pe.wait_ge(sem("rel_bias_loaded"), 64)
            for i in range(4):
                last = pe.matmul(b[0:8, i * P:(i + 1) * P], lhsT=rel_bias_rows[:, i, :], rhs=K("reverse"),
                                 start=True, stop=True)
            close_job(last)

            pe.wait_ge(sem("job_emptied"), done_jobs[0])
            pe.wait_ge(sem("zeros_ready"), 1)
            for i in range(4):
                pe.matmul(bank[i][:, :], lhsT=zeros[:, 0:P], rhs=zeros[:, :], start=True, stop=False, skip_group_check=True)

            def prepare(count, selected):
                pe.wait_ge(sem("selected"), count)
                if selected is not None:
                    pe.wait_ge(sem("pick_wT_ready"), selected)
                for k in range(KD):
                    for tb in range(2):
                        pe.matmul(bank[6][:, k * SLOTS:(k + 1) * SLOTS], lhsT=h_rows[:, tb, k * P:(k + 1) * P],
                                  rhs=pick[:, tb, :], start=(tb == 0), stop=(tb == 1))
                for tb in range(2):
                    last = pe.transpose(bank[7][:, tb * P:(tb + 1) * P], pick_w[:, tb, :], ident)
                last.then_inc(sem("gathered"), 1)

            def expert(u, n, prep, arrivals):
                gate, up, down = expert_w(u)
                pe.wait_ge(sem("xe_ready"), prep - 1)
                pe.wait_ge(sem(f"gate_full{u}"), arrivals)
                for w, b in ((gate, bank[4]), (up, bank[5])):
                    if b is bank[5]:
                        pe.wait_ge(sem(f"up_full{u}"), arrivals)
                    for k in range(KD):
                        for half in range(2):
                            last = pe.matmul(b[64 * half:64 * half + 64, 0:HALF_E], lhsT=xeT[:, k, :],
                                             rhs=w[:, k, half * HALF_E:(half + 1) * HALF_E],
                                             start=(k == 0), stop=(k == KD - 1))
                last.then_inc(sem("gate_up_done"), 1)
                prepare(prep, prep - 1)
                pe.wait_ge(sem("hidden_ready"), n)
                for c in range(3):
                    last = pe.transpose(bank[5][:, c * P:(c + 1) * P], hidden[:, c * P:(c + 1) * P], ident)
                last.then_inc(sem("hidden_turned"), 1)
                pe.wait_ge(sem("hiddenT_ready"), n)
                pe.wait_ge(sem("xe_ready"), prep)
                pe.wait_ge(sem(f"down_full{u}"), arrivals)
                for f in range(6):
                    for half in range(2):
                        last = pe.matmul(bank[6][64 * half:64 * half + 64, :],
                                         lhsT=hiddenT[:, f % 3, 64 * (f // 3):64 * (f // 3) + 64],
                                         rhs=down[:, f, half * 512:(half + 1) * 512], start=(f == 0), stop=(f == 5))
                last.then_inc(sem("down_done"), 1)
                pe.wait_ge(sem("y_ready"), n)
                pe.wait_ge(sem("pick_wT_ready"), prep - 1)
                for c in range(4):
                    for half in range(2):
                        m = 4 * half + c
                        pe.matmul(bank[m // 2][:, (m % 2) * T:(m % 2 + 1) * T],
                                  lhsT=y_e[64 * half:64 * half + 64, c * P:(c + 1) * P],
                                  rhs=pick_wT[64 * half:64 * half + 64, u, :],
                                  start=False, stop=False, skip_group_check=True)

            prepare(1, None)
            with pe.Fori(0, N_EXPERTS // 2) as it:
                for u in range(2):
                    expert(u, it * 2 + u + 1, it * 2 + u + 2, it * 16 + 16)
            pe.wait_ge(sem("busiest_ready"), 1)
            most = pe.value_load(busiest[0:1, 0:1], min_val=0, max_val=T)
            with pe.If(most > SLOTS):
                with pe.Fori(1, PASSES) as ps:
                    prepare(ps * (N_EXPERTS + 1) + 1, ps * (N_EXPERTS + 1))
                    with pe.Fori(0, N_EXPERTS // 2) as it:
                        for u in range(2):
                            expert(u, ps * N_EXPERTS + it * 2 + u + 1, ps * (N_EXPERTS + 1) + it * 2 + u + 2,
                                   ps * (8 * N_EXPERTS) + it * 16 + 16)
            for i in range(4):
                last = pe.matmul(bank[i][:, :], lhsT=zeros[:, 0:P], rhs=zeros[:, :], start=False, stop=True, skip_group_check=True)
            last.then_inc(sem("experts_done"), 1)

            pe.wait_ge(sem("y_moe_read"), 1)
            for i in range(4):
                col_job(f"col_ada{i}", 8 + i)
            sum_job("sum_final", "fin1", squares, KD)

            def feed_forward(key, ada_items):
                pe.wait_ge(sem("job_emptied"), done_jobs[0])
                pe.wait_ge(sem(f"{key}_ready"), 1)

                def gate_up(s, slot, half, parity, arrivals, act_read):
                    w = ring(slot).rearrange("p (k g n) -> p k g n", k=KD, g=2)
                    if half == 0:
                        pe.wait_ge(sem(f"{key}_in_full{slot}"), arrivals)
                    if act_read is not None:
                        pe.wait_ge(sem(f"{key}_act"), act_read)
                    for g in range(2):
                        last = product(bank[4 + parity][:, g * T:(g + 1) * T],
                                       [w[:, k, g, half * P:(half + 1) * P] for k in range(KD)],
                                       [hT[:, k, :] for k in range(KD)])
                    last.then_inc(sem(f"{key}_gate_up_done"), 1)

                def down(s, slot, half, parity, arrivals, first=False):
                    w = ring(slot)[:, 0:2 * D].rearrange("p (k n) -> p k n", k=2)
                    if half == 0:
                        pe.wait_ge(sem(f"{key}_out_full{slot}"), arrivals)
                    pe.wait_ge(sem(f"{key}_act"), s)
                    for m in range(KD):
                        last = pe.matmul(bank[m // 2][:, (m % 2) * T:(m % 2 + 1) * T], lhsT=w[:, half, m * P:(m + 1) * P],
                                         rhs=ff_act[:, parity, :], start=(first and m % 2 == 0), stop=False,
                                         skip_group_check=True)
                    last.then_inc(sem(f"{key}_down_done"), 1)
                    return last

                gate_up(1, 2, 0, 0, 32, None)
                gate_up(2, 2, 1, 1, 32, None)
                down(1, 3, 0, 0, 16, first=True)
                with pe.Fori(0, FF_LOOPS) as it:
                    for j in range(4):
                        s = it * 4 + j + 3
                        slot = 2 * (j // 2)
                        if j == 0:
                            gate_up(s, 0, 0, 0, it * 32 + 32, s - 2)
                            down(s - 1, 3, 1, 1, None)
                        elif j == 1:
                            gate_up(s, 0, 1, 1, None, s - 2)
                            down(s - 1, 1, 0, 0, it * 16 + 16)
                        elif j == 2:
                            gate_up(s, 2, 0, 0, it * 32 + 64, s - 2)
                            down(s - 1, 1, 1, 1, None)
                        else:
                            gate_up(s, 2, 1, 1, None, s - 2)
                            down(s - 1, 3, 0, 0, it * 16 + 32)
                        if ada_items and j % 2 == 1:
                            u = j // 2
                            pe.wait_ge(sem("mod_acc_step"), it * 16 + 8 * (12 + u + 1))
                            for m in range(4):
                                last = pe.matmul(bank[6 + u][:, m:m + 1], lhsT=mod_acc[:, u, m * P:(m + 1) * P],
                                                 rhs=K("ones")[:, 0:1], start=True, stop=True)
                            last.then_inc(sem("ada_col_ready"), 1)
                down(4 * FF_LOOPS + 2, 3, 1, 1, None)
                for i in range(4):
                    last = pe.matmul(bank[i][:, :], lhsT=zeros[:, 0:P], rhs=zeros[:, :], start=False, stop=True,
                                     skip_group_check=True)
                last.then_inc(sem(f"{key}_sum_done"), 1)
                pe.wait_ge(sem(f"{key}_sum_read"), 1)

            sum_job("sum_ffn1", "ffn1", squares, KD)
            feed_forward("ffn1", True)
            sum_job("sum_mix", "mix", squares, KD)
            pe.wait_ge(sem("mix_ready"), 1)
            ring_arrived("mid", "w2_lat")
            w = ring_w("mid", "w2_lat")
            linear_job("z_lat", w, [(0, P), (P, P)], hT)
            linear_job("z_kv", w, [(256, P), (320, 96)], hT)
            for name, col, item in (("caq", "col_ada14", 22), ("cak", "col_ada15", 23)):
                ring_arrived("mid", f"w2_{name}")
                for i in range(2):
                    linear_job(f"z_{name}{i}", ring_w("mid", f"w2_{name}"), [(256 * i, P), (256 * i + P, P)], hT)
                col_job(col, item)
            ring_arrived("mid", "w2_cav")
            w = ring_w("mid", "w2_cav")
            for tb in range(2):
                b = open_job(f"z_cav{tb}")
                close_job(product(b[:, :], [hT[:, k, tb * P:(tb + 1) * P] for k in range(KD)], [w[:, k, :] for k in range(KD)]))
            b = open_job("lat_sum")
            pe.wait_ge(sem("lat_squares"), 1)
            product(b[:, 0:T], [K("ones")] * 2, [squares[:, 0, :], squares[:, 1, :]])
            close_job(product(b[:, T:2 * T], [K("ones")], [squares[:, 2, :]]))
            col_job("col_ada16", 24)
            for gate in ("ga", "gb"):
                for i in range(4):
                    name = f"w2_{gate}{i // 2}"
                    if i % 2 == 0:
                        ring_arrived("mid", name)
                    linear_job(f"z_{gate}{i}" + ("_2" if gate == "gb" else ""), ring_w("mid", name),
                               [(256 * (i % 2), P), (256 * (i % 2) + P, P)], hT)
                if gate == "ga":
                    col_job("col_ada17", 25)
            pe.wait_ge(sem("w_uq_full"), 16)
            pe.wait_ge(sem("w_ukv_full"), 16)
            pe.wait_ge(sem("lat_ready"), 1)
            both = ring(PLACE[("mid", "mla_up")][0])
            uq = both[:, 0:1536].rearrange("p (k n) -> p k n", k=2)
            ukv = both[:, 1536:2560].rearrange("p (k h n) -> p k h n", k=1, h=8)
            for i in range(4):
                linear_job(f"mla_q{i}", uq, [(192 * i, 96), (192 * i + 96, 96)], latT)
            for i in range(4):
                linear_job(f"mla_k{i}", both[:, 1536:2560].rearrange("p (k n) -> p k n", k=1),
                           [(256 * i, 64), (256 * i + P, 64)], latT[:, 2:3, :])
            for tb in range(2):
                b = open_job(f"mla_v{tb}")
                close_job(product(b[:, :], [latT[:, 2, tb * P:(tb + 1) * P]], [ukv[:, 0, :, 64:128]]))
            pe.wait_ge(sem("mla_qk_ready"), 1)
            for i in range(4):
                b = open_job(f"pe_rot{i}")
                close_job(pe.matmul(b[0:96, :], lhsT=K("rot_half")[0:96, 0:96], rhs=mla_q[0:96, 2 * i:2 * i + 2, :],
                                    start=True, stop=True))
            b = open_job("kpe_rot")
            close_job(pe.matmul(b[0:96, 0:T], lhsT=K("rot_half")[0:96, 0:96], rhs=squares[0:96, 3, :], start=True, stop=True))
            pe.wait_ge(sem("mla_ready"), 1)
            attention("mla")
            pe.wait_ge(sem("bias_loaded"), 32)
            attention("ca")
            ring_arrived("mid", "w_branch_a")
            ring_arrived("mid", "w_branch_b")
            pe.wait_ge(sem("job_emptied"), done_jobs[0])
            for i in range(4):
                for ab, at in (("a", 0), ("b", 4)):
                    w = ring(PLACE[("mid", f"w_branch_{ab}")][0]).rearrange("p (k n) -> p k n", k=4)
                    linear_job(f"branch_{ab}{i}", w, [(256 * i, P), (256 * i + P, P)], squares[:, at:at + 4, :])
            pe.wait_ge(sem("merged_ready"), 4)
            for i in range(4):
                if i % 2 == 0:
                    ring_arrived("mid", f"w_out2_{i // 2}")
                linear_job(f"out2_{i}", ring_w("mid", f"w_out2_{i // 2}"), [(256 * (i % 2), P), (256 * (i % 2) + P, P)], hT)
            sum_job("sum_ffn2", "ffn2", squares, KD)
            feed_forward("ffn2", False)
            sum_job("sum_last", "last", squares, KD)
            pe.wait_ge(sem("last_ready"), 1)
            for i in range(4):
                turn_job(f"y_turn{i}", [xT[:, 4 * (i % 2) + c, (i // 2) * P:(i // 2 + 1) * P] for c in range(4)])
            assert done_jobs[0] == len(JOBS)

        @block.vector
        def _(dve):
            n_step, emptied, n_item = [0], [0], [0]

            def step(instruction):
                n_step[0] += 1
                instruction.then_inc(sem("dve_step"), 1)
                dve.wait_ge(sem("dve_step"), n_step[0])

            def ring_arrived(part, name):
                slot, loads = PLACE[(part, name)]
                dve.wait_ge(sem(f"ring_full{slot}"), 16 * loads)

            def take_job(name):
                assert JOB[name] == emptied[0], (name, JOBS[emptied[0]])
                dve.wait_ge(sem("job_ready"), JOB[name] + 1)
                return job_bank(name)

            def empty_job(instruction):
                instruction.then_inc(sem("job_emptied"), 1)
                emptied[0] += 1

            def job_done_here():
                dve.wait_ge(sem("job_emptied"), emptied[0])

            def mod_item(w, scalars, u, first):
                for k in range(KD):
                    if k == 0:
                        i = nc.vector.tensor_scalar(mod_acc[:, u, :], w[:, k, :], scalars[k], None, ALU.mult)
                    else:
                        dve.wait_ge(sem("mod_acc_step"), first + k)
                        i = nc.vector.scalar_tensor_tensor(out=mod_acc[:, u, :], in0=w[:, k, :], scalar=scalars[k],
                                                           in1=mod_acc[:, u, :], op0=ALU.mult, op1=ALU.add)
                    i.then_inc(sem("mod_acc_step"), 1)

            cond_1 = [cond[:, k, 0:1] for k in range(KD)]
            cond_2 = [cond2[:, k:k + 1] for k in range(KD)]

            def item(part, name):
                n = n_item[0]
                n_item[0] += 1
                ring_arrived(part, name)
                mod_item(ring_w(part, name), cond_1 if part == "pre" else cond_2, n % 2, 8 * n)

            def col_job(name, dst, bias):
                b = take_job(name)
                empty_job(nc.vector.tensor_tensor(dst, b[:, 0:4], bias, ALU.add))

            def mod_col(name, n):
                col_job(name, mod[:, 16 + 4 * n:20 + 4 * n], cols_a[:, 16 + 4 * n:20 + 4 * n])

            def ada_col(name, n):
                col_job(name, ada[:, 4 * n:4 * n + 4], cols_b[:, 4 * n:4 * n + 4])

            def make_gain(key, g, scale):
                s = SET[key]
                step(nc.vector.scalar_tensor_tensor(out=gains[:, s * KD:(s + 1) * KD], in0=scale, scalar=1.0, in1=g,
                                                    op0=ALU.add, op1=ALU.mult))

            def norm_mean(job, dst):
                b = take_job(job)
                empty_job(nc.vector.tensor_scalar(dst, b[:, 0:T], 1.0 / D, None, ALU.mult))

            def norm_divide(key, src, dst, stat):
                dve.wait_ge(sem(f"{key}_root"), 1)
                step(nc.vector.reciprocal(stat, stat))
                for k in range(KD):
                    i = nc.vector.tensor_tensor(dst[:, k, :], src[:, k, :], stat, ALU.mult)
                step(i)

            def norm_modulate(key, dst, shifts, shift_at):
                for k in range(KD):
                    i = nc.vector.tensor_scalar(dst[:, k, :], dst[:, k, :], gain(key, k),
                                                shifts[:, shift_at + k:shift_at + k + 1], ALU.mult, ALU.add)
                i.then_inc(sem(f"{key}_ready"), 1)

            def norm_gain(key, dst, name, col):
                for k in range(KD):
                    i = nc.vector.tensor_scalar(dst[:, k, :], dst[:, k, :], col(name, k), None, ALU.mult)
                i.then_inc(sem(f"{key}_ready"), 1)
                dve.wait_ge(sem(f"{key}_ready"), 1)

            nc.vector.memset(zeros[:, :], 0.0).then_inc(sem("zeros_ready"), 1)
            for c in (0, T + 1):
                nc.vector.memset(conv_in[:, :, c:c + 1], 0.0)
            nc.vector.memset(weights[:, :, 32:33], 0.0)
            step(nc.vector.memset(places[:, :, 32:33], -1.0))
            dve.wait_ge(sem("positions_loaded"), 16)
            dve.wait_ge(sem("consts_loaded"), 16)
            pos, near, arg, arg_cos, wrap = (angle[64:96, i, :] for i in range(5))
            step(nc.vector.tensor_copy(pos, turns[64:96, :]))
            step(nc.vector.tensor_scalar(pos, pos, K("inv_freq")[64:96, :], None, ALU.mult))
            step(nc.vector.tensor_scalar(turns[64:96, :], pos, 1.0 / TWO_PI, None, ALU.mult))
            step(nc.vector.tensor_copy(near, turns[64:96, :]))
            for i, part in enumerate((PI_A, PI_B, PI_C)):
                step(nc.vector.scalar_tensor_tensor(out=arg, in0=near, scalar=-part, in1=pos if i == 0 else arg,
                                                    op0=ALU.mult, op1=ALU.add))
            step(nc.vector.tensor_scalar(arg_cos, arg, TWO_PI / 4, None, ALU.add))
            for a in (arg, arg_cos):
                for op, turn in ((ALU.is_gt, -TWO_PI), (ALU.is_lt, TWO_PI)):
                    limit = TWO_PI / 2 if turn < 0 else -TWO_PI / 2
                    step(nc.vector.tensor_scalar(wrap, a, limit, turn, op, ALU.mult))
                    step(nc.vector.tensor_tensor(a, a, wrap, ALU.add))
                i = nc.vector.tensor_scalar(a, a, 3.1415925, -3.1415925, ALU.min, ALU.max)
            i.then_inc(sem("angles_ready"), 1)

            for name, cols in (("rows_a", cols_a), ("rows_b", cols_b)):
                b = take_job(name)
                empty_job(nc.vector.tensor_copy(cols[:, :], b[:, 0:cols.shape[1]]))
            for what, dst in (("x", xT[:, :, :]), ("ctx", ctxT)):
                for i in range(4):
                    take_job(f"{what}_turn{i}")
                    empty_job(nc.vector.tensor_copy(dst[:, 2 * i:2 * i + 2, :], job_wide(f"{what}_turn{i}")))
            norm_mean("sum_x", rstd[:, 0:T])
            norm_mean("sum_ctx", rstd[:, T:2 * T])
            norm_divide("n1", xT, hT, rstd[:, 0:T])
            norm_divide("c1", ctxT, mixT, rstd[:, T:2 * T])
            for i in range(4):
                b = take_job(f"mod{i}")[:, 0:8].rearrange("p (m c) -> p m c", c=2)
                bias = cols_a[:, 4 * i:4 * i + 4]
                nc.vector.tensor_tensor(mod[:, 4 * i:4 * i + 4], b[:, :, 0], bias, ALU.add)
                empty_job(nc.vector.tensor_tensor(mod_ctx[:, 4 * i:4 * i + 4], b[:, :, 1], bias, ALU.add))
            job_done_here()
            g1 = cols_a[:, 48:56]
            make_gain("n1", g1, mod[:, 8:16])
            make_gain("c1", g1, mod_ctx[:, 8:16])
            norm_modulate("c1", mixT, mod_ctx, 0)
            norm_modulate("n1", hT, mod, 0)

            take_job("z_k")
            empty_job(nc.vector.tensor_copy(qk[:, 4:6, :], job_wide("z_k")))
            take_job("z_v")
            empty_job(nc.vector.tensor_copy(v1, job_bank("z_v")[:, :].rearrange("p (b n) -> p b n", b=4)))
            item("pre", "gt1a")
            mod_col("col_gt1a", 0)
            for i in range(2):
                take_job(f"z_q{i}")
                empty_job(nc.vector.tensor_copy(qk[:, 2 * i:2 * i + 2, :], job_wide(f"z_q{i}")))
            item("pre", "gt1b")
            mod_col("col_gt1b", 1)
            for i in range(2):
                take_job(f"z_gb{i}")
                empty_job(nc.vector.tensor_copy(gate_b[:, 2 * i:2 * i + 2, :], job_wide(f"z_gb{i}")))
            item("pre", "sh2a")
            mod_col("col_sh2a", 2)
            for i in range(2):
                take_job(f"z_gc{i}")
                empty_job(nc.vector.tensor_copy(conv_out[:, 2 * i:2 * i + 2, :], job_wide(f"z_gc{i}")))
            item("pre", "sh2b")
            mod_col("col_sh2b", 3)
            for i in range(2):
                take_job(f"z_u{i}")
                empty_job(nc.vector.tensor_tensor(conv_in[:, 2 * i:2 * i + 2, 1:T + 1], job_wide(f"z_u{i}"),
                                                  conv_out[:, 2 * i:2 * i + 2, :], ALU.mult))
            item("pre", "sc2a")
            col_job("col_sc2a", mod[:, 32:36], cols_a[:, 32:36])
            nc.vector.memset(mod_acc[0:1, 1, 0:1], 0.0).then_inc(sem("conv_in_ready"), 1)
            for i in range(3):
                take_job(f"qk_sum{i}")
                empty_job(nc.vector.tensor_scalar(qk_tmp[:, 2 * i:2 * i + 2, :], job_wide(f"qk_sum{i}"), 1.0 / 64, None, ALU.mult))
            dve.wait_ge(sem("qk_root"), 1)
            step(nc.vector.reciprocal(qk_tmp, qk_tmp))
            for lo, hi, name in ((0, 4, "q_norm_g"), (4, 6, "k_norm_g")):
                i = nc.vector.scalar_tensor_tensor(out=qk[:, lo:hi, :], in0=qk[:, lo:hi, :], scalar=col_a(name),
                                                   in1=qk_tmp[:, lo:hi, :], op0=ALU.mult, op1=ALU.mult)
            i.then_inc(sem("qk_ready"), 1)
            dve.wait_ge(sem("qk_ready"), 1)

            def tables(cos, sin, n):
                return [t.rearrange("p (a t) -> p a t", a=1).broadcast_to((t.shape[0], n, T)) for t in (cos, sin)]

            for i, (lo, hi) in enumerate(((0, 2), (2, 4), (5, 6))):
                b = take_job(f"qk_rot{i}")[:, 0:(hi - lo) * T].rearrange("p (a t) -> p a t", t=T)
                cos, sin = tables(K("axial_cos"), K("axial_sin"), hi - lo)
                empty_job(nc.vector.tensor_tensor(qk_tmp[:, lo:hi, :], b, sin, ALU.mult))
                step(nc.vector.tensor_tensor(qk[:, lo:hi, :], qk[:, lo:hi, :], cos, ALU.mult))
                i = nc.vector.tensor_tensor(qk[:, lo:hi, :], qk[:, lo:hi, :], qk_tmp[:, lo:hi, :], ALU.add)
            i.then_inc(sem("rope1_ready"), 1)
            item("pre", "sc2b")
            mod_col("col_sc2b", 5)
            item("pre", "gt2a")
            mod_col("col_gt2a", 6)

            def attention(key):
                index, instances, scale = ATTENTIONS[key]
                n = len(instances)
                for i in range(n + 3):
                    if i < n:
                        w = instances[i]["keys"]
                        scores = bank[4 + i % 2]
                        dve.wait_ge(sem(f"{key}_scores"), i + 1)
                        if instances[i]["mask"]:
                            late = scores[0:64, w - 64:w]
                            step(nc.vector.tensor_scalar(late, late, NEG, None, ALU.add))
                        step(nc.vector.reduce_max(stats[:, index, 2, i:i + 1], scores[:, 0:w], AX_X))
                        nc.vector.tensor_scalar(stats[:, index, 0, i:i + 1], stats[:, index, 2, i:i + 1], -scale, None,
                                                ALU.mult).then_inc(sem(f"{key}_negmax"), 1)
                    if 1 <= i <= n:
                        j = i - 1
                        w = instances[j]["keys"]
                        dve.wait_ge(sem(f"{key}_exp"), j + 1)
                        step(nc.vector.reciprocal(stats[:, index, 2, j:j + 1], stats[:, index, 1, j:j + 1]))
                        nc.vector.tensor_scalar(probs[:, j % 2, 0:w], probs[:, j % 2, 0:w], stats[:, index, 2, j:j + 1],
                                                None, ALU.mult).then_inc(sem(f"{key}_probs"), 1)
                    if i >= 3 and instances[i - 3]["last"]:
                        job = instances[i - 3]["job"]
                        take_job(job)
                        empty_job(nc.vector.tensor_copy(ATT_OUT[key](int(job[-1])), job_bank(job)[:, 0:T]))

            attention("at1")
            item("pre", "gt2b")
            mod_col("col_gt2b", 7)
            mg = h_rows[:, :, :].rearrange("p b (k t) -> p (b k) t", t=T)
            for i in range(4):
                take_job(f"head_sum{i}")
                empty_job(nc.vector.tensor_scalar(mg[:, 2 * i:2 * i + 2, :], job_wide(f"head_sum{i}"), 1.0 / 64, None, ALU.mult))
            dve.wait_ge(sem("mg_root"), 1)
            step(nc.vector.reciprocal(mg, mg))
            for k in range(KD):
                i = nc.vector.scalar_tensor_tensor(out=mixT[:, k, :], in0=mixT[:, k, :],
                                                   scalar=cols_a[:, ROWS_A["attn_out_g"] + k:ROWS_A["attn_out_g"] + k + 1],
                                                   in1=mg[:, k, :], op0=ALU.mult, op1=ALU.mult)
            i.then_inc(sem("mg_ready"), 1)

            def residual_job(name, i, gate, at):
                take_job(name)
                for c in range(2):
                    k = 2 * i + c
                    ins_ = nc.vector.scalar_tensor_tensor(out=xT[:, k, :], in0=job_wide(name)[:, c, :],
                                                          scalar=gate[:, at + k:at + k + 1], in1=xT[:, k, :],
                                                          op0=ALU.mult, op1=ALU.add)
                empty_job(ins_)

            for i in range(4):
                residual_job(f"merge{i}", i, mod, 16)
            make_gain("n2", cols_a[:, 56:64], mod[:, 32:40])
            norm_mean("sum_n2", rstd[:, 0:T])
            norm_divide("n2", xT, hT, rstd[:, 0:T])
            norm_modulate("n2", hT, mod, 24)

            b = take_job("logits")
            for tb in range(2):
                i = nc.vector.tensor_copy(logits[:, tb, :], b[:, 64 * tb:64 * tb + 36])
            empty_job(i)
            job_done_here()
            for tb in range(2):
                step(nc.vector.reduce_max(picked[:, tb, 28:29], logits[:, tb, 0:4], AX_X))
                nc.vector.tensor_scalar(picked[:, tb, 0:1], picked[:, tb, 28:29], -1.0, None, ALU.mult)\
                  .then_inc(sem("router_max"), 1)
                step(nc.vector.scalar_tensor_tensor(out=picked[:, tb, 24:28], in0=logits[:, tb, 0:4],
                                                    scalar=picked[:, tb, 28:29], in1=K("group_rank"),
                                                    op0=ALU.is_equal, op1=ALU.mult))
                step(nc.vector.reduce_max(picked[:, tb, 29:30], picked[:, tb, 24:28], AX_X))
                step(nc.vector.tensor_scalar(picked[:, tb, 24:28], picked[:, tb, 24:28], picked[:, tb, 29:30], None, ALU.is_equal))
                step(nc.vector.tensor_scalar(picked[:, tb, 30:31], picked[:, tb, 29:30], -float(GROUP_SIZE),
                                             float(GROUP_SIZE * N_GROUPS), ALU.mult, ALU.add))
                step(nc.vector.tensor_scalar(picked[:, tb, 8:16], logits[:, tb, 4:12], picked[:, tb, 24:25], None, ALU.mult))
                for g in range(1, N_GROUPS):
                    step(nc.vector.scalar_tensor_tensor(out=picked[:, tb, 8:16], in0=logits[:, tb, 4 + 8 * g:12 + 8 * g],
                                                        scalar=picked[:, tb, 24 + g:25 + g], in1=picked[:, tb, 8:16],
                                                        op0=ALU.mult, op1=ALU.add))
                step(nc.vector.max(out=picked[:, tb, 16:24], in_=picked[:, tb, 8:16]))
                step(nc.vector.max_index(out=picked_i[:, tb, :], in_max=picked[:, tb, 16:24], in_values=picked[:, tb, 8:16]))
                step(nc.vector.tensor_copy(picked[:, tb, 31:33], picked_i[:, tb, 0:2]))
                step(nc.vector.tensor_scalar(picked[:, tb, 31:33], picked[:, tb, 31:33], picked[:, tb, 30:31], None, ALU.add))
                nc.vector.tensor_scalar(picked[:, tb, 3:4], picked[:, tb, 16:17], -1.0, None, ALU.mult)\
                  .then_inc(sem("router_top"), 1)
                step(nc.vector.tensor_scalar(route_tmp[:, tb, :], K("expert_id"), picked[:, tb, 31:32], None, ALU.is_equal))
                nc.vector.scalar_tensor_tensor(out=assigned[:, tb, :], in0=K("expert_id"), scalar=picked[:, tb, 32:33],
                                               in1=route_tmp[:, tb, :], op0=ALU.is_equal, op1=ALU.add)
            step(nc.vector.tensor_copy(picked[:, 0, 36:37], picked[:, 0, 31:32]))
            nc.vector.tensor_copy(picked[:, 0, 36:37], picked[:, 0, 31:32]).then_inc(sem("assigned"), 1)
            for i in range(4):
                take_job(f"h2_turn{i}")
                empty_job(nc.vector.tensor_copy(h_rows[:, i // 2, 512 * (i % 2):512 * (i % 2) + 512], job_bank(f"h2_turn{i}")[:, :]))
            dve.wait_ge(sem("group_exp"), 2)
            dve.wait_ge(sem("second_exp"), 2)
            for tb in range(2):
                step(nc.vector.tensor_scalar(picked[:, tb, 33:34], picked[:, tb, 2:3], 1.0, None, ALU.add))
                step(nc.vector.tensor_tensor(picked[:, tb, 33:34], picked[:, tb, 33:34], picked[:, tb, 1:2], ALU.mult))
                step(nc.vector.reciprocal(picked[:, tb, 34:35], picked[:, tb, 33:34]))
                step(nc.vector.tensor_tensor(picked[:, tb, 35:36], picked[:, tb, 34:35], picked[:, tb, 2:3], ALU.mult))
                step(nc.vector.tensor_scalar(weights[:, tb, 0:32], K("expert_id"), picked[:, tb, 31:32], picked[:, tb, 34:35],
                                             ALU.is_equal, ALU.mult))
                step(nc.vector.tensor_scalar(route_tmp[:, tb, :], K("expert_id"), picked[:, tb, 32:33], picked[:, tb, 35:36],
                                             ALU.is_equal, ALU.mult))
                step(nc.vector.tensor_tensor(weights[:, tb, 0:32], weights[:, tb, 0:32], route_tmp[:, tb, :], ALU.add))
            b = take_job("positions")
            for tb in range(2):
                step(nc.vector.tensor_scalar(route_tmp[:, tb, :], assigned[:, tb, :], -NO_SLOT, NO_SLOT, ALU.mult, ALU.add))
                step(nc.vector.tensor_tensor(places[:, tb, 0:32], b[:, 32 * tb:32 * tb + 32], route_tmp[:, tb, :], ALU.add))
            empty_job(nc.vector.reduce_max(picked[0:1, 0, 37:38], b[0:1, 64:96], AX_X))
            job_done_here()
            nc.vector.tensor_copy(busiest[0:1, 0:1], picked[0:1, 0, 37:38]).then_inc(sem("busiest_ready"), 1)
            take_job("bias_turn")
            empty_job(nc.vector.tensor_copy(bias_rows, job_bank("bias_turn")[0:8, :]))
            job_done_here()

            def select(e, count, gathered):
                if gathered is not None:
                    dve.wait_ge(sem("gathered"), gathered)
                for tb in range(2):
                    place = places[:, tb, bass.ds(e, 1)]
                    nc.vector.tensor_scalar(pick[:, tb, :], K("slot")[:, 0:SLOTS], place, None, ALU.is_equal)
                    i = nc.vector.tensor_scalar(pick_w[:, tb, :], K("slot"), place, weights[:, tb, bass.ds(e, 1)],
                                                ALU.is_equal, ALU.mult)
                i.then_inc(sem("selected"), 1)

            def take_turned(u, count):
                dve.wait_ge(sem("gathered"), count)
                nc.vector.tensor_copy(pick_wT[:, u, :], bank[7][:, 0:T]).then_inc(sem("pick_wT_ready"), 1)

            def expert(u, e, n, prep):
                select(e + 1, prep, prep - 1)
                dve.wait_ge(sem("gate_act_ready"), n)
                nc.vector.tensor_tensor(hidden, gate_act, bank[5][:, 0:HALF_E], ALU.mult).then_inc(sem("hidden_ready"), 1)
                take_turned(1 - u, prep)

            select(0, 1, None)
            take_turned(0, 1)
            with dve.Fori(0, N_EXPERTS // 2) as it:
                for u in range(2):
                    expert(u, it * 2 + u, it * 2 + u + 1, it * 2 + u + 2)
            most = dve.value_load(busiest[0:1, 0:1], min_val=0, max_val=T)
            with dve.If(most > SLOTS):
                with dve.Fori(1, PASSES) as ps:
                    nc.vector.tensor_scalar(places, places, -float(SLOTS), None, ALU.add).then_inc(sem("places_moved"), 1)
                    dve.wait_ge(sem("places_moved"), ps)
                    select(0, None, ps * (N_EXPERTS + 1))
                    take_turned(0, ps * (N_EXPERTS + 1) + 1)
                    with dve.Fori(0, N_EXPERTS // 2) as it:
                        for u in range(2):
                            expert(u, it * 2 + u, ps * N_EXPERTS + it * 2 + u + 1, ps * (N_EXPERTS + 1) + it * 2 + u + 2)

            def residual_sum(done, read, gate, at):
                dve.wait_ge(sem(done), 1)
                for k in range(KD):
                    i = nc.vector.scalar_tensor_tensor(out=xT[:, k, :], in0=bank[k // 2][:, (k % 2) * T:(k % 2 + 1) * T],
                                                       scalar=gate[:, at + k:at + k + 1], in1=xT[:, k, :],
                                                       op0=ALU.mult, op1=ALU.add)
                i.then_inc(sem(read), 1)
                dve.wait_ge(sem(read), 1)

            residual_sum("experts_done", "y_moe_read", mod, 40)

            for i in range(4):
                item("ada", f"ada{i}")
                ada_col(f"col_ada{i}", i)
            norm_mean("sum_final", rstd[:, 0:T])
            norm_divide("fin1", xT, xT, rstd[:, 0:T])
            norm_gain("fin1", xT, "final_g", col_a)
            job_done_here()
            make_gain("ffn1", cols_b[:, 72:80], ada[:, 8:16])
            norm_mean("sum_ffn1", rstd[:, 0:T])
            norm_divide("ffn1", xT, hT, rstd[:, 0:T])
            norm_modulate("ffn1", hT, ada, 0)

            def feed_forward(key, with_ada, gate_at):
                def one(s, parity, down):
                    dve.wait_ge(sem(f"{key}_silu"), s)
                    if down is not None:
                        dve.wait_ge(sem(f"{key}_down_done"), down)
                    nc.vector.tensor_tensor(ff_act[:, parity, :], silu_g[:, parity, :], bank[4 + parity][:, T:2 * T],
                                            ALU.mult).then_inc(sem(f"{key}_act"), 1)

                one(1, 0, None)
                one(2, 1, None)
                with dve.Fori(0, FF_LOOPS) as it:
                    for j in range(4):
                        one(it * 4 + j + 3, j % 2, it * 4 + j + 1)
                        if with_ada and j % 2 == 0:
                            u = j // 2
                            dve.wait_ge(sem(f"ada_full{4 + u}"), it * 16 + 16)
                            mod_item(ring(4 + u).rearrange("p (k n) -> p k n", k=KD), cond_2, u, it * 16 + 8 * (12 + u))
                        elif with_ada:
                            u = j // 2
                            dve.wait_ge(sem("ada_col_ready"), it * 2 + u + 1)
                            at = it * 8 + 16 + 4 * u
                            nc.vector.tensor_tensor(ada[:, bass.ds(at, 4)], bank[6 + u][:, 0:4], cols_b[:, bass.ds(at, 4)],
                                                    ALU.add).then_inc(sem("ada_col_read"), 1)
                if with_ada:
                    n_item[0] += 2 * FF_LOOPS
                    dve.wait_ge(sem("ada_col_read"), 2 * FF_LOOPS)
                step(nc.vector.tensor_scalar(half_gate[:, :], ada[:, gate_at:gate_at + KD], 0.5, None, ALU.mult))
                residual_sum(f"{key}_sum_done", f"{key}_sum_read", half_gate, 0)

            feed_forward("ffn1", True, 16)
            make_gain("mix", cols_b[:, 80:88], ada[:, 32:40])
            norm_mean("sum_mix", rstd[:, 0:T])
            norm_divide("mix", xT, hT, rstd[:, 0:T])
            norm_modulate("mix", hT, ada, 24)
            take_job("z_lat")
            empty_job(nc.vector.tensor_copy(latT[:, 0:2, :], job_wide("z_lat")))
            b = take_job("z_kv")
            nc.vector.tensor_copy(latT[:, 2, :], b[:, 0:T])
            empty_job(nc.vector.tensor_copy(squares[0:96, 3, :], b[0:96, T:2 * T]))
            for i in range(2):
                take_job(f"z_caq{i}")
                empty_job(nc.vector.tensor_scalar(ca_q[:, 2 * i:2 * i + 2, :], job_wide(f"z_caq{i}"), 0.125, None, ALU.mult))
            item("mid", "ada14")
            ada_col("col_ada14", 14)
            for i in range(2):
                take_job(f"z_cak{i}")
                empty_job(nc.vector.tensor_copy(ca_k[:, 2 * i:2 * i + 2, :], job_wide(f"z_cak{i}")))
            item("mid", "ada15")
            ada_col("col_ada15", 15)
            for i in range(2):
                take_job(f"z_cav{i}")
                empty_job(nc.vector.tensor_copy(ca_v[:, i, :], job_bank(f"z_cav{i}")[:, :]))
            b = take_job("lat_sum")
            nc.vector.tensor_scalar(rstd[:, 0:T], b[:, 0:T], 1.0 / 256, None, ALU.mult)
            empty_job(nc.vector.tensor_scalar(rstd[:, T:2 * T], b[:, T:2 * T], 1.0 / P, None, ALU.mult))
            item("mid", "ada16")
            ada_col("col_ada16", 16)
            dve.wait_ge(sem("lat_root"), 1)
            step(nc.vector.reciprocal(rstd[:, :], rstd[:, :]))
            for c in range(3):
                i = nc.vector.scalar_tensor_tensor(out=latT[:, c, :], in0=latT[:, c, :],
                                                   scalar=cols_b[:, ROWS_B["mla_q_norm"] + c:ROWS_B["mla_q_norm"] + c + 1],
                                                   in1=rstd[:, (c // 2) * T:(c // 2 + 1) * T], op0=ALU.mult, op1=ALU.mult)
            i.then_inc(sem("lat_ready"), 1)
            for i in range(4):
                take_job(f"z_ga{i}")
                empty_job(nc.vector.tensor_copy(gate_aT[:, 2 * i:2 * i + 2, :], job_wide(f"z_ga{i}")))
            item("mid", "ada17")
            ada_col("col_ada17", 17)
            for i in range(4):
                take_job(f"z_gb{i}_2")
                empty_job(nc.vector.tensor_copy(gate_bT[:, 2 * i:2 * i + 2, :], job_wide(f"z_gb{i}_2")))
            for i in range(4):
                take_job(f"mla_q{i}")
                empty_job(nc.vector.tensor_copy(mla_q[0:96, 2 * i:2 * i + 2, :], job_wide(f"mla_q{i}")[0:96, :, :]))
            for i in range(4):
                take_job(f"mla_k{i}")
                empty_job(nc.vector.tensor_copy(mla_k[0:64, 2 * i:2 * i + 2, :], job_wide(f"mla_k{i}")[0:64, :, :]))
            for i in range(2):
                take_job(f"mla_v{i}")
                empty_job(nc.vector.tensor_copy(mla_v[:, i, :], job_bank(f"mla_v{i}")[:, :]))
            nc.vector.tensor_copy(picked[:, 0, 36:37], picked[:, 0, 31:32]).then_inc(sem("mla_qk_ready"), 1)
            dve.wait_ge(sem("rope_ready"), 1)
            pe3 = pe_tmp.rearrange("p (a t) -> p a t", a=2)[64:96, :, :]
            cos, sin = tables(rope_cs[64:96, 1, :], rope_cs[64:96, 0, :], 2)
            for i in range(4):
                take_job(f"pe_rot{i}")
                q = mla_q[64:96, 2 * i:2 * i + 2, :]
                empty_job(nc.vector.tensor_tensor(pe3, job_wide(f"pe_rot{i}")[64:96, :, :], sin, ALU.mult))
                step(nc.vector.tensor_tensor(q, q, cos, ALU.mult))
                step(nc.vector.tensor_tensor(q, q, pe3, ALU.add))
            b = take_job("kpe_rot")
            kpe = squares[64:96, 3, :]
            empty_job(nc.vector.tensor_tensor(pe_tmp[64:96, 0:T], b[64:96, 0:T], rope_cs[64:96, 0, :], ALU.mult))
            step(nc.vector.tensor_tensor(kpe, kpe, rope_cs[64:96, 1, :], ALU.mult))
            step(nc.vector.tensor_tensor(kpe, kpe, pe_tmp[64:96, 0:T], ALU.add))
            nc.vector.tensor_copy(mla_k[64:96, :, :], squares[64:96, 3:4, :].broadcast_to((32, 8, T)))\
              .then_inc(sem("mla_ready"), 1)
            attention("mla")
            attention("ca")
            dve.wait_ge(sem("gates_ready"), 2)
            for i in range(4):
                pair = slice(2 * i, 2 * i + 2)
                take_job(f"branch_a{i}")
                empty_job(nc.vector.tensor_tensor(hT[:, pair, :], gate_aT[:, pair, :], job_wide(f"branch_a{i}"), ALU.mult))
                take_job(f"branch_b{i}")
                empty_job(nc.vector.tensor_tensor(gate_bT[:, pair, :], gate_bT[:, pair, :], job_wide(f"branch_b{i}"), ALU.mult))
                job_done_here()
                nc.vector.tensor_tensor(hT[:, pair, :], hT[:, pair, :], gate_bT[:, pair, :], ALU.add)\
                  .then_inc(sem("merged_ready"), 1)
            for i in range(4):
                residual_job(f"out2_{i}", i, ada, 40)
            make_gain("ffn2", cols_b[:, 88:96], ada[:, 56:64])
            norm_mean("sum_ffn2", rstd[:, 0:T])
            norm_divide("ffn2", xT, hT, rstd[:, 0:T])
            norm_modulate("ffn2", hT, ada, 48)
            feed_forward("ffn2", False, 64)
            norm_mean("sum_last", rstd[:, 0:T])
            norm_divide("last", xT, xT, rstd[:, 0:T])
            norm_gain("last", xT, "final_norm", col_b)
            for i in range(4):
                take_job(f"y_turn{i}")
                empty_job(nc.vector.tensor_copy(h_rows[:, i // 2, 512 * (i % 2):512 * (i % 2) + 512], job_bank(f"y_turn{i}")[:, :]))
            assert emptied[0] == len(JOBS)


_INS = ["x", "c", "ctx", "c_ctx", "w_mod", "b_mod", "norm1_g", "w_in", "q_norm_g", "k_norm_g", "conv_w", "attn_out_g",
        "conv_out_g", "w_out", "norm2_g", "w_group", "w_router", "w_gate", "w_up", "w_down", "final_g", "c_2",
        "positions_2", "w_ada_2", "b_ada_2", "ffn1_norm_2", "ffn1_w_in_2", "ffn1_w_out_2", "mix_norm_2", "w_in_2",
        "mla_q_norm_2", "mla_w_uq_2", "mla_kv_norm_2", "mla_w_ukv_2", "rel_bias_2", "w_branch_a_2",
        "w_branch_b_2", "w_out_2", "ffn2_norm_2", "ffn2_w_in_2", "ffn2_w_out_2", "final_norm_2"]


def shape_constants():
    import numpy as np

    offsets, width = const_offsets()
    out = np.zeros((P, width), np.float32)

    def put(name, value):
        at, n = offsets[name]
        out[:, at:at + n] = value

    i = np.arange(P)
    put("ident", np.eye(P))
    put("ones", 1.0)
    put("heads64", i[:, None] // 64 == i[None, :] // 64)
    put("reverse", i[:, None] + i[None, :] == P - 1)
    put("before", i[:, None] < i[None, :])
    first = (i % 32) < 16
    rot = np.zeros((P, P))
    rot[i[first] + 16, i[first]] = -1.0
    rot[i[~first] - 16, i[~first]] = 1.0
    put("rot_axial", rot)
    half = np.zeros((P, P))
    half[64:96, 64:96] = rot[64:96, 64:96]
    put("rot_half", half)
    put("slot", np.tile(np.arange(SLOTS), 2)[None, :])
    put("expert_id", np.arange(N_EXPERTS)[None, :])
    put("group_rank", (N_GROUPS - np.arange(N_GROUPS))[None, :])
    put("eps", EPS)
    inv_freq = (np.float32(10000.0) ** (-np.arange(0, 32, 2, dtype=np.float32) / np.float32(32))).astype(np.float32)
    put("inv_freq", inv_freq[i % 16][:, None])
    t = np.arange(T)
    where = np.where((i[:, None] % 64) < 32, (t // 64)[None, :], (t % 64)[None, :]).astype(np.float32)
    angle = (where * inv_freq[i % 16][:, None]).astype(np.float32)
    put("axial_cos", np.cos(angle))
    put("axial_sin", np.sin(angle))
    return out


def kernel(**inputs):
    import numpy as _np
    import concourse.bacc as _bacc
    from concourse import mybir as _mybir
    from concourse.bass_utils import run_bass_kernel_spmd as _run

    nc = _bacc.Bacc("TRN2", target_bir_lowering=False, num_devices=1, dynamic_dma_scratch_size=4096)
    arrays, aps = {}, {}
    given = {name: _np.ascontiguousarray(inputs[name]) for name in _INS}
    given["shape_constants"] = shape_constants()
    for name, a in given.items():
        arrays[f"in_{name}_dram"] = a
        aps[name] = nc.dram_tensor(f"in_{name}_dram", a.shape, _mybir.dt.from_np(a.dtype), kind="ExternalInput").ap()
    out = nc.dram_tensor("out_0_dram", (1, T, D), _mybir.dt.float32, kind="ExternalOutput").ap()
    mixed_blocks_kernel(nc, aps, out)
    r = _run(nc, [arrays], core_ids=[0])
    return r.results[0]["out_0_dram"]
```

```python
import concourse.bass as bass
from concourse import mybir
from contextlib import ExitStack

F32 = mybir.dt.float32
BF16 = mybir.dt.bfloat16
I32 = mybir.dt.int32
U32 = mybir.dt.uint32
ALU = mybir.AluOpType
ACT = mybir.ActivationFunctionType
AX_X = mybir.AxisListType.X

P = 128
T = 256
D = 1024
KD = D // P
EPS = 1e-6
N_GROUPS, GROUP_SIZE = 4, 8
N_EXPERTS = N_GROUPS * GROUP_SIZE
D_EXPERT = 768
HALF_E = D_EXPERT // 2
SLOTS = 64
PASSES = T // SLOTS
D_FF = 2816
FF_CHUNK = 256
FF_LOOPS = (D_FF // FF_CHUNK - 1) // 2
CHUNK = 64
NO_SLOT = 10000.0
NEG = -1e30
ROPE_SCALE_2 = 96 ** -0.5
TWO_PI = 6.283185307179586
PI_A, PI_B = 6.28125, 0.0019350051879882812
PI_C = TWO_PI - PI_A - PI_B

CONST_COLS = [("ident", 128), ("ones", 128), ("mean", 128), ("heads64", 128), ("rot_axial", 128), ("rot_half", 128),
              ("reverse", 128), ("before", 128), ("slot", 128), ("expert_id", 32), ("group_rank", 4),
              ("eps", 1), ("inv_freq", 1), ("select", 2), ("axial_cos", 256), ("axial_sin", 256)]


def const_offsets():
    at, out = 0, {}
    for name, width in CONST_COLS:
        out[name] = (at, width)
        at += width
    return out, at


ROWS_A = {"b_mod": 0, "norm1_g": 48, "norm2_g": 56, "final_g": 64, "c": 72, "c_ctx": 80, "q_norm_g": 88,
          "k_norm_g": 89, "attn_out_g": 90, "conv_out_g": 94, "conv_w": 98}
N_ROWS_A = 110
ROWS_B = {"b_ada": 0, "ffn1_norm": 72, "mix_norm": 80, "ffn2_norm": 88, "final_norm": 96, "c": 104,
          "mla_q_norm": 112, "mla_kv_norm": 114}
N_ROWS_B = 115

JOBS = (["rows_a", "rows_b"] + [f"x_turn{i}" for i in range(4)] + [f"ctx_turn{i}" for i in range(4)]
        + ["sum_x", "sum_ctx", "modrow0", "modrow1", "mod0", "modrow2", "mod1", "modrow3", "mod2", "mod3"]
        + ["z_k", "z_v", "col_gt1a", "z_q0", "z_q1", "col_gt1b", "z_gb0", "z_gb1", "col_sh2a",
           "z_gc0", "z_gc1", "col_sh2b", "z_u0", "z_u1", "col_sc2a"]
        + [f"qk_sum{i}" for i in range(3)] + ["row_sc2b", "row_gt2a", "col_sc2b", "col_gt2a"] + [f"qk_rot{i}" for i in range(3)]
        + [f"attn_o{i}" for i in range(4)] + [f"head_sum{i}" for i in range(4)] + ["row_gt2b", "col_gt2b"]
        + [f"merge{i}" for i in range(4)] + ["sum_n2", "logits"] + [f"h2_turn{i}" for i in range(4)]
        + ["positions", "bias_turn"]
        + ["row_ada0", "sum_final", "row_ada1", "col_ada0", "row_ada2", "col_ada1", "row_ada3", "col_ada2", "col_ada3", "sum_ffn1"]
        + ["sum_mix", "z_lat", "z_kv", "z_caq0", "z_caq1", "col_ada14", "z_cak0", "z_cak1", "col_ada15", "z_cav0", "z_cav1",
           "lat_sum", "col_ada16", "z_ga0", "z_ga1", "z_ga2", "z_ga3", "col_ada17", "z_gb0_2", "z_gb1_2", "z_gb2_2", "z_gb3_2"]
        + [f"mla_q{i}" for i in range(4)] + [f"mla_k{i}" for i in range(4)] + ["mla_v0", "mla_v1"]
        + [f"pe_rot{i}" for i in range(4)] + ["kpe_rot"]
        + [f"mla_o{i}" for i in range(4)] + [f"ca_o{i}" for i in range(4)]
        + [f"branch_{ab}{i}" for i in range(4) for ab in "ab"] + [f"out2_{i}" for i in range(4)]
        + ["sum_ffn2", "sum_last"] + [f"y_turn{i}" for i in range(4)])
JOB = {name: j for j, name in enumerate(JOBS)}
assert len(JOB) == len(JOBS)

RING = 6
SLOT_W = 4096
PRE = ([(f"mod{i}", f"modrow{i}") for i in range(4)]
       + [("w_kv", "z_v"), ("gt1a", 0), ("w_q", "z_q1"), ("gt1b", 1), ("w_gb", "z_gb1"), ("sh2a", 2), ("w_gc", "z_gc1"),
          ("sh2b", 3), ("w_u", "z_u1"), ("sc2a", 4), ("sc2b", "row_sc2b"), ("gt2a", "row_gt2a"), ("gt2b", "row_gt2b"), ("w_out0", "merge1"),
          ("w_out1", "merge3")])
MID = ([("ada14", 15), ("w2_lat", "z_kv"), ("w2_caq", "z_caq1"), ("w2_cak", "z_cak1"), ("ada15", 16), ("w2_cav", "z_cav1"),
        ("ada16", 17), ("w2_ga0", "z_ga1"), ("w2_ga1", "z_ga3"), ("ada17", 18), ("w2_gb0", "z_gb1_2"),
        ("w2_gb1", "z_gb3_2"), ("mla_up", "mla_v1"), ("w_branch_a", "branch_a3"), ("w_branch_b", "branch_b3"),
        ("w_out2_0", "out2_1"), ("w_out2_1", "out2_3")])


def ring_places():
    place, loads = {}, [0] * RING
    for part, items in (("pre", PRE), ("ada", [(f"ada{i}", f"row_ada{i}") for i in range(4)]), ("mid", MID)):
        for at, (name, _) in enumerate(items):
            s = at % RING
            if name == "w_out1":
                s = 4
            if name != "mla_up":
                loads[s] += 1
            place[(part, name)] = (s, loads[s])
    return place


def mixed_blocks_kernel(nc, ins, out):
    C, n_const = const_offsets()
    PLACE = ring_places()

    with ExitStack() as ctx:
        def sb(name, shape, dt=F32):
            return ctx.enter_context(nc.sbuf_tensor(name, shape, dt))

        sems = {}

        def sem(name):
            if name not in sems:
                sems[name] = ctx.enter_context(nc.semaphore(name))
            return sems[name]

        consts = sb("consts", [P, n_const])
        rows_a = sb("rows_a", [N_ROWS_A, P])
        rows_b = sb("rows_b", [N_ROWS_B, P])
        cols_a = sb("cols_a", [P, N_ROWS_A])
        cols_b = sb("cols_b", [P, N_ROWS_B])
        xT = sb("xT", [P, KD, T])
        hT = sb("hT", [P, KD, T])
        squares = sb("squares", [P, KD, T])
        mixT = sb("mixT", [P, KD, T])
        h_rows = sb("h_rows", [P, 2, D])
        rstd = sb("rstd", [P, 2 * T])
        small = sb("small", [P, 2048])
        cond = sb("cond", [P, KD, 32])
        cond_ada = sb("cond_ada", [P, KD, 32])
        warmed = sb("warmed", [1, 32])
        cond2 = sb("cond2", [P, KD])
        mod = sb("mod", [P, 6 * KD])
        mod_ctx = sb("mod_ctx", [P, 2 * KD])
        ada = sb("ada", [P, 9 * KD])
        gains = sb("gains", [P, 3 * KD])
        mod_acc = sb("mod_acc", [P, 2, 512])
        stats = sb("stats", [P, 3, 3, 16])
        router = sb("router", [P, KD, 36])
        route = sb("route", [P, 2, 168])
        picked = sb("picked", [P, 2, 40])
        picked_i = sb("picked_i", [P, 2, 8], U32)
        busiest = sb("busiest", [1, 1], I32)
        zeros = sb("zeros", [P, 512], BF16)
        ARENA = 9 * SLOT_W
        arena = sb("arena", [P, ARENA])

        def ring(slot):
            return arena[:, slot * SLOT_W:(slot + 1) * SLOT_W]

        def ring_w(part, name):
            return ring(PLACE[(part, name)][0]).rearrange("p (k n) -> p k n", k=KD)

        EW = KD * D_EXPERT

        def expert_w(u):
            base = 3 * EW * u
            gate = arena[:, base:base + EW].rearrange("p (k n) -> p k n", k=KD)
            up = arena[:, base + EW:base + 2 * EW].rearrange("p (k n) -> p k n", k=KD)
            down = arena[:, base + 2 * EW:base + 3 * EW].rearrange("p (k n) -> p k n", k=6)
            return gate, up, down

        temp_at = [RING * SLOT_W]

        def temp(*shape):
            n = 1
            for s in shape:
                n *= s
            a = arena[:, temp_at[0]:temp_at[0] + n]
            temp_at[0] += n
            assert temp_at[0] <= ARENA
            if len(shape) == 1:
                return a
            names = "abc"[:len(shape)]
            spec = {names[i]: shape[i] for i in range(len(shape))}
            return a.rearrange(f"p ({' '.join(names)}) -> p {' '.join(names)}", **spec)

        logits, assigned = route[:, :, 0:36], route[:, :, 36:68]
        places, weights = route[:, :, 68:101], route[:, :, 101:134]
        route_tmp = route[:, :, 134:166]
        rel_bias_rows = sb("rel_bias_rows", [P, 4, 8])
        half_gate = sb("half_gate", [P, KD])
        x_rows, ctx_rows = temp(2, D), temp(2, D)
        ctxT = h_rows[:, :, :].rearrange("p b (k t) -> p (b k) t", t=T)
        ctx_squares = x_rows.rearrange("p b (k t) -> p (b k) t", t=T)
        gate_aT, gate_bT = ctxT, mixT[:, :, :]
        qk = temp(6, T)
        v1 = temp(4, P)
        gate_b = temp(4, T)
        conv_in = temp(4, T + 2)
        conv_out = temp(4, T)
        qk_tmp = temp(6, T)
        temp_at[0] = RING * SLOT_W
        mla_q, mla_k = temp(8, T), temp(8, T)
        mla_v = temp(2, 512)
        ca_q, ca_k, ca_v = temp(4, T), temp(4, T), temp(2, 512)
        ca_bias = temp(3072)
        bias_early = ca_bias[:, 0:8 * P].rearrange("p (h k) -> p h k", h=8)
        bias_late = ca_bias[:, 8 * P:24 * P].rearrange("p (h k) -> p h k", h=8)
        latT = small[:, 0:3 * T].rearrange("p (c t) -> p c t", c=3)
        pe_tmp = small[:, 768:768 + 512]
        angle = squares[:, 0:5, :]
        bias_rows = small[0:8, 1536:2048]
        rope_cs = sb("rope_cs", [P, 2, T])
        turns = squares[:, 5, :].bitcast(I32)
        probs = small[:, 0:1024].rearrange("p (b k) -> p b k", b=2)
        probsT = small[:, 1024:2048].rearrange("p (b n) -> p b n", b=2)
        pick = mixT[:, 0, 0:2 * SLOTS].rearrange("p (b s) -> p b s", b=2)
        pick_w = mixT[:, 1, :].rearrange("p (b s) -> p b s", b=2)
        xeT = mixT[:, 2:4, :].rearrange("p a t -> p (a t)").rearrange("p (k s) -> p k s", k=KD)
        gate_act = mixT[:, 4:6, :].rearrange("p a t -> p (a t)")[:, 0:HALF_E]
        hidden = mixT[:, 6:8, :].rearrange("p a t -> p (a t)")[:, 0:HALF_E]
        hiddenT = small[:, 0:HALF_E].rearrange("p (c s) -> p c s", c=3)
        y_e = small[:, 512:1024]
        pick_wT = small[:, 1024:1536].rearrange("p (b t) -> p b t", b=2)
        silu_g = small[:, 0:512].rearrange("p (b t) -> p b t", b=2)
        ff_act = small[:, 512:1024].rearrange("p (b t) -> p b t", b=2)

        bank = [ctx.enter_context(nc.psum_tensor(f"bank{i}", [P, 512], F32)) for i in range(8)]
        bias_scratch = nc.dram_tensor("bias_scratch", (8, 512), F32, kind="Internal").ap()

        def K(name):
            at, width = C[name]
            return consts[:, at:at + width]

        def col_a(name, i=0):
            return cols_a[:, ROWS_A[name] + i:ROWS_A[name] + i + 1]

        def col_b(name, i=0):
            return cols_b[:, ROWS_B[name] + i:ROWS_B[name] + i + 1]

        def job_bank(name):
            return bank[JOB[name] % 4]

        def job_wide(name):
            return job_bank(name)[:, :].rearrange("p (a t) -> p a t", a=2)

        SET = {"n1": 0, "c1": 1, "n2": 0, "ffn1": 1, "mix": 2, "ffn2": 0}

        def gain(key, k):
            return gains[:, SET[key] * KD + k:SET[key] * KD + k + 1]

        def attention_1():
            for h in range(8):
                g = 64 * (h // 4)
                for qb in range(2):
                    yield dict(job=f"attn_o{h // 2}", last=(h % 2 == 1 and qb == 1), col=64 * (h % 2), qb=qb, keys=512,
                               q=[qk[g:g + 64, h % 4, qb * P:qb * P + P]],
                               k=[qk[g:g + 64, 4:6, :].rearrange("p a t -> p (a t)")],
                               v=[v1[:, b, g:g + 64] for b in range(4)], mask=False)

        def attention_mla():
            for h in range(8):
                for qb in range(2):
                    n = (qb + 1) * P
                    yield dict(job=f"mla_o{h // 2}", last=(h % 2 == 1 and qb == 1), col=64 * (h % 2), qb=qb, keys=n,
                               q=[mla_q[0:96, h, qb * P:qb * P + P]], k=[mla_k[0:96, h, 0:n]],
                               v=[mla_v[:, b, 64 * h:64 * h + 64] for b in range(qb + 1)], mask=True)

        def attention_ca():
            for h in range(8):
                p = 64 * (h % 2)
                for qb in range(2):
                    n = (qb + 1) * P
                    bias = bias_late[:, h, :] if qb else bias_early[:, h, :]
                    yield dict(job=f"ca_o{h // 2}", last=(h % 2 == 1 and qb == 1), col=p, qb=qb, keys=n,
                               q=[ca_q[p:p + 64, h // 2, qb * P:qb * P + P], K("reverse")],
                               k=[ca_k[p:p + 64, h // 2, 0:n], bias],
                               v=[ca_v[:, b, 64 * h:64 * h + 64] for b in range(qb + 1)], mask=True)

        ATTENTIONS = {"at1": (0, list(attention_1()), 0.125), "mla": (1, list(attention_mla()), ROPE_SCALE_2),
                      "ca": (2, list(attention_ca()), 1.0)}
        ATT_OUT = {"at1": lambda c: mixT[:, c, :], "mla": lambda c: squares[:, c, :], "ca": lambda c: squares[:, 4 + c, :]}

        block = ctx.enter_context(nc.Block())

        def wait_item_read(eng, reader):
            if isinstance(reader, int):
                eng.wait_ge(sem("mod_acc_step"), 8 * (reader + 1))
            else:
                eng.wait_ge(sem("job_ready"), JOB[reader] + 1)

        def chunked(ap, lo, hi):
            return ap[:, lo:hi].rearrange("(k p) n -> p k n", p=P)

        @block.sync
        def _(sp):
            readers = {}

            def load(part, name, src, reader, width=512, k=KD):
                slot, use = PLACE[(part, name)]
                if slot in readers:
                    wait_item_read(sp, readers[slot])
                dst = ring(slot).rearrange("p (k n) -> p k n", k=k)[:, :, 0:width]
                sp.dma_start(dst, src).then_inc(sem(f"ring_full{slot}"), 16)
                readers[slot] = reader

            sp.dma_start(x_rows, ins["x"][0].rearrange("(b p) d -> p b d", p=P)).then_inc(sem("x_loaded"), 16)
            sp.dma_start(ctx_rows, ins["ctx"][0].rearrange("(b p) d -> p b d", p=P)).then_inc(sem("ctx_loaded"), 16)
            w_mod, w_in, w_out = ins["w_mod"][0], ins["w_in"][0], ins["w_out"][0]
            seg = {"gt1a": 2048, "gt1b": 2560, "sh2a": 3072, "sh2b": 3584, "sc2a": 4096, "sc2b": 4608, "gt2a": 5120, "gt2b": 5632}
            win = {"w_q": (0, 512), "w_kv": (512, 256), "w_gb": (768, 512), "w_gc": (1280, 512), "w_u": (1792, 512)}
            for name, reader in PRE:
                if name in win:
                    at, width = win[name]
                    load("pre", name, chunked(w_in, at, at + width), reader, width)
                elif name.startswith("w_out"):
                    at = 512 * int(name[-1])
                    load("pre", name, chunked(w_out, at, at + 512), reader)
                else:
                    at = seg[name] if name in seg else 512 * int(name[-1])
                    load("pre", name, chunked(w_mod, at, at + 512), reader)

            w_gate, w_up, w_down = ins["w_gate"][0], ins["w_up"][0], ins["w_down"][0]

            def load_gate_up(u, e):
                gate, up, _ = expert_w(u)
                sp.dma_start(gate, w_gate[bass.ds(e, 1)].rearrange("a (k p) n -> p (a k) n", p=P))\
                  .then_inc(sem(f"gate_full{u}"), 16)
                sp.dma_start(up, w_up[bass.ds(e, 1)].rearrange("a (k p) n -> p (a k) n", p=P))\
                  .then_inc(sem(f"up_full{u}"), 16)

            def load_down(u, e):
                _, _, down = expert_w(u)
                sp.dma_start(down, w_down[bass.ds(e, 1)].rearrange("a (k p) n -> p (a k) n", p=P))\
                  .then_inc(sem(f"down_full{u}"), 16)

            def load_expert(u, e, done):
                sp.wait_ge(sem("gate_up_done"), done)
                load_gate_up(u, e)
                sp.wait_ge(sem("down_done"), done)
                load_down(u, e)

            for s in range(3):
                wait_item_read(sp, readers[s])
            load_gate_up(0, 0)
            for s in range(3, RING):
                wait_item_read(sp, readers[s])
            readers.clear()
            load_down(0, 0)
            sp.wait_ge(sem("mg_ready"), KD)
            load_gate_up(1, 1)
            load_down(1, 1)
            with sp.Fori(1, N_EXPERTS // 2) as it:
                for u in range(2):
                    load_expert(u, it * 2 + u, it * 2 + u - 1)
            sp.wait_ge(sem("busiest_ready"), 1)
            most = sp.value_load(busiest[0:1, 0:1], min_val=0, max_val=T)
            with sp.If(most > SLOTS):
                with sp.Fori(1, PASSES) as ps:
                    with sp.Fori(0, N_EXPERTS // 2) as it:
                        for u in range(2):
                            load_expert(u, it * 2 + u, ps * N_EXPERTS + it * 2 + u - 1)
                sp.wait_ge(sem("gate_up_done"), PASSES * N_EXPERTS)
                sp.wait_ge(sem("down_done"), PASSES * N_EXPERTS)

            w_ada = ins["w_ada_2"][0]
            sp.wait_ge(sem("gate_up_done"), N_EXPERTS - 1)
            sp.wait_ge(sem("down_done"), N_EXPERTS - 1)
            for i in range(4):
                load("ada", f"ada{i}", chunked(w_ada, 512 * i, 512 * i + 512), f"row_ada{i}")

            def load_ff_in(slot, w, c, key):
                dst = ring(slot).rearrange("p (k g n) -> p k g n", k=KD, g=2)
                for g in range(2):
                    sp.dma_start(dst[:, :, g, :], w[:, bass.ds(c * FF_CHUNK + g * D_FF, FF_CHUNK)]
                                 .rearrange("(k p) n -> p k n", p=P)).then_inc(sem(f"{key}_in_full{slot}"), 16)

            def load_ff_out(slot, w, c, key):
                dst = ring(slot)[:, 0:2 * D].rearrange("p (k n) -> p k n", k=2)
                sp.dma_start(dst, w[bass.ds(c * FF_CHUNK, FF_CHUNK), :].rearrange("(k p) n -> p k n", p=P))\
                  .then_inc(sem(f"{key}_out_full{slot}"), 16)

            def load_ada(it, u):
                sp.wait_ge(sem("mod_acc_step"), it * 16 + 8 * (4 + u))
                sp.dma_start(ring(4 + u).rearrange("p (k n) -> p k n", k=KD),
                             w_ada[:, bass.ds(it * 1024 + (4 + u) * 512, 512)]
                             .rearrange("(k p) n -> p k n", p=P)).then_inc(sem(f"ada_full{4 + u}"), 16)

            def feed_forward(key, w_in_ff, w_out_ff, with_ada):
                for s in (2, 3):
                    wait_item_read(sp, readers[s])
                load_ff_in(2, w_in_ff, 0, key)
                load_ff_out(3, w_out_ff, 0, key)
                for s in (0, 1):
                    wait_item_read(sp, readers[s])
                if with_ada:
                    sp.wait_ge(sem("experts_done"), 1)
                with sp.Fori(0, FF_LOOPS) as it:
                    sp.wait_ge(sem(f"{key}_gate_up_done"), it * 4 + 1)
                    load_ff_in(0, w_in_ff, it * 2 + 1, key)
                    if with_ada:
                        load_ada(it, 0)
                    sp.wait_ge(sem(f"{key}_down_done"), it * 4 + 1)
                    load_ff_out(1, w_out_ff, it * 2 + 1, key)
                    sp.wait_ge(sem(f"{key}_gate_up_done"), it * 4 + 2)
                    load_ff_in(2, w_in_ff, it * 2 + 2, key)
                    if with_ada:
                        load_ada(it, 1)
                    sp.wait_ge(sem(f"{key}_down_done"), it * 4 + 2)
                    load_ff_out(3, w_out_ff, it * 2 + 2, key)
                sp.wait_ge(sem(f"{key}_sum_done"), 1)
                readers.clear()

            feed_forward("ffn1", ins["ffn1_w_in_2"][0], ins["ffn1_w_out_2"][0], True)
            w_in2 = ins["w_in_2"][0]
            w2 = {"w2_lat": (0, 416), "w2_caq": (416, 512), "w2_cak": (928, 512), "w2_cav": (1440, 512),
                  "w2_ga0": (1952, 512), "w2_ga1": (2464, 512), "w2_gb0": (2976, 512), "w2_gb1": (3488, 512)}
            sp.wait_ge(sem("mod_acc_step"), 8 * 15)
            for name, reader in MID:
                if name.startswith("ada"):
                    i = int(name[3:])
                    load("mid", name, chunked(w_ada, 512 * i, 512 * i + 512), reader)
                elif name == "mla_up":
                    slot, _ = PLACE[("mid", name)]
                    wait_item_read(sp, readers[slot])
                    sp.dma_start(ring(slot)[:, 0:1536].rearrange("p (k n) -> p k n", k=2),
                                 ins["mla_w_uq_2"][0].rearrange("(k p) n -> p k n", p=P)).then_inc(sem("w_uq_full"), 16)
                    sp.dma_start(ring(slot)[:, 1536:2560], ins["mla_w_ukv_2"][0]).then_inc(sem("w_ukv_full"), 16)
                    readers[slot] = reader
                elif name.startswith("w_branch"):
                    load("mid", name, chunked(ins[name + "_2"][0], 0, D), reader, D, 4)
                elif name.startswith("w_out2"):
                    at = 512 * int(name[-1])
                    load("mid", name, chunked(ins["w_out_2"][0], at, at + 512), reader)
                else:
                    at, width = w2[name]
                    load("mid", name, chunked(w_in2, at, at + width), reader, width)
            feed_forward("ffn2", ins["ffn2_w_in_2"][0], ins["ffn2_w_out_2"][0], False)
            sp.wait_ge(sem("job_emptied"), len(JOBS))
            sp.dma_start(out[0].rearrange("(b p) d -> p b d", p=P), h_rows[:, :, :]).then_inc(sem("stored"), 16)
            sp.wait_ge(sem("stored"), 16)

        @block.gpsimd
        def _(pool):
            n_step = [0]

            def step(instruction):
                n_step[0] += 1
                instruction.then_inc(sem("pool_step"), 1)
                pool.wait_ge(sem("pool_step"), n_step[0])

            pool.wait_ge(sem("job_emptied"), JOB["z_u1"] + 1)
            for tap in range(3):
                for c in range(4):
                    w = col_a("conv_w", 4 * tap + c)
                    dst = conv_out[:, c, :] if tap == 0 else mixT[:, 4 + c, :]
                    i = nc.gpsimd.tensor_scalar(dst, conv_in[:, c, tap:tap + T], w, 0.0, ALU.mult, ALU.add)
                step(i)
                if tap:
                    step(nc.gpsimd.tensor_tensor(conv_out, conv_out, mixT[:, 4:8, :], ALU.add))
            nc.gpsimd.tensor_tensor(mixT[:, 4:8, :], conv_out, gate_b, ALU.mult).then_inc(sem("conv_done"), 1)
            pool.wait_ge(sem("job_emptied"), JOB["bias_turn"] + 1)
            pool.dma_start(bias_scratch, bias_rows).then_inc(sem("bias_stored"), 16)
            pool.wait_ge(sem("bias_stored"), 16)
            pool.wait_ge(sem("experts_done"), 1)
            for tile, first in ((bias_early, 129), (bias_late, 1)):
                src = bass.AP(bias_scratch.tensor, first, [[1, P], [512, 8], [1, tile.shape[2]]])
                pool.dma_start(tile, src).then_inc(sem("bias_loaded"), 16)


        @block.scalar
        def _(act):
            n_step = [0]

            def step(instruction):
                n_step[0] += 1
                instruction.then_inc(sem("act_step"), 1)
                act.wait_ge(sem("act_step"), n_step[0])

            n_warm = [0]

            def warm(function):
                act.wait_ge(sem("consts_loaded"), 16)
                nc.scalar.activation(warmed[0:1, n_warm[0]:n_warm[0] + 1], K("eps")[0:1, :], function)
                n_warm[0] += 1

            act.dma_start(consts[:, :], ins["shape_constants"]).then_inc(sem("consts_loaded"), 16)
            act.dma_start(rows_a[:, :], ins["vectors_a"]).then_inc(sem("rows_a_loaded"), 16)
            act.dma_start(rows_b[:, :], ins["vectors_b"]).then_inc(sem("rows_b_loaded"), 16)
            act.dma_start(turns[64:96, :], ins["positions_2"][0].partition_broadcast(32)).then_inc(sem("positions_loaded"), 16)
            act.dma_start(router[:, :, 0:4], ins["w_group"][0].rearrange("(k p) n -> p k n", p=P))\
               .then_inc(sem("router_loaded"), 16)
            act.dma_start(router[:, :, 4:36], ins["w_router"][0].rearrange("(k p) n -> p k n", p=P))\
               .then_inc(sem("router_loaded"), 16)
            for b in range(4):
                act.dma_start(rel_bias_rows[:, b, :], ins["rel_bias_2"][0][385 - P * b:513 - P * b, :])\
                   .then_inc(sem("rel_bias_loaded"), 16)

            act.wait_ge(sem("cond_zeroed"), 1)
            act.wait_ge(sem("job_emptied"), 1)
            for i, name in enumerate(("c", "c_ctx")):
                r = ROWS_A[name]
                ins_ = nc.scalar.activation(cond[:, :, i], cols_a[:, r:r + KD], ACT.Silu)
                ins_.then_inc(sem("cond_ready"), 1)
            act.wait_ge(sem("job_emptied"), 2)
            c2 = cols_b[:, ROWS_B["c"]:ROWS_B["c"] + KD]
            nc.scalar.activation(cond2[:, :], c2, ACT.Silu).then_inc(sem("cond_ready"), 1)
            nc.scalar.activation(cond_ada[:, :, 0], c2, ACT.Silu).then_inc(sem("cond_ready"), 1)

            def head_squares(key, src, dst, source, value=1):
                act.wait_ge(sem(source), value)
                nc.scalar.activation(dst, src, ACT.Square).then_inc(sem(f"{key}_squares"), 1)
                warm(ACT.Sqrt)

            def norm_squares(key, src, dst, source, first, by):
                for i in range(KD // 2):
                    act.wait_ge(sem(source), first + by * i)
                    nc.scalar.activation(dst[:, 2 * i:2 * i + 2, :], src[:, 2 * i:2 * i + 2, :], ACT.Square)\
                      .then_inc(sem(f"{key}_squares"), 1)

            def norm_root(key, job, dst):
                act.wait_ge(sem("job_ready"), JOB[job] + 1)
                nc.scalar.activation(dst, job_bank(job)[:, 0:T], ACT.Sqrt, bias=K("eps")).then_inc(sem(f"{key}_root"), 1)

            def head_root(key, jobs, dst):
                for i, job in enumerate(jobs):
                    act.wait_ge(sem("job_ready"), JOB[job] + 1)
                    nc.scalar.activation(dst[:, 2 * i:2 * i + 2, :], job_wide(job), ACT.Sqrt, bias=K("eps"))\
                      .then_inc(sem(f"{key}_root"), 1)

            def norm_shift(key, dst, shifts, shift_at):
                for k in range(KD):
                    act.wait_ge(sem(f"{key}_scaled"), k + 1)
                    nc.scalar.activation(dst[:, k, :], dst[:, k, :], ACT.Identity,
                                         bias=shifts[:, shift_at + k:shift_at + k + 1]).then_inc(sem(f"{key}_ready"), 1)

            act.wait_ge(sem("angles_ready"), 1)
            nc.scalar.activation(rope_cs[64:96, :, :], angle[64:96, 2:4, :], ACT.Sin).then_inc(sem("rope_ready"), 1)
            act.wait_ge(sem("rope_ready"), 1)

            def attention(key):
                index, instances, scale = ATTENTIONS[key]
                n = len(instances)
                for i in range(n + 2):
                    if i < n:
                        it = instances[i]
                        act.wait_ge(sem(f"{key}_negmax"), i + 1)
                        if i >= 2:
                            act.wait_ge(sem(f"{key}_turned"), i - 1)
                        nc.scalar.activation(probs[:, i % 2, 0:it["keys"]], bank[4 + i % 2][:, 0:it["keys"]], ACT.Exp,
                                             bias=stats[:, index, 0, i:i + 1], scale=scale,
                                             accum_out=stats[:, index, 1, i:i + 1]).then_inc(sem(f"{key}_exp"), 1)
                    if i >= 2:
                        j = i - 2
                        act.wait_ge(sem(f"{key}_turned"), j + 1)
                        w = instances[j]["keys"]
                        nc.scalar.activation(probsT[:, j % 2, 0:w], bank[6 + j % 2][:, 0:w], ACT.Copy)\
                          .then_inc(sem(f"{key}_probsT"), 1)

            norm_squares("n1", xT, squares, "job_emptied", JOB["x_turn0"] + 1, 1)
            act.wait_ge(sem("job_ready"), JOB["x_turn3"] + 1)
            norm_squares("c1", ctxT, ctx_squares, "job_emptied", JOB["ctx_turn0"] + 1, 1)
            warm(ACT.Sqrt)
            norm_root("n1", "sum_x", rstd[:, 0:T])
            norm_root("c1", "sum_ctx", rstd[:, T:2 * T])
            norm_shift("c1", mixT, mod_ctx, 0)
            norm_shift("n1", hT, mod, 0)
            head_squares("qk", qk, squares[:, 0:6, :], "job_emptied", JOB["z_q1"] + 1)
            head_root("qk", [f"qk_sum{i}" for i in range(3)], qk_tmp)
            warm(ACT.Exp)
            attention("at1")
            act.wait_ge(sem("conv_done"), 1)
            head_squares("mg", mixT[:, :, :], squares[:, :, :], "job_emptied", JOB["attn_o3"] + 1)
            head_root("mg", [f"head_sum{i}" for i in range(4)], h_rows[:, :, :].rearrange("p b (k t) -> p (b k) t", t=T))
            norm_squares("n2", xT, squares, "job_emptied", JOB["merge0"] + 1, 1)
            norm_root("n2", "sum_n2", rstd[:, 0:T])
            norm_shift("n2", hT, mod, 24)
            warm(ACT.Exp)
            act.wait_ge(sem("router_max"), 2)
            for b in range(2):
                nc.scalar.activation(picked[:, b, 4:8], route[:, b, 0:4], ACT.Exp, bias=picked[:, b, 0:1],
                                     accum_out=picked[:, b, 1:2]).then_inc(sem("group_exp"), 1)
            act.wait_ge(sem("router_top"), 2)
            for b in range(2):
                nc.scalar.activation(picked[:, b, 2:3], picked[:, b, 17:18], ACT.Exp, bias=picked[:, b, 3:4])\
                  .then_inc(sem("second_exp"), 1)

            def expert_in(count):
                act.wait_ge(sem("gathered"), count)
                nc.scalar.activation(xeT, bank[6][:, :].rearrange("p (k s) -> p k s", k=KD), ACT.Copy)\
                  .then_inc(sem("xe_ready"), 1)

            def expert_steps(n, prep):
                act.wait_ge(sem("gate_up_done"), n)
                nc.scalar.activation(gate_act, bank[4][:, 0:HALF_E], ACT.Silu).then_inc(sem("gate_act_ready"), 1)
                expert_in(prep)
                act.wait_ge(sem("hidden_turned"), n)
                nc.scalar.activation(hiddenT, bank[5][:, 0:HALF_E].rearrange("p (c s) -> p c s", c=3), ACT.Copy)\
                  .then_inc(sem("hiddenT_ready"), 1)
                act.wait_ge(sem("down_done"), n)
                nc.scalar.activation(y_e, bank[6][:, :], ACT.Copy).then_inc(sem("y_ready"), 1)

            expert_in(1)
            with act.Fori(0, N_EXPERTS // 2) as it:
                for u in range(2):
                    expert_steps(it * 2 + u + 1, it * 2 + u + 2)
            act.wait_ge(sem("busiest_ready"), 1)
            most = act.value_load(busiest[0:1, 0:1], min_val=0, max_val=T)
            with act.If(most > SLOTS):
                with act.Fori(1, PASSES) as ps:
                    expert_in(ps * (N_EXPERTS + 1) + 1)
                    with act.Fori(0, N_EXPERTS // 2) as it:
                        for u in range(2):
                            expert_steps(ps * N_EXPERTS + it * 2 + u + 1, ps * (N_EXPERTS + 1) + it * 2 + u + 2)

            warm(ACT.Sqrt)
            norm_squares("fin1", xT, squares, "y_moe_read", 1, 1)
            norm_root("fin1", "sum_final", rstd[:, 0:T])

            def feed_forward(key):
                def one(s, parity):
                    act.wait_ge(sem(f"{key}_gate_up_done"), s)
                    nc.scalar.activation(silu_g[:, parity, :], bank[4 + parity][:, 0:T], ACT.Silu)\
                      .then_inc(sem(f"{key}_silu"), 1)
                one(1, 0)
                one(2, 1)
                with act.Fori(0, FF_LOOPS) as it:
                    for j in range(4):
                        one(it * 4 + j + 3, j % 2)

            norm_squares("ffn1", xT, squares, "fin1_ready", 2, 2)
            norm_root("ffn1", "sum_ffn1", rstd[:, 0:T])
            norm_shift("ffn1", hT, ada, 0)
            warm(ACT.Silu)
            feed_forward("ffn1")
            warm(ACT.Sqrt)
            norm_squares("mix", xT, squares, "ffn1_sum_read", 1, 1)
            norm_root("mix", "sum_mix", rstd[:, 0:T])
            norm_shift("mix", hT, ada, 24)
            head_squares("lat", latT, squares[:, 0:3, :], "job_emptied", JOB["z_kv"] + 1)
            act.wait_ge(sem("job_emptied"), JOB["lat_sum"] + 1)
            nc.scalar.activation(rstd[:, :], rstd[:, :], ACT.Sqrt, bias=K("eps")).then_inc(sem("lat_root"), 1)
            for gate, job in ((gate_aT, "z_ga3"), (gate_bT, "z_gb3_2")):
                act.wait_ge(sem("job_emptied"), JOB[job] + 1)
                nc.scalar.activation(gate, gate, ACT.Sigmoid).then_inc(sem("gates_ready"), 1)
            warm(ACT.Exp)
            act.wait_ge(sem("bias_stored"), 16)
            attention("mla")
            attention("ca")
            warm(ACT.Sqrt)
            norm_squares("ffn2", xT, squares, "job_emptied", JOB["out2_0"] + 1, 1)
            norm_root("ffn2", "sum_ffn2", rstd[:, 0:T])
            norm_shift("ffn2", hT, ada, 48)
            warm(ACT.Silu)
            feed_forward("ffn2")
            warm(ACT.Sqrt)
            norm_squares("last", xT, squares, "ffn2_sum_read", 1, 1)
            norm_root("last", "sum_last", rstd[:, 0:T])

        @block.tensor
        def _(pe):
            ident = K("ident")
            done_jobs = [0]

            def ring_arrived(part, name):
                slot, loads = PLACE[(part, name)]
                pe.wait_ge(sem(f"ring_full{slot}"), 16 * loads)

            def open_job(name):
                j = JOB[name]
                assert j == done_jobs[0], (name, JOBS[done_jobs[0]])
                if j >= 4:
                    pe.wait_ge(sem("job_emptied"), j - 3)
                return bank[j % 4]

            def close_job(last):
                last.then_inc(sem("job_ready"), 1)
                done_jobs[0] += 1

            def product(dst, lhs, rhs, by_chunk=None):
                n = len(lhs)
                for i in range(n):
                    if by_chunk is not None:
                        pe.wait_ge(sem(by_chunk), i + 1)
                    last = pe.matmul(dst, lhsT=lhs[i], rhs=rhs[i], start=(i == 0), stop=(i == n - 1))
                return last

            def turn_job(name, pieces):
                b = open_job(name)
                for i, piece in enumerate(pieces):
                    last = pe.transpose(b[:, i * P:(i + 1) * P], piece, ident)
                close_job(last)

            def sum_job(name, key, src):
                b = open_job(name)
                for k in range(KD):
                    if k % 2 == 0:
                        pe.wait_ge(sem(f"{key}_squares"), k // 2 + 1)
                    last = pe.matmul(b[:, 0:T], lhsT=K("mean"), rhs=src[:, k, :], start=(k == 0), stop=(k == KD - 1))
                close_job(last)

            def row_job(part, name, item, condition):
                b = open_job(name)
                ring_arrived(part, item)
                w = ring_w(part, item)
                for k in range(KD):
                    last = pe.matmul(b[32 * (k % 4):32 * (k % 4) + 32, :], lhsT=condition[:, k, :], rhs=w[:, k, :],
                                     start=(k < 4), stop=(k >= 4))
                close_job(last)

            def turn_row_job(name, u, row_name):
                b = open_job(name)
                pe.wait_ge(sem("job_emptied"), JOB[row_name] + 1)
                for m in range(4):
                    last = pe.matmul(b[:, 2 * m:2 * m + 2], lhsT=mod_acc[:, u, m * P:(m + 1) * P], rhs=K("select"),
                                     start=True, stop=True)
                close_job(last)

            def col_job(name, item):
                b = open_job(name)
                pe.wait_ge(sem("mod_acc_step"), 8 * (item + 1))
                for m in range(4):
                    last = pe.matmul(b[:, m:m + 1], lhsT=mod_acc[:, item % 2, m * P:(m + 1) * P],
                                     rhs=K("ones")[:, 0:1], start=True, stop=True)
                close_job(last)

            def linear_job(name, w, cols, src, by_chunk=None):
                b = open_job(name)
                for i, (lo, n) in enumerate(cols):
                    last = product(b[0:n, i * T:(i + 1) * T], [w[:, k, lo:lo + n] for k in range(w.shape[1])],
                                   [src[:, k, :] for k in range(w.shape[1])], by_chunk if i == 0 else None)
                close_job(last)

            pe.wait_ge(sem("consts_loaded"), 16)
            for name, rows in (("rows_a", rows_a), ("rows_b", rows_b)):
                b = open_job(name)
                pe.wait_ge(sem(f"{name}_loaded"), 16)
                n = rows.shape[0]
                close_job(pe.transpose(b[:, 0:n], rows[:, :], ident[0:n, 0:n]))
            for what, rows in (("x", x_rows), ("ctx", ctx_rows)):
                pe.wait_ge(sem(f"{what}_loaded"), 16)
                for i in range(4):
                    turn_job(f"{what}_turn{i}", [rows[:, b, (2 * i + c) * P:(2 * i + c + 1) * P]
                                                 for c in range(2) for b in range(2)])
            sum_job("sum_x", "n1", squares)
            sum_job("sum_ctx", "c1", ctx_squares)
            pe.wait_ge(sem("cond_ready"), 2)
            for i in range(4):
                row_job("pre", f"modrow{i}", f"mod{i}", cond)
                if i >= 1:
                    turn_row_job(f"mod{i - 1}", (i - 1) % 2, f"modrow{i - 1}")
            turn_row_job("mod3", 1, "modrow3")
            ring_arrived("pre", "w_kv")
            w = ring_w("pre", "w_kv")
            b = open_job("z_k")
            product(b[:, 0:T], [w[:, k, 0:P] for k in range(KD)], [mixT[:, k, :] for k in range(KD)], "c1_ready")
            close_job(product(b[:, T:2 * T], [w[:, k, 0:P] for k in range(KD)], [hT[:, k, :] for k in range(KD)], "n1_ready"))
            b = open_job("z_v")
            for kb in range(4):
                src = mixT if kb < 2 else hT
                last = product(b[:, kb * P:(kb + 1) * P], [src[:, k, (kb % 2) * P:(kb % 2) * P + P] for k in range(KD)],
                               [w[:, k, P:2 * P] for k in range(KD)])
            close_job(last)
            col_job("col_gt1a", 0)
            ring_arrived("pre", "w_q")
            w = ring_w("pre", "w_q")
            for i in range(2):
                b = open_job(f"z_q{i}")
                for c in range(2):
                    for k in range(KD):
                        for a in range(2):
                            head = 2 * i + c + 4 * a
                            last = pe.matmul(b[64 * a:64 * a + 64, c * T:(c + 1) * T], lhsT=w[:, k, 64 * head:64 * head + 64],
                                             rhs=hT[:, k, :], start=(k == 0), stop=(k == KD - 1))
                close_job(last)
            col_job("col_gt1b", 1)
            for item, (name, col) in enumerate((("gb", "col_sh2a"), ("gc", "col_sh2b"), ("u", "col_sc2a"))):
                ring_arrived("pre", f"w_{name}")
                for i in range(2):
                    linear_job(f"z_{name}{i}", ring_w("pre", f"w_{name}"), [(256 * i, P), (256 * i + P, P)], hT)
                col_job(col, 2 + item)
            pe.wait_ge(sem("qk_squares"), 1)
            for i in range(3):
                b = open_job(f"qk_sum{i}")
                close_job(pe.matmul(b[:, :], lhsT=K("heads64"), rhs=squares[:, 2 * i:2 * i + 2, :], start=True, stop=True))
            row_job("pre", "row_sc2b", "sc2b", cond)
            row_job("pre", "row_gt2a", "gt2a", cond)
            turn_row_job("col_sc2b", 0, "row_sc2b")
            turn_row_job("col_gt2a", 1, "row_gt2a")
            pe.wait_ge(sem("qk_ready"), 1)
            for i, chunks in enumerate(((0, 2), (2, 4), (5, 6))):
                b = open_job(f"qk_rot{i}")
                w = (chunks[1] - chunks[0]) * T
                close_job(pe.matmul(b[:, 0:w], lhsT=K("rot_axial"), rhs=qk[:, chunks[0]:chunks[1], :], start=True, stop=True))

            def attention(key):
                _, instances, _ = ATTENTIONS[key]
                n = len(instances)
                job = None
                for i in range(n + 3):
                    if i < n:
                        it = instances[i]
                        if i >= 2:
                            pe.wait_ge(sem(f"{key}_exp"), i - 1)
                        product(bank[4 + i % 2][:, 0:it["keys"]], it["q"], it["k"]).then_inc(sem(f"{key}_scores"), 1)
                    if 2 <= i <= n + 1:
                        j = i - 2
                        pe.wait_ge(sem(f"{key}_probs"), j + 1)
                        if j >= 2:
                            pe.wait_ge(sem(f"{key}_probsT"), j - 1)
                        for b in range(instances[j]["keys"] // P):
                            last = pe.transpose(bank[6 + j % 2][:, b * P:(b + 1) * P], probs[:, j % 2, b * P:(b + 1) * P], ident)
                        last.then_inc(sem(f"{key}_turned"), 1)
                    if i >= 3:
                        j = i - 3
                        it = instances[j]
                        if it["job"] != job:
                            job = it["job"]
                            open_job(job)
                        pe.wait_ge(sem(f"{key}_probsT"), j + 1)
                        nk = it["keys"] // P
                        last = product(job_bank(job)[it["col"]:it["col"] + 64, it["qb"] * P:(it["qb"] + 1) * P], it["v"],
                                       [probsT[:, j % 2, b * P:(b + 1) * P] for b in range(nk)])
                        if it["last"]:
                            close_job(last)

            pe.wait_ge(sem("rope1_ready"), 1)
            attention("at1")
            pe.wait_ge(sem("mg_squares"), 1)
            for i in range(4):
                b = open_job(f"head_sum{i}")
                close_job(pe.matmul(b[:, :], lhsT=K("heads64"), rhs=squares[:, 2 * i:2 * i + 2, :], start=True, stop=True))
            row_job("pre", "row_gt2b", "gt2b", cond)
            turn_row_job("col_gt2b", 0, "row_gt2b")
            for i in range(4):
                if i % 2 == 0:
                    ring_arrived("pre", f"w_out{i // 2}")
                linear_job(f"merge{i}", ring_w("pre", f"w_out{i // 2}"), [(256 * (i % 2), P), (256 * (i % 2) + P, P)], mixT,
                           "mg_ready" if i == 0 else None)
            sum_job("sum_n2", "n2", squares)
            pe.wait_ge(sem("router_loaded"), 32)
            b = open_job("logits")
            for tb in range(2):
                last = product(b[:, 64 * tb:64 * tb + 36], [hT[:, k, tb * P:(tb + 1) * P] for k in range(KD)],
                               [router[:, k, :] for k in range(KD)], "n2_ready" if tb == 0 else None)
            close_job(last)
            for i in range(4):
                turn_job(f"h2_turn{i}", [hT[:, 4 * (i % 2) + c, (i // 2) * P:(i // 2 + 1) * P] for c in range(4)])
            b = open_job("positions")
            pe.wait_ge(sem("assigned"), 1)
            a0, a1 = assigned[:, 0, :], assigned[:, 1, :]
            product(b[:, 0:32], [K("before")], [a0])
            product(b[:, 32:64], [K("ones"), K("before")], [a0, a1])
            close_job(product(b[:, 64:96], [K("ones"), K("ones")], [a0, a1]))
            b = open_job("bias_turn")
            pe.wait_ge(sem("rel_bias_loaded"), 64)
            for i in range(4):
                last = pe.matmul(b[0:8, i * P:(i + 1) * P], lhsT=rel_bias_rows[:, i, :], rhs=K("reverse"),
                                 start=True, stop=True)
            close_job(last)

            pe.wait_ge(sem("job_emptied"), done_jobs[0])
            pe.wait_ge(sem("zeros_ready"), 1)
            for i in range(4):
                pe.matmul(bank[i][:, :], lhsT=zeros[:, 0:P], rhs=zeros[:, :], start=True, stop=False, skip_group_check=True)

            def prepare(count, selected):
                pe.wait_ge(sem("selected"), count)
                if selected is not None:
                    pe.wait_ge(sem("pick_wT_ready"), selected)
                for k in range(KD):
                    for tb in range(2):
                        pe.matmul(bank[6][:, k * SLOTS:(k + 1) * SLOTS], lhsT=h_rows[:, tb, k * P:(k + 1) * P],
                                  rhs=pick[:, tb, :], start=(tb == 0), stop=(tb == 1))
                for tb in range(2):
                    last = pe.transpose(bank[7][:, tb * P:(tb + 1) * P], pick_w[:, tb, :], ident)
                last.then_inc(sem("gathered"), 1)

            def expert(u, n, prep, arrivals):
                gate, up, down = expert_w(u)
                pe.wait_ge(sem("xe_ready"), prep - 1)
                pe.wait_ge(sem(f"gate_full{u}"), arrivals)
                for w, b in ((gate, bank[4]), (up, bank[5])):
                    if b is bank[5]:
                        pe.wait_ge(sem(f"up_full{u}"), arrivals)
                    for k in range(KD):
                        for half in range(2):
                            last = pe.matmul(b[64 * half:64 * half + 64, 0:HALF_E], lhsT=xeT[:, k, :],
                                             rhs=w[:, k, half * HALF_E:(half + 1) * HALF_E],
                                             start=(k == 0), stop=(k == KD - 1))
                last.then_inc(sem("gate_up_done"), 1)
                prepare(prep, prep - 1)
                pe.wait_ge(sem("hidden_ready"), n)
                for c in range(3):
                    last = pe.transpose(bank[5][:, c * P:(c + 1) * P], hidden[:, c * P:(c + 1) * P], ident)
                last.then_inc(sem("hidden_turned"), 1)
                pe.wait_ge(sem("hiddenT_ready"), n)
                pe.wait_ge(sem("xe_ready"), prep)
                pe.wait_ge(sem(f"down_full{u}"), arrivals)
                for f in range(6):
                    for half in range(2):
                        last = pe.matmul(bank[6][64 * half:64 * half + 64, :],
                                         lhsT=hiddenT[:, f % 3, 64 * (f // 3):64 * (f // 3) + 64],
                                         rhs=down[:, f, half * 512:(half + 1) * 512], start=(f == 0), stop=(f == 5))
                last.then_inc(sem("down_done"), 1)
                pe.wait_ge(sem("y_ready"), n)
                pe.wait_ge(sem("pick_wT_ready"), prep - 1)
                for c in range(4):
                    for half in range(2):
                        m = 4 * half + c
                        pe.matmul(bank[m // 2][:, (m % 2) * T:(m % 2 + 1) * T],
                                  lhsT=y_e[64 * half:64 * half + 64, c * P:(c + 1) * P],
                                  rhs=pick_wT[64 * half:64 * half + 64, u, :],
                                  start=False, stop=False, skip_group_check=True)

            prepare(1, None)
            with pe.Fori(0, N_EXPERTS // 2) as it:
                for u in range(2):
                    expert(u, it * 2 + u + 1, it * 2 + u + 2, it * 16 + 16)
            pe.wait_ge(sem("busiest_ready"), 1)
            most = pe.value_load(busiest[0:1, 0:1], min_val=0, max_val=T)
            with pe.If(most > SLOTS):
                with pe.Fori(1, PASSES) as ps:
                    prepare(ps * (N_EXPERTS + 1) + 1, ps * (N_EXPERTS + 1))
                    with pe.Fori(0, N_EXPERTS // 2) as it:
                        for u in range(2):
                            expert(u, ps * N_EXPERTS + it * 2 + u + 1, ps * (N_EXPERTS + 1) + it * 2 + u + 2,
                                   ps * (8 * N_EXPERTS) + it * 16 + 16)
            for i in range(4):
                last = pe.matmul(bank[i][:, :], lhsT=zeros[:, 0:P], rhs=zeros[:, :], start=False, stop=True, skip_group_check=True)
            last.then_inc(sem("experts_done"), 1)

            pe.wait_ge(sem("y_moe_read"), 4)
            pe.wait_ge(sem("cond_ready"), 4)
            row_job("ada", "row_ada0", "ada0", cond_ada)
            sum_job("sum_final", "fin1", squares)
            for i in range(1, 4):
                row_job("ada", f"row_ada{i}", f"ada{i}", cond_ada)
                turn_row_job(f"col_ada{i - 1}", (i - 1) % 2, f"row_ada{i - 1}")
            turn_row_job("col_ada3", 1, "row_ada3")

            def feed_forward(key, ada_items):
                pe.wait_ge(sem("job_emptied"), done_jobs[0])

                def gate_up(s, slot, half, parity, arrivals, act_read, first=False):
                    w = ring(slot).rearrange("p (k g n) -> p k g n", k=KD, g=2)
                    if half == 0:
                        pe.wait_ge(sem(f"{key}_in_full{slot}"), arrivals)
                    if act_read is not None:
                        pe.wait_ge(sem(f"{key}_act"), act_read)
                    for g in range(2):
                        last = product(bank[4 + parity][:, g * T:(g + 1) * T],
                                       [w[:, k, g, half * P:(half + 1) * P] for k in range(KD)],
                                       [hT[:, k, :] for k in range(KD)], f"{key}_ready" if first and g == 0 else None)
                    last.then_inc(sem(f"{key}_gate_up_done"), 1)

                def down(s, slot, half, parity, arrivals, first=False):
                    w = ring(slot)[:, 0:2 * D].rearrange("p (k n) -> p k n", k=2)
                    if half == 0:
                        pe.wait_ge(sem(f"{key}_out_full{slot}"), arrivals)
                    pe.wait_ge(sem(f"{key}_act"), s)
                    for m in range(KD):
                        last = pe.matmul(bank[m // 2][:, (m % 2) * T:(m % 2 + 1) * T], lhsT=w[:, half, m * P:(m + 1) * P],
                                         rhs=ff_act[:, parity, :], start=(first and m % 2 == 0), stop=False,
                                         skip_group_check=True)
                    last.then_inc(sem(f"{key}_down_done"), 1)
                    return last

                gate_up(1, 2, 0, 0, 32, None, first=True)
                gate_up(2, 2, 1, 1, 32, None)
                down(1, 3, 0, 0, 16, first=True)
                with pe.Fori(0, FF_LOOPS) as it:
                    for j in range(4):
                        s = it * 4 + j + 3
                        slot = 2 * (j // 2)
                        if j == 0:
                            gate_up(s, 0, 0, 0, it * 32 + 32, s - 2)
                            down(s - 1, 3, 1, 1, None)
                        elif j == 1:
                            gate_up(s, 0, 1, 1, None, s - 2)
                            down(s - 1, 1, 0, 0, it * 16 + 16)
                        elif j == 2:
                            gate_up(s, 2, 0, 0, it * 32 + 64, s - 2)
                            down(s - 1, 1, 1, 1, None)
                        else:
                            gate_up(s, 2, 1, 1, None, s - 2)
                            down(s - 1, 3, 0, 0, it * 16 + 32)
                        if ada_items and j % 2 == 1:
                            u = j // 2
                            pe.wait_ge(sem("mod_acc_step"), it * 16 + 8 * (5 + u + 1))
                            for m in range(4):
                                last = pe.matmul(bank[6 + u][:, m:m + 1], lhsT=mod_acc[:, u, m * P:(m + 1) * P],
                                                 rhs=K("ones")[:, 0:1], start=True, stop=True)
                            last.then_inc(sem("ada_col_ready"), 1)
                down(4 * FF_LOOPS + 2, 3, 1, 1, None)
                for i in range(4):
                    last = pe.matmul(bank[i][:, :], lhsT=zeros[:, 0:P], rhs=zeros[:, :], start=False, stop=True,
                                     skip_group_check=True)
                last.then_inc(sem(f"{key}_sum_done"), 1)
                pe.wait_ge(sem(f"{key}_sum_read"), 4)

            sum_job("sum_ffn1", "ffn1", squares)
            feed_forward("ffn1", True)
            sum_job("sum_mix", "mix", squares)
            ring_arrived("mid", "w2_lat")
            w = ring_w("mid", "w2_lat")
            linear_job("z_lat", w, [(0, P), (P, P)], hT, "mix_ready")
            linear_job("z_kv", w, [(256, P), (320, 96)], hT)
            for name, col, item in (("caq", "col_ada14", 15), ("cak", "col_ada15", 16)):
                ring_arrived("mid", f"w2_{name}")
                for i in range(2):
                    linear_job(f"z_{name}{i}", ring_w("mid", f"w2_{name}"), [(256 * i, P), (256 * i + P, P)], hT)
                col_job(col, item)
            ring_arrived("mid", "w2_cav")
            w = ring_w("mid", "w2_cav")
            for tb in range(2):
                b = open_job(f"z_cav{tb}")
                close_job(product(b[:, :], [hT[:, k, tb * P:(tb + 1) * P] for k in range(KD)], [w[:, k, :] for k in range(KD)]))
            b = open_job("lat_sum")
            pe.wait_ge(sem("lat_squares"), 1)
            product(b[:, 0:T], [K("ones")] * 2, [squares[:, 0, :], squares[:, 1, :]])
            close_job(product(b[:, T:2 * T], [K("ones")], [squares[:, 2, :]]))
            col_job("col_ada16", 17)
            for gate in ("ga", "gb"):
                for i in range(4):
                    name = f"w2_{gate}{i // 2}"
                    if i % 2 == 0:
                        ring_arrived("mid", name)
                    linear_job(f"z_{gate}{i}" + ("_2" if gate == "gb" else ""), ring_w("mid", name),
                               [(256 * (i % 2), P), (256 * (i % 2) + P, P)], hT)
                if gate == "ga":
                    col_job("col_ada17", 18)
            pe.wait_ge(sem("w_uq_full"), 16)
            pe.wait_ge(sem("w_ukv_full"), 16)
            pe.wait_ge(sem("lat_ready"), 1)
            both = ring(PLACE[("mid", "mla_up")][0])
            uq = both[:, 0:1536].rearrange("p (k n) -> p k n", k=2)
            ukv = both[:, 1536:2560].rearrange("p (k h n) -> p k h n", k=1, h=8)
            for i in range(4):
                linear_job(f"mla_q{i}", uq, [(192 * i, 96), (192 * i + 96, 96)], latT)
            for i in range(4):
                linear_job(f"mla_k{i}", both[:, 1536:2560].rearrange("p (k n) -> p k n", k=1),
                           [(256 * i, 64), (256 * i + P, 64)], latT[:, 2:3, :])
            for tb in range(2):
                b = open_job(f"mla_v{tb}")
                close_job(product(b[:, :], [latT[:, 2, tb * P:(tb + 1) * P]], [ukv[:, 0, :, 64:128]]))
            pe.wait_ge(sem("mla_qk_ready"), 1)
            for i in range(4):
                b = open_job(f"pe_rot{i}")
                close_job(pe.matmul(b[0:96, :], lhsT=K("rot_half")[0:96, 0:96], rhs=mla_q[0:96, 2 * i:2 * i + 2, :],
                                    start=True, stop=True))
            b = open_job("kpe_rot")
            close_job(pe.matmul(b[0:96, 0:T], lhsT=K("rot_half")[0:96, 0:96], rhs=squares[0:96, 3, :], start=True, stop=True))
            pe.wait_ge(sem("mla_ready"), 1)
            attention("mla")
            pe.wait_ge(sem("bias_loaded"), 32)
            attention("ca")
            ring_arrived("mid", "w_branch_a")
            ring_arrived("mid", "w_branch_b")
            pe.wait_ge(sem("job_emptied"), done_jobs[0])
            for i in range(4):
                for ab, at in (("a", 0), ("b", 4)):
                    w = ring(PLACE[("mid", f"w_branch_{ab}")][0]).rearrange("p (k n) -> p k n", k=4)
                    linear_job(f"branch_{ab}{i}", w, [(256 * i, P), (256 * i + P, P)], squares[:, at:at + 4, :])
            pe.wait_ge(sem("merged_ready"), 4)
            for i in range(4):
                if i % 2 == 0:
                    ring_arrived("mid", f"w_out2_{i // 2}")
                linear_job(f"out2_{i}", ring_w("mid", f"w_out2_{i // 2}"), [(256 * (i % 2), P), (256 * (i % 2) + P, P)], hT)
            sum_job("sum_ffn2", "ffn2", squares)
            feed_forward("ffn2", False)
            sum_job("sum_last", "last", squares)
            for i in range(4):
                pe.wait_ge(sem("last_ready"), 4 * min(i, 1) + 4)
                turn_job(f"y_turn{i}", [xT[:, 4 * (i % 2) + c, (i // 2) * P:(i // 2 + 1) * P] for c in range(4)])
            assert done_jobs[0] == len(JOBS)

        @block.vector
        def _(dve):
            n_step, emptied, n_item = [0], [0], [0]

            def step(instruction):
                n_step[0] += 1
                instruction.then_inc(sem("dve_step"), 1)
                dve.wait_ge(sem("dve_step"), n_step[0])

            def ring_arrived(part, name):
                slot, loads = PLACE[(part, name)]
                dve.wait_ge(sem(f"ring_full{slot}"), 16 * loads)

            def take_job(name):
                assert JOB[name] == emptied[0], (name, JOBS[emptied[0]])
                dve.wait_ge(sem("job_ready"), JOB[name] + 1)
                return job_bank(name)

            def empty_job(instruction):
                instruction.then_inc(sem("job_emptied"), 1)
                emptied[0] += 1

            def job_done_here():
                dve.wait_ge(sem("job_emptied"), emptied[0])

            def mod_item(w, scalars, u, first):
                for k in range(KD):
                    if k == 0:
                        i = nc.vector.tensor_scalar(mod_acc[:, u, :], w[:, k, :], scalars[k], None, ALU.mult)
                    else:
                        dve.wait_ge(sem("mod_acc_step"), first + k)
                        i = nc.vector.scalar_tensor_tensor(out=mod_acc[:, u, :], in0=w[:, k, :], scalar=scalars[k],
                                                           in1=mod_acc[:, u, :], op0=ALU.mult, op1=ALU.add)
                    i.then_inc(sem("mod_acc_step"), 1)

            cond_1 = [cond[:, k, 0:1] for k in range(KD)]
            cond_2 = [cond2[:, k:k + 1] for k in range(KD)]

            def item(part, name):
                n = n_item[0]
                n_item[0] += 1
                ring_arrived(part, name)
                mod_item(ring_w(part, name), cond_1 if part == "pre" else cond_2, n % 2, 8 * n)

            def col_job(name, dst, bias):
                b = take_job(name)
                empty_job(nc.vector.tensor_tensor(dst, b[:, 0:4], bias, ALU.add))

            def mod_col(name, n):
                col_job(name, mod[:, 16 + 4 * n:20 + 4 * n], cols_a[:, 16 + 4 * n:20 + 4 * n])

            def ada_col(name, n):
                col_job(name, ada[:, 4 * n:4 * n + 4], cols_b[:, 4 * n:4 * n + 4])

            def make_gain(key, g, scale):
                s = SET[key]
                step(nc.vector.scalar_tensor_tensor(out=gains[:, s * KD:(s + 1) * KD], in0=scale, scalar=1.0, in1=g,
                                                    op0=ALU.add, op1=ALU.mult))

            def norm_root(key, job, stat):
                take_job(job)
                dve.wait_ge(sem(f"{key}_root"), 1)
                empty_job(nc.vector.reciprocal(stat, stat))
                job_done_here()

            def norm_scale(key, src, dst, stat):
                for k in range(KD):
                    nc.vector.scalar_tensor_tensor(out=dst[:, k, :], in0=src[:, k, :], scalar=gain(key, k), in1=stat,
                                                   op0=ALU.mult, op1=ALU.mult).then_inc(sem(f"{key}_scaled"), 1)

            def norm_gain(key, name, col, stat):
                for k in range(KD):
                    nc.vector.scalar_tensor_tensor(out=xT[:, k, :], in0=xT[:, k, :], scalar=col(name, k), in1=stat,
                                                   op0=ALU.mult, op1=ALU.mult).then_inc(sem(f"{key}_ready"), 1)

            def copy_rows(job, u):
                take_job(job)
                empty_job(nc.vector.tensor_copy(mod_acc[:, u, :], job_bank(job)[:, :]))

            def row_col(name, dst, bias):
                b = take_job(name)[:, 0:8].rearrange("p (m c) -> p m c", c=2)
                empty_job(nc.vector.tensor_tensor(dst, b[:, :, 0], bias, ALU.add))

            nc.vector.memset(zeros[:, :], 0.0).then_inc(sem("zeros_ready"), 1)
            nc.vector.memset(cond[:, :, :], 0.0)
            nc.vector.memset(cond_ada[:, :, :], 0.0).then_inc(sem("cond_zeroed"), 1)
            for c in (0, T + 1):
                nc.vector.memset(conv_in[:, :, c:c + 1], 0.0)
            nc.vector.memset(weights[:, :, 32:33], 0.0)
            step(nc.vector.memset(places[:, :, 32:33], -1.0))
            dve.wait_ge(sem("positions_loaded"), 16)
            dve.wait_ge(sem("consts_loaded"), 16)
            pos, near, arg, arg_cos, wrap = (angle[64:96, i, :] for i in range(5))
            step(nc.vector.tensor_copy(pos, turns[64:96, :]))
            step(nc.vector.tensor_scalar(pos, pos, K("inv_freq")[64:96, :], None, ALU.mult))
            step(nc.vector.tensor_scalar(turns[64:96, :], pos, 1.0 / TWO_PI, None, ALU.mult))
            step(nc.vector.tensor_copy(near, turns[64:96, :]))
            for i, part in enumerate((PI_A, PI_B, PI_C)):
                step(nc.vector.scalar_tensor_tensor(out=arg, in0=near, scalar=-part, in1=pos if i == 0 else arg,
                                                    op0=ALU.mult, op1=ALU.add))
            step(nc.vector.tensor_scalar(arg_cos, arg, TWO_PI / 4, None, ALU.add))
            for a in (arg, arg_cos):
                for op, turn in ((ALU.is_gt, -TWO_PI), (ALU.is_lt, TWO_PI)):
                    limit = TWO_PI / 2 if turn < 0 else -TWO_PI / 2
                    step(nc.vector.tensor_scalar(wrap, a, limit, turn, op, ALU.mult))
                    step(nc.vector.tensor_tensor(a, a, wrap, ALU.add))
                i = nc.vector.tensor_scalar(a, a, 3.1415925, -3.1415925, ALU.min, ALU.max)
            i.then_inc(sem("angles_ready"), 1)

            for name, cols in (("rows_a", cols_a), ("rows_b", cols_b)):
                b = take_job(name)
                empty_job(nc.vector.tensor_copy(cols[:, :], b[:, 0:cols.shape[1]]))
            for what, dst in (("x", xT[:, :, :]), ("ctx", ctxT)):
                for i in range(4):
                    take_job(f"{what}_turn{i}")
                    empty_job(nc.vector.tensor_copy(dst[:, 2 * i:2 * i + 2, :], job_wide(f"{what}_turn{i}")))
            norm_root("n1", "sum_x", rstd[:, 0:T])
            norm_root("c1", "sum_ctx", rstd[:, T:2 * T])
            copy_rows("modrow0", 0)
            for i in range(4):
                if i < 3:
                    copy_rows(f"modrow{i + 1}", (i + 1) % 2)
                b = take_job(f"mod{i}")[:, 0:8].rearrange("p (m c) -> p m c", c=2)
                bias = cols_a[:, 4 * i:4 * i + 4]
                nc.vector.tensor_tensor(mod[:, 4 * i:4 * i + 4], b[:, :, 0], bias, ALU.add)
                empty_job(nc.vector.tensor_tensor(mod_ctx[:, 4 * i:4 * i + 4], b[:, :, 1], bias, ALU.add))
            job_done_here()
            g1 = cols_a[:, 48:56]
            make_gain("n1", g1, mod[:, 8:16])
            make_gain("c1", g1, mod_ctx[:, 8:16])
            norm_scale("c1", ctxT, mixT, rstd[:, T:2 * T])
            norm_scale("n1", xT, hT, rstd[:, 0:T])

            item("pre", "gt1a")
            take_job("z_k")
            empty_job(nc.vector.tensor_copy(qk[:, 4:6, :], job_wide("z_k")))
            take_job("z_v")
            empty_job(nc.vector.tensor_copy(v1, job_bank("z_v")[:, :].rearrange("p (b n) -> p b n", b=4)))
            mod_col("col_gt1a", 0)
            item("pre", "gt1b")
            for i in range(2):
                take_job(f"z_q{i}")
                empty_job(nc.vector.tensor_copy(qk[:, 2 * i:2 * i + 2, :], job_wide(f"z_q{i}")))
            mod_col("col_gt1b", 1)
            item("pre", "sh2a")
            for i in range(2):
                take_job(f"z_gb{i}")
                empty_job(nc.vector.tensor_copy(gate_b[:, 2 * i:2 * i + 2, :], job_wide(f"z_gb{i}")))
            mod_col("col_sh2a", 2)
            item("pre", "sh2b")
            for i in range(2):
                take_job(f"z_gc{i}")
                empty_job(nc.vector.tensor_copy(conv_out[:, 2 * i:2 * i + 2, :], job_wide(f"z_gc{i}")))
            mod_col("col_sh2b", 3)
            item("pre", "sc2a")
            for i in range(2):
                take_job(f"z_u{i}")
                empty_job(nc.vector.tensor_tensor(conv_in[:, 2 * i:2 * i + 2, 1:T + 1], job_wide(f"z_u{i}"),
                                                  conv_out[:, 2 * i:2 * i + 2, :], ALU.mult))
            col_job("col_sc2a", mod[:, 32:36], cols_a[:, 32:36])
            for i in range(3):
                take_job(f"qk_sum{i}")
                dve.wait_ge(sem("qk_root"), i + 1)
                tmp = qk_tmp[:, 2 * i:2 * i + 2, :]
                empty_job(nc.vector.reciprocal(tmp, tmp))
            copy_rows("row_sc2b", 0)
            copy_rows("row_gt2a", 1)
            job_done_here()
            for lo, hi, name in ((0, 4, "q_norm_g"), (4, 6, "k_norm_g")):
                i = nc.vector.scalar_tensor_tensor(out=qk[:, lo:hi, :], in0=qk[:, lo:hi, :], scalar=col_a(name),
                                                   in1=qk_tmp[:, lo:hi, :], op0=ALU.mult, op1=ALU.mult)
            i.then_inc(sem("qk_ready"), 1)
            dve.wait_ge(sem("qk_ready"), 1)
            row_col("col_sc2b", mod[:, 36:40], cols_a[:, 36:40])
            row_col("col_gt2a", mod[:, 40:44], cols_a[:, 40:44])

            def tables(cos, sin, n):
                return [t.rearrange("p (a t) -> p a t", a=1).broadcast_to((t.shape[0], n, T)) for t in (cos, sin)]

            for i, (lo, hi) in enumerate(((0, 2), (2, 4), (5, 6))):
                b = take_job(f"qk_rot{i}")[:, 0:(hi - lo) * T].rearrange("p (a t) -> p a t", t=T)
                cos, sin = tables(K("axial_cos"), K("axial_sin"), hi - lo)
                empty_job(nc.vector.tensor_tensor(qk_tmp[:, lo:hi, :], b, sin, ALU.mult))
                step(nc.vector.tensor_tensor(qk[:, lo:hi, :], qk[:, lo:hi, :], cos, ALU.mult))
                i = nc.vector.tensor_tensor(qk[:, lo:hi, :], qk[:, lo:hi, :], qk_tmp[:, lo:hi, :], ALU.add)
            i.then_inc(sem("rope1_ready"), 1)

            def attention(key):
                index, instances, scale = ATTENTIONS[key]
                n = len(instances)
                for i in range(n + 4):
                    if i < n:
                        w = instances[i]["keys"]
                        scores = bank[4 + i % 2]
                        dve.wait_ge(sem(f"{key}_scores"), i + 1)
                        if instances[i]["mask"]:
                            late = scores[0:64, w - 64:w]
                            step(nc.vector.tensor_scalar(late, late, NEG, None, ALU.add))
                        step(nc.vector.reduce_max(stats[:, index, 2, i:i + 1], scores[:, 0:w], AX_X))
                        nc.vector.tensor_scalar(stats[:, index, 0, i:i + 1], stats[:, index, 2, i:i + 1], -scale, None,
                                                ALU.mult).then_inc(sem(f"{key}_negmax"), 1)
                    if 1 <= i <= n:
                        j = i - 1
                        w = instances[j]["keys"]
                        dve.wait_ge(sem(f"{key}_exp"), j + 1)
                        step(nc.vector.reciprocal(stats[:, index, 2, j:j + 1], stats[:, index, 1, j:j + 1]))
                        nc.vector.tensor_scalar(probs[:, j % 2, 0:w], probs[:, j % 2, 0:w], stats[:, index, 2, j:j + 1],
                                                None, ALU.mult).then_inc(sem(f"{key}_probs"), 1)
                    if i >= 4 and instances[i - 4]["last"]:
                        job = instances[i - 4]["job"]
                        take_job(job)
                        empty_job(nc.vector.tensor_copy(ATT_OUT[key](int(job[-1])), job_bank(job)[:, 0:T]))

            attention("at1")
            mg = h_rows[:, :, :].rearrange("p b (k t) -> p (b k) t", t=T)
            for i in range(4):
                take_job(f"head_sum{i}")
                dve.wait_ge(sem("mg_root"), i + 1)
                empty_job(nc.vector.reciprocal(mg[:, 2 * i:2 * i + 2, :], mg[:, 2 * i:2 * i + 2, :]))
            copy_rows("row_gt2b", 0)
            job_done_here()
            for k in range(KD):
                nc.vector.scalar_tensor_tensor(out=mixT[:, k, :], in0=mixT[:, k, :],
                                               scalar=cols_a[:, ROWS_A["attn_out_g"] + k:ROWS_A["attn_out_g"] + k + 1],
                                               in1=mg[:, k, :], op0=ALU.mult, op1=ALU.mult).then_inc(sem("mg_ready"), 1)
            row_col("col_gt2b", mod[:, 44:48], cols_a[:, 44:48])
            job_done_here()

            def residual_job(name, i, gate, at):
                take_job(name)
                for c in range(2):
                    k = 2 * i + c
                    ins_ = nc.vector.scalar_tensor_tensor(out=xT[:, k, :], in0=job_wide(name)[:, c, :],
                                                          scalar=gate[:, at + k:at + k + 1], in1=xT[:, k, :],
                                                          op0=ALU.mult, op1=ALU.add)
                empty_job(ins_)

            for i in range(4):
                residual_job(f"merge{i}", i, mod, 16)
            make_gain("n2", cols_a[:, 56:64], mod[:, 32:40])
            norm_root("n2", "sum_n2", rstd[:, 0:T])
            norm_scale("n2", xT, hT, rstd[:, 0:T])

            b = take_job("logits")
            for tb in range(2):
                i = nc.vector.tensor_copy(logits[:, tb, :], b[:, 64 * tb:64 * tb + 36])
            empty_job(i)
            job_done_here()
            for tb in range(2):
                step(nc.vector.reduce_max(picked[:, tb, 28:29], logits[:, tb, 0:4], AX_X))
                nc.vector.tensor_scalar(picked[:, tb, 0:1], picked[:, tb, 28:29], -1.0, None, ALU.mult)\
                  .then_inc(sem("router_max"), 1)
                step(nc.vector.scalar_tensor_tensor(out=picked[:, tb, 24:28], in0=logits[:, tb, 0:4],
                                                    scalar=picked[:, tb, 28:29], in1=K("group_rank"),
                                                    op0=ALU.is_equal, op1=ALU.mult))
                step(nc.vector.reduce_max(picked[:, tb, 29:30], picked[:, tb, 24:28], AX_X))
                step(nc.vector.tensor_scalar(picked[:, tb, 24:28], picked[:, tb, 24:28], picked[:, tb, 29:30], None, ALU.is_equal))
                step(nc.vector.tensor_scalar(picked[:, tb, 30:31], picked[:, tb, 29:30], -float(GROUP_SIZE),
                                             float(GROUP_SIZE * N_GROUPS), ALU.mult, ALU.add))
                step(nc.vector.tensor_scalar(picked[:, tb, 8:16], logits[:, tb, 4:12], picked[:, tb, 24:25], None, ALU.mult))
                for g in range(1, N_GROUPS):
                    step(nc.vector.scalar_tensor_tensor(out=picked[:, tb, 8:16], in0=logits[:, tb, 4 + 8 * g:12 + 8 * g],
                                                        scalar=picked[:, tb, 24 + g:25 + g], in1=picked[:, tb, 8:16],
                                                        op0=ALU.mult, op1=ALU.add))
                step(nc.vector.max(out=picked[:, tb, 16:24], in_=picked[:, tb, 8:16]))
                step(nc.vector.max_index(out=picked_i[:, tb, :], in_max=picked[:, tb, 16:24], in_values=picked[:, tb, 8:16]))
                step(nc.vector.tensor_copy(picked[:, tb, 31:33], picked_i[:, tb, 0:2]))
                step(nc.vector.tensor_scalar(picked[:, tb, 31:33], picked[:, tb, 31:33], picked[:, tb, 30:31], None, ALU.add))
                nc.vector.tensor_scalar(picked[:, tb, 3:4], picked[:, tb, 16:17], -1.0, None, ALU.mult)\
                  .then_inc(sem("router_top"), 1)
                step(nc.vector.tensor_scalar(route_tmp[:, tb, :], K("expert_id"), picked[:, tb, 31:32], None, ALU.is_equal))
                nc.vector.scalar_tensor_tensor(out=assigned[:, tb, :], in0=K("expert_id"), scalar=picked[:, tb, 32:33],
                                               in1=route_tmp[:, tb, :], op0=ALU.is_equal, op1=ALU.add)
            nc.vector.tensor_copy(picked[:, 0, 36:37], picked[:, 0, 31:32]).then_inc(sem("assigned"), 1)
            for i in range(4):
                take_job(f"h2_turn{i}")
                empty_job(nc.vector.tensor_copy(h_rows[:, i // 2, 512 * (i % 2):512 * (i % 2) + 512], job_bank(f"h2_turn{i}")[:, :]))
            dve.wait_ge(sem("group_exp"), 2)
            dve.wait_ge(sem("second_exp"), 2)
            for tb in range(2):
                step(nc.vector.tensor_scalar(picked[:, tb, 33:34], picked[:, tb, 2:3], 1.0, None, ALU.add))
                step(nc.vector.tensor_tensor(picked[:, tb, 33:34], picked[:, tb, 33:34], picked[:, tb, 1:2], ALU.mult))
                step(nc.vector.reciprocal(picked[:, tb, 34:35], picked[:, tb, 33:34]))
                step(nc.vector.tensor_tensor(picked[:, tb, 35:36], picked[:, tb, 34:35], picked[:, tb, 2:3], ALU.mult))
                step(nc.vector.tensor_scalar(weights[:, tb, 0:32], K("expert_id"), picked[:, tb, 31:32], picked[:, tb, 34:35],
                                             ALU.is_equal, ALU.mult))
                step(nc.vector.tensor_scalar(route_tmp[:, tb, :], K("expert_id"), picked[:, tb, 32:33], picked[:, tb, 35:36],
                                             ALU.is_equal, ALU.mult))
                step(nc.vector.tensor_tensor(weights[:, tb, 0:32], weights[:, tb, 0:32], route_tmp[:, tb, :], ALU.add))
            b = take_job("positions")
            for tb in range(2):
                step(nc.vector.tensor_scalar(route_tmp[:, tb, :], assigned[:, tb, :], -NO_SLOT, NO_SLOT, ALU.mult, ALU.add))
                step(nc.vector.tensor_tensor(places[:, tb, 0:32], b[:, 32 * tb:32 * tb + 32], route_tmp[:, tb, :], ALU.add))
            empty_job(nc.vector.reduce_max(picked[0:1, 0, 37:38], b[0:1, 64:96], AX_X))
            job_done_here()
            nc.vector.tensor_copy(busiest[0:1, 0:1], picked[0:1, 0, 37:38]).then_inc(sem("busiest_ready"), 1)
            take_job("bias_turn")
            empty_job(nc.vector.tensor_copy(bias_rows, job_bank("bias_turn")[0:8, :]))
            job_done_here()

            def select(e, count, gathered):
                if gathered is not None:
                    dve.wait_ge(sem("gathered"), gathered)
                for tb in range(2):
                    place = places[:, tb, bass.ds(e, 1)]
                    nc.vector.tensor_scalar(pick[:, tb, :], K("slot")[:, 0:SLOTS], place, None, ALU.is_equal)
                    i = nc.vector.tensor_scalar(pick_w[:, tb, :], K("slot"), place, weights[:, tb, bass.ds(e, 1)],
                                                ALU.is_equal, ALU.mult)
                i.then_inc(sem("selected"), 1)

            def take_turned(u, count):
                dve.wait_ge(sem("gathered"), count)
                nc.vector.tensor_copy(pick_wT[:, u, :], bank[7][:, 0:T]).then_inc(sem("pick_wT_ready"), 1)

            def expert(u, e, n, prep):
                select(e + 1, prep, prep - 1)
                dve.wait_ge(sem("gate_act_ready"), n)
                nc.vector.tensor_tensor(hidden, gate_act, bank[5][:, 0:HALF_E], ALU.mult).then_inc(sem("hidden_ready"), 1)
                take_turned(1 - u, prep)

            select(0, 1, None)
            take_turned(0, 1)
            with dve.Fori(0, N_EXPERTS // 2) as it:
                for u in range(2):
                    expert(u, it * 2 + u, it * 2 + u + 1, it * 2 + u + 2)
            most = dve.value_load(busiest[0:1, 0:1], min_val=0, max_val=T)
            with dve.If(most > SLOTS):
                with dve.Fori(1, PASSES) as ps:
                    nc.vector.tensor_scalar(places, places, -float(SLOTS), None, ALU.add).then_inc(sem("places_moved"), 1)
                    dve.wait_ge(sem("places_moved"), ps)
                    select(0, None, ps * (N_EXPERTS + 1))
                    take_turned(0, ps * (N_EXPERTS + 1) + 1)
                    with dve.Fori(0, N_EXPERTS // 2) as it:
                        for u in range(2):
                            expert(u, it * 2 + u, ps * N_EXPERTS + it * 2 + u + 1, ps * (N_EXPERTS + 1) + it * 2 + u + 2)

            def residual_sum(done, read, gate, at):
                dve.wait_ge(sem(done), 1)
                for k in range(KD):
                    i = nc.vector.scalar_tensor_tensor(out=xT[:, k, :], in0=bank[k // 2][:, (k % 2) * T:(k % 2 + 1) * T],
                                                       scalar=gate[:, at + k:at + k + 1], in1=xT[:, k, :],
                                                       op0=ALU.mult, op1=ALU.add)
                    if k % 2 == 1:
                        i.then_inc(sem(read), 1)
                dve.wait_ge(sem(read), 4)

            residual_sum("experts_done", "y_moe_read", mod, 40)

            copy_rows("row_ada0", 0)
            norm_root("fin1", "sum_final", rstd[:, 0:T])
            norm_gain("fin1", "final_g", col_a, rstd[:, 0:T])
            for i in range(4):
                if i < 3:
                    copy_rows(f"row_ada{i + 1}", (i + 1) % 2)
                row_col(f"col_ada{i}", ada[:, 4 * i:4 * i + 4], cols_b[:, 4 * i:4 * i + 4])
            job_done_here()
            make_gain("ffn1", cols_b[:, 72:80], ada[:, 8:16])
            dve.wait_ge(sem("fin1_ready"), KD)
            norm_root("ffn1", "sum_ffn1", rstd[:, 0:T])
            norm_scale("ffn1", xT, hT, rstd[:, 0:T])

            def feed_forward(key, with_ada, gate_at):
                def one(s, parity, down):
                    dve.wait_ge(sem(f"{key}_silu"), s)
                    if down is not None:
                        dve.wait_ge(sem(f"{key}_down_done"), down)
                    nc.vector.tensor_tensor(ff_act[:, parity, :], silu_g[:, parity, :], bank[4 + parity][:, T:2 * T],
                                            ALU.mult).then_inc(sem(f"{key}_act"), 1)

                one(1, 0, None)
                one(2, 1, None)
                with dve.Fori(0, FF_LOOPS) as it:
                    for j in range(4):
                        one(it * 4 + j + 3, j % 2, it * 4 + j + 1)
                        if with_ada and j % 2 == 0:
                            u = j // 2
                            dve.wait_ge(sem(f"ada_full{4 + u}"), it * 16 + 16)
                            mod_item(ring(4 + u).rearrange("p (k n) -> p k n", k=KD), cond_2, u, it * 16 + 8 * (5 + u))
                        elif with_ada:
                            u = j // 2
                            dve.wait_ge(sem("ada_col_ready"), it * 2 + u + 1)
                            at = it * 8 + 16 + 4 * u
                            nc.vector.tensor_tensor(ada[:, bass.ds(at, 4)], bank[6 + u][:, 0:4], cols_b[:, bass.ds(at, 4)],
                                                    ALU.add).then_inc(sem("ada_col_read"), 1)
                if with_ada:
                    n_item[0] += 2 * FF_LOOPS
                    dve.wait_ge(sem("ada_col_read"), 2 * FF_LOOPS)
                step(nc.vector.tensor_scalar(half_gate[:, :], ada[:, gate_at:gate_at + KD], 0.5, None, ALU.mult))
                residual_sum(f"{key}_sum_done", f"{key}_sum_read", half_gate, 0)

            feed_forward("ffn1", True, 16)
            make_gain("mix", cols_b[:, 80:88], ada[:, 32:40])
            norm_root("mix", "sum_mix", rstd[:, 0:T])
            norm_scale("mix", xT, hT, rstd[:, 0:T])
            take_job("z_lat")
            empty_job(nc.vector.tensor_copy(latT[:, 0:2, :], job_wide("z_lat")))
            b = take_job("z_kv")
            nc.vector.tensor_copy(latT[:, 2, :], b[:, 0:T])
            empty_job(nc.vector.tensor_copy(squares[0:96, 3, :], b[0:96, T:2 * T]))
            item("mid", "ada14")
            for i in range(2):
                take_job(f"z_caq{i}")
                empty_job(nc.vector.tensor_scalar(ca_q[:, 2 * i:2 * i + 2, :], job_wide(f"z_caq{i}"), 0.125, None, ALU.mult))
            ada_col("col_ada14", 14)
            item("mid", "ada15")
            for i in range(2):
                take_job(f"z_cak{i}")
                empty_job(nc.vector.tensor_copy(ca_k[:, 2 * i:2 * i + 2, :], job_wide(f"z_cak{i}")))
            ada_col("col_ada15", 15)
            item("mid", "ada16")
            for i in range(2):
                take_job(f"z_cav{i}")
                empty_job(nc.vector.tensor_copy(ca_v[:, i, :], job_bank(f"z_cav{i}")[:, :]))
            b = take_job("lat_sum")
            nc.vector.tensor_scalar(rstd[:, 0:T], b[:, 0:T], 1.0 / 256, None, ALU.mult)
            empty_job(nc.vector.tensor_scalar(rstd[:, T:2 * T], b[:, T:2 * T], 1.0 / P, None, ALU.mult))
            ada_col("col_ada16", 16)
            item("mid", "ada17")
            dve.wait_ge(sem("lat_root"), 1)
            step(nc.vector.reciprocal(rstd[:, :], rstd[:, :]))
            for c in range(3):
                i = nc.vector.scalar_tensor_tensor(out=latT[:, c, :], in0=latT[:, c, :],
                                                   scalar=cols_b[:, ROWS_B["mla_q_norm"] + c:ROWS_B["mla_q_norm"] + c + 1],
                                                   in1=rstd[:, (c // 2) * T:(c // 2 + 1) * T], op0=ALU.mult, op1=ALU.mult)
            i.then_inc(sem("lat_ready"), 1)
            for i in range(4):
                take_job(f"z_ga{i}")
                empty_job(nc.vector.tensor_copy(gate_aT[:, 2 * i:2 * i + 2, :], job_wide(f"z_ga{i}")))
            ada_col("col_ada17", 17)
            for i in range(4):
                take_job(f"z_gb{i}_2")
                empty_job(nc.vector.tensor_copy(gate_bT[:, 2 * i:2 * i + 2, :], job_wide(f"z_gb{i}_2")))
            for i in range(4):
                take_job(f"mla_q{i}")
                empty_job(nc.vector.tensor_copy(mla_q[0:96, 2 * i:2 * i + 2, :], job_wide(f"mla_q{i}")[0:96, :, :]))
            for i in range(4):
                take_job(f"mla_k{i}")
                empty_job(nc.vector.tensor_copy(mla_k[0:64, 2 * i:2 * i + 2, :], job_wide(f"mla_k{i}")[0:64, :, :]))
            for i in range(2):
                take_job(f"mla_v{i}")
                empty_job(nc.vector.tensor_copy(mla_v[:, i, :], job_bank(f"mla_v{i}")[:, :]))
            nc.vector.tensor_copy(picked[:, 0, 36:37], picked[:, 0, 31:32]).then_inc(sem("mla_qk_ready"), 1)
            dve.wait_ge(sem("rope_ready"), 1)
            pe3 = pe_tmp.rearrange("p (a t) -> p a t", a=2)[64:96, :, :]
            cos, sin = tables(rope_cs[64:96, 1, :], rope_cs[64:96, 0, :], 2)
            for i in range(4):
                take_job(f"pe_rot{i}")
                q = mla_q[64:96, 2 * i:2 * i + 2, :]
                empty_job(nc.vector.tensor_tensor(pe3, job_wide(f"pe_rot{i}")[64:96, :, :], sin, ALU.mult))
                step(nc.vector.tensor_tensor(q, q, cos, ALU.mult))
                step(nc.vector.tensor_tensor(q, q, pe3, ALU.add))
            b = take_job("kpe_rot")
            kpe = squares[64:96, 3, :]
            empty_job(nc.vector.tensor_tensor(pe_tmp[64:96, 0:T], b[64:96, 0:T], rope_cs[64:96, 0, :], ALU.mult))
            step(nc.vector.tensor_tensor(kpe, kpe, rope_cs[64:96, 1, :], ALU.mult))
            step(nc.vector.tensor_tensor(kpe, kpe, pe_tmp[64:96, 0:T], ALU.add))
            nc.vector.tensor_copy(mla_k[64:96, :, :], squares[64:96, 3:4, :].broadcast_to((32, 8, T)))\
              .then_inc(sem("mla_ready"), 1)
            attention("mla")
            attention("ca")
            dve.wait_ge(sem("gates_ready"), 2)
            for i in range(4):
                pair = slice(2 * i, 2 * i + 2)
                take_job(f"branch_a{i}")
                empty_job(nc.vector.tensor_tensor(hT[:, pair, :], gate_aT[:, pair, :], job_wide(f"branch_a{i}"), ALU.mult))
                take_job(f"branch_b{i}")
                empty_job(nc.vector.tensor_tensor(gate_bT[:, pair, :], gate_bT[:, pair, :], job_wide(f"branch_b{i}"), ALU.mult))
                job_done_here()
                nc.vector.tensor_tensor(hT[:, pair, :], hT[:, pair, :], gate_bT[:, pair, :], ALU.add)\
                  .then_inc(sem("merged_ready"), 1)
            for i in range(4):
                residual_job(f"out2_{i}", i, ada, 40)
            make_gain("ffn2", cols_b[:, 88:96], ada[:, 56:64])
            norm_root("ffn2", "sum_ffn2", rstd[:, 0:T])
            norm_scale("ffn2", xT, hT, rstd[:, 0:T])
            feed_forward("ffn2", False, 64)
            norm_root("last", "sum_last", rstd[:, 0:T])
            norm_gain("last", "final_norm", col_b, rstd[:, 0:T])
            for i in range(4):
                take_job(f"y_turn{i}")
                empty_job(nc.vector.tensor_copy(h_rows[:, i // 2, 512 * (i % 2):512 * (i % 2) + 512], job_bank(f"y_turn{i}")[:, :]))
            assert emptied[0] == len(JOBS)


_INS = ["x", "c", "ctx", "c_ctx", "w_mod", "b_mod", "norm1_g", "w_in", "q_norm_g", "k_norm_g", "conv_w", "attn_out_g",
        "conv_out_g", "w_out", "norm2_g", "w_group", "w_router", "w_gate", "w_up", "w_down", "final_g", "c_2",
        "positions_2", "w_ada_2", "b_ada_2", "ffn1_norm_2", "ffn1_w_in_2", "ffn1_w_out_2", "mix_norm_2", "w_in_2",
        "mla_q_norm_2", "mla_w_uq_2", "mla_kv_norm_2", "mla_w_ukv_2", "rel_bias_2", "w_branch_a_2",
        "w_branch_b_2", "w_out_2", "ffn2_norm_2", "ffn2_w_in_2", "ffn2_w_out_2", "final_norm_2"]


def shape_constants():
    import numpy as np

    offsets, width = const_offsets()
    out = np.zeros((P, width), np.float32)

    def put(name, value):
        at, n = offsets[name]
        out[:, at:at + n] = value

    i = np.arange(P)
    put("ident", np.eye(P))
    put("ones", 1.0)
    put("mean", 1.0 / D)
    put("heads64", (i[:, None] // 64 == i[None, :] // 64) / 64.0)
    put("select", i[:, None] % 32 == np.arange(2)[None, :])
    put("reverse", i[:, None] + i[None, :] == P - 1)
    put("before", i[:, None] < i[None, :])
    first = (i % 32) < 16
    rot = np.zeros((P, P))
    rot[i[first] + 16, i[first]] = -1.0
    rot[i[~first] - 16, i[~first]] = 1.0
    put("rot_axial", rot)
    half = np.zeros((P, P))
    half[64:96, 64:96] = rot[64:96, 64:96]
    put("rot_half", half)
    put("slot", np.tile(np.arange(SLOTS), 2)[None, :])
    put("expert_id", np.arange(N_EXPERTS)[None, :])
    put("group_rank", (N_GROUPS - np.arange(N_GROUPS))[None, :])
    put("eps", EPS)
    inv_freq = (np.float32(10000.0) ** (-np.arange(0, 32, 2, dtype=np.float32) / np.float32(32))).astype(np.float32)
    put("inv_freq", inv_freq[i % 16][:, None])
    t = np.arange(T)
    where = np.where((i[:, None] % 64) < 32, (t // 64)[None, :], (t % 64)[None, :]).astype(np.float32)
    angle = (where * inv_freq[i % 16][:, None]).astype(np.float32)
    put("axial_cos", np.cos(angle))
    put("axial_sin", np.sin(angle))
    return out


def kernel(**inputs):
    import numpy as _np
    import concourse.bacc as _bacc
    from concourse import mybir as _mybir
    from concourse.bass_utils import run_bass_kernel_spmd as _run

    nc = _bacc.Bacc("TRN2", target_bir_lowering=False, num_devices=1, dynamic_dma_scratch_size=4096)
    arrays, aps = {}, {}
    given = {name: _np.ascontiguousarray(inputs[name]) for name in _INS}
    given["shape_constants"] = shape_constants()

    def rows(*names):
        return _np.ascontiguousarray(_np.concatenate([_np.ravel(given[name]) for name in names]).reshape(-1, P))

    given["vectors_a"] = rows("b_mod", "norm1_g", "norm2_g", "final_g", "c", "c_ctx", "q_norm_g", "q_norm_g",
                              "k_norm_g", "k_norm_g", "attn_out_g", "conv_out_g", "conv_w")
    given["vectors_b"] = rows("b_ada_2", "ffn1_norm_2", "mix_norm_2", "ffn2_norm_2", "final_norm_2", "c_2",
                              "mla_q_norm_2", "mla_kv_norm_2")
    for name in ("b_mod", "norm1_g", "norm2_g", "final_g", "c", "c_ctx", "q_norm_g", "k_norm_g", "attn_out_g",
                 "conv_out_g", "conv_w", "b_ada_2", "ffn1_norm_2", "mix_norm_2", "ffn2_norm_2", "final_norm_2", "c_2",
                 "mla_q_norm_2", "mla_kv_norm_2"):
        del given[name]
    for name, a in given.items():
        arrays[f"in_{name}_dram"] = a
        aps[name] = nc.dram_tensor(f"in_{name}_dram", a.shape, _mybir.dt.from_np(a.dtype), kind="ExternalInput").ap()
    out = nc.dram_tensor("out_0_dram", (1, T, D), _mybir.dt.float32, kind="ExternalOutput").ap()
    mixed_blocks_kernel(nc, aps, out)
    r = _run(nc, [arrays], core_ids=[0])
    return r.results[0]["out_0_dram"]
```

```python
import concourse.bass as bass
from concourse import mybir
from contextlib import ExitStack

F32 = mybir.dt.float32
F32R = mybir.dt.float32r
BF16 = mybir.dt.bfloat16
I32 = mybir.dt.int32
U32 = mybir.dt.uint32
ALU = mybir.AluOpType
ACT = mybir.ActivationFunctionType
AX_X = mybir.AxisListType.X

P = 128
T = 256
D = 1024
KD = D // P
EPS = 1e-6
N_GROUPS, GROUP_SIZE = 4, 8
N_EXPERTS = N_GROUPS * GROUP_SIZE
D_EXPERT = 768
HALF_E = D_EXPERT // 2
SLOTS = 64
PASSES = T // SLOTS
D_FF = 2816
FF_CHUNK = 256
FF_LOOPS = (D_FF // FF_CHUNK - 1) // 2
NO_SLOT = 10000.0
NEG = -1e30
ROPE_SCALE_2 = 96 ** -0.5
TWO_PI = 6.283185307179586
PI_A, PI_B = 6.28125, 0.0019350051879882812
PI_C = TWO_PI - PI_A - PI_B

CONST_COLS = [("ident", 128), ("ones", 128), ("mean", 128), ("heads64", 128), ("rot_axial", 128), ("rot_half", 128),
              ("reverse", 128), ("before", 128), ("slot", 128), ("expert_id", 32), ("group_rank", 4),
              ("eps", 1), ("inv_freq", 1), ("select", 2), ("axial_cos", 256), ("axial_sin", 256)]


def const_offsets():
    at, out = 0, {}
    for name, width in CONST_COLS:
        out[name] = (at, width)
        at += width
    return out, at


ROWS_A = {"b_mod": 0, "norm1_g": 48, "norm2_g": 56, "final_g": 64, "c": 72, "c_ctx": 80, "q_norm_g": 88,
          "k_norm_g": 89, "attn_out_g": 90, "conv_out_g": 94, "conv_w": 98}
N_ROWS_A = 110
ROWS_B = {"b_ada": 0, "ffn1_norm": 72, "mix_norm": 80, "ffn2_norm": 88, "final_norm": 96, "c": 104,
          "mla_q_norm": 112, "mla_kv_norm": 114}
N_ROWS_B = 115

JOBS = (["rows_a", "rows_b"] + [f"x_turn{i}" for i in range(4)] + [f"ctx_turn{i}" for i in range(4)]
        + ["sum_x", "sum_ctx", "modrow0", "modrow1", "mod0", "modrow2", "mod1", "modrow3", "mod2", "mod3"]
        + ["z_k", "z_v", "col_gt1a", "z_q0", "z_q1", "col_gt1b", "z_gb0", "z_gb1", "col_sh2a",
           "z_gc0", "z_gc1", "col_sh2b", "z_u0", "z_u1", "col_sc2a"]
        + [f"qk_sum{i}" for i in range(3)] + ["row_sc2b", "row_gt2a", "col_sc2b", "col_gt2a"] + [f"qk_rot{i}" for i in range(3)]
        + [f"attn_o{i}" for i in range(4)] + [f"head_sum{i}" for i in range(4)] + ["row_gt2b", "col_gt2b"]
        + [f"merge{i}" for i in range(4)] + ["sum_n2", "logits"] + [f"h2_turn{i}" for i in range(4)]
        + ["positions", "bias_turn"]
        + ["row_ada0", "sum_final", "row_ada1", "col_ada0", "row_ada2", "col_ada1", "row_ada3", "col_ada2", "col_ada3", "sum_ffn1"]
        + ["sum_mix", "z_lat", "z_kv", "z_caq0", "z_caq1", "col_ada14", "z_cak0", "z_cak1", "col_ada15", "z_cav0", "z_cav1",
           "lat_sum", "col_ada16", "z_ga0", "z_ga1", "z_ga2", "z_ga3", "col_ada17"]
        + [f"mla_q{i}" for i in range(4)] + [f"mla_k{i}" for i in range(4)] + ["mla_v0", "mla_v1", "z_gb0_2", "z_gb1_2"]
        + [f"pe_rot{i}" for i in range(4)] + ["kpe_rot", "z_gb2_2", "z_gb3_2"]
        + [f"mla_o{i}" for i in range(4)] + [f"ca_o{i}" for i in range(4)]
        + [f"branch_{ab}{i}" for i in range(4) for ab in "ab"] + [f"out2_{i}" for i in range(4)]
        + ["sum_ffn2", "sum_last"] + [f"y_turn{i}" for i in range(4)])
JOB = {name: j for j, name in enumerate(JOBS)}
assert len(JOB) == len(JOBS)

RING = 6
SLOT_W = 4096
PRE = ([(f"mod{i}", f"modrow{i}") for i in range(4)]
       + [("w_kv", "z_v"), ("gt1a", 0), ("w_q", "z_q1"), ("gt1b", 1), ("w_gb", "z_gb1"), ("sh2a", 2), ("w_gc", "z_gc1"),
          ("sh2b", 3), ("w_u", "z_u1"), ("sc2a", 4), ("sc2b", "row_sc2b"), ("gt2a", "row_gt2a"), ("gt2b", "row_gt2b"), ("w_out0", "merge1"),
          ("w_out1", "merge3")])
MID = ([("ada14", 15), ("w2_lat", "z_kv"), ("w2_caq", "z_caq1"), ("w2_cak", "z_cak1"), ("ada15", 16), ("w2_cav", "z_cav1"),
        ("ada16", 17), ("w2_ga0", "z_ga1"), ("w2_ga1", "z_ga3"), ("ada17", 18), ("mla_up", "mla_v1"),
        ("w2_gb0", "z_gb1_2"), ("w2_gb1", "z_gb3_2"), ("w_branch_a", "branch_a3"), ("w_branch_b", "branch_b3"),
        ("w_out2_0", "out2_1"), ("w_out2_1", "out2_3")])


def ring_places():
    place, loads = {}, [0] * RING
    for part, items in (("pre", PRE), ("ada", [(f"ada{i}", f"row_ada{i}") for i in range(4)]), ("mid", MID)):
        for at, (name, _) in enumerate(items):
            s = at % RING
            if name == "w_out1":
                s = 4
            if part == "ada" and at >= 2:
                s = at + 1
            if name != "mla_up":
                loads[s] += 1
            place[(part, name)] = (s, loads[s])
    return place


def mixed_blocks_kernel(nc, ins, out):
    C, n_const = const_offsets()
    PLACE = ring_places()

    with ExitStack() as ctx:
        def sb(name, shape, dt=F32):
            return ctx.enter_context(nc.sbuf_tensor(name, shape, dt))

        sems = {}

        def sem(name):
            if name not in sems:
                sems[name] = ctx.enter_context(nc.semaphore(name))
            return sems[name]

        consts = sb("consts", [P, n_const])
        rows_a = sb("rows_a", [N_ROWS_A, P])
        rows_b = sb("rows_b", [N_ROWS_B, P])
        cols_a = sb("cols_a", [P, N_ROWS_A])
        cols_b = sb("cols_b", [P, N_ROWS_B])
        xT = sb("xT", [P, KD, T])
        hT = sb("hT", [P, KD, T])
        squares = sb("squares", [P, KD, T])
        mixT = sb("mixT", [P, KD, T])
        h_rows = sb("h_rows", [P, 2, D])
        rstd = sb("rstd", [P, 2 * T])
        small_at = nc.sbuf_base
        small = sb("small", [P, 2048])
        cond = sb("cond", [P, KD, 32])
        cond_ada = sb("cond_ada", [P, KD, 32])
        warmed = sb("warmed", [1, 32])
        cond2 = sb("cond2", [P, KD])
        mod = sb("mod", [P, 6 * KD])
        mod_ctx = sb("mod_ctx", [P, 2 * KD])
        ada = sb("ada", [P, 9 * KD])
        gains = sb("gains", [P, 3 * KD])
        mod_acc = sb("mod_acc", [P, 2, 512])
        stats = sb("stats", [P, 3, 3, 16])
        router = sb("router", [P, KD, 36])
        route = sb("route", [P, 2, 168])
        picked = sb("picked", [P, 2, 40])
        picked_i = sb("picked_i", [P, 2, 8], U32)
        busiest = sb("busiest", [1, 1], I32)
        zeros = sb("zeros", [P, 512], BF16)
        ARENA = 9 * SLOT_W
        arena_at = nc.sbuf_base
        arena = sb("arena", [P, ARENA])

        def rounded(name, at, size, base=arena_at):
            return nc.alloc_sbuf_tensor_at(name, [P, size], F32R, offset=base + 4 * at).ap()

        ff_w_lo = {slot: rounded(f"ff_w_lo{slot}", slot * SLOT_W, SLOT_W) for slot in (0, 2)}
        ff_w_hi = {slot: rounded(f"ff_w_hi{slot}", (RING + slot // 2) * SLOT_W, SLOT_W) for slot in (0, 2)}
        ff_out_lo = {slot: rounded(f"ff_out_lo{slot}", slot * SLOT_W, 2 * D) for slot in (1, 3)}
        ff_out_hi = {slot: rounded(f"ff_out_hi{slot}", slot * SLOT_W + 2 * D, 2 * D) for slot in (1, 3)}
        ff_act_hi, ff_act_lo = (rounded(f"ff_act_{part}", at, 2 * T, small_at).rearrange("p (b t) -> p b t", b=2)
                                for part, at in (("hi", 1024), ("lo", 1536)))
        ff_x_hi = rounded("ff_x_hi", 8 * SLOT_W, KD * T).rearrange("p (k t) -> p k t", k=KD)
        ff_x_lo = rounded("ff_x_lo", 8 * SLOT_W + KD * T, KD * T).rearrange("p (k t) -> p k t", k=KD)

        def ff_half(w, half):
            return w.rearrange("p (k g n) -> p k g n", k=KD, g=2)[:, :, :, half * P:(half + 1) * P]

        def ring(slot):
            return arena[:, slot * SLOT_W:(slot + 1) * SLOT_W]

        def ring_w(part, name):
            return ring(PLACE[(part, name)][0]).rearrange("p (k n) -> p k n", k=KD)

        EW = KD * D_EXPERT

        def expert_w(u):
            base = 3 * EW * u
            gate = arena[:, base:base + EW].rearrange("p (k n) -> p k n", k=KD)
            up = arena[:, base + EW:base + 2 * EW].rearrange("p (k n) -> p k n", k=KD)
            down = arena[:, base + 2 * EW:base + 3 * EW].rearrange("p (k n) -> p k n", k=6)
            return gate, up, down

        temp_at = [RING * SLOT_W]

        def temp(*shape):
            n = 1
            for s in shape:
                n *= s
            a = arena[:, temp_at[0]:temp_at[0] + n]
            temp_at[0] += n
            assert temp_at[0] <= ARENA
            if len(shape) == 1:
                return a
            names = "abc"[:len(shape)]
            spec = {names[i]: shape[i] for i in range(len(shape))}
            return a.rearrange(f"p ({' '.join(names)}) -> p {' '.join(names)}", **spec)

        logits, assigned = route[:, :, 0:36], route[:, :, 36:68]
        places, weights = route[:, :, 68:101], route[:, :, 101:134]
        route_tmp = route[:, :, 134:166]
        rel_bias_rows = sb("rel_bias_rows", [P, 4, 8])
        half_gate = sb("half_gate", [P, KD])
        x_rows, ctx_rows = temp(2, D), temp(2, D)
        ctxT = h_rows[:, :, :].rearrange("p b (k t) -> p (b k) t", t=T)
        ctx_squares = x_rows.rearrange("p b (k t) -> p (b k) t", t=T)
        gate_aT, gate_bT = ctxT, mixT[:, :, :]
        qk = temp(6, T)
        v1 = temp(4, P)
        gate_b = temp(4, T)
        conv_in = temp(4, T + 2)
        conv_out = temp(4, T)
        qk_tmp = temp(6, T)
        temp_at[0] = RING * SLOT_W
        mla_q, mla_k = temp(8, T), temp(8, T)
        mla_v = temp(2, 512)
        ca_q, ca_k, ca_v = temp(4, T), temp(4, T), temp(2, 512)
        ca_bias = temp(3072)
        bias_early = ca_bias[:, 0:8 * P].rearrange("p (h k) -> p h k", h=8)
        bias_late = ca_bias[:, 8 * P:24 * P].rearrange("p (h k) -> p h k", h=8)
        latT = small[:, 0:3 * T].rearrange("p (c t) -> p c t", c=3)
        pe_tmp = small[:, 768:768 + 512]
        angle = small[:, 0:5 * T].rearrange("p (a t) -> p a t", a=5)
        bias_rows = small[0:8, 1536:2048]
        rope_cs = sb("rope_cs", [P, 2, T])
        turns = small[:, 5 * T:6 * T].bitcast(I32)
        probs = small[:, 0:1024].rearrange("p (b k) -> p b k", b=2)
        probsT = small[:, 1024:2048].rearrange("p (b n) -> p b n", b=2)
        pick = mixT[:, 0, 0:2 * SLOTS].rearrange("p (b s) -> p b s", b=2)
        pick_w = mixT[:, 1, :].rearrange("p (b s) -> p b s", b=2)
        xeT = mixT[:, 2:4, :].rearrange("p a t -> p (a t)").rearrange("p (k s) -> p k s", k=KD)
        gate_act = mixT[:, 4:6, :].rearrange("p a t -> p (a t)")[:, 0:HALF_E]
        hidden = mixT[:, 6:8, :].rearrange("p a t -> p (a t)")[:, 0:HALF_E]
        hiddenT = small[:, 0:HALF_E].rearrange("p (c s) -> p c s", c=3)
        y_e = small[:, 512:1024]
        pick_wT = small[:, 1024:1536].rearrange("p (b t) -> p b t", b=2)
        silu_g = small[:, 0:512].rearrange("p (b t) -> p b t", b=2)
        ff_act = small[:, 512:1024].rearrange("p (b t) -> p b t", b=2)

        bank = [ctx.enter_context(nc.psum_tensor(f"bank{i}", [P, 512], F32)) for i in range(8)]
        bias_scratch = nc.dram_tensor("bias_scratch", (8, 512), F32, kind="Internal").ap()

        def K(name):
            at, width = C[name]
            return consts[:, at:at + width]

        def col_a(name, i=0):
            return cols_a[:, ROWS_A[name] + i:ROWS_A[name] + i + 1]

        def col_b(name, i=0):
            return cols_b[:, ROWS_B[name] + i:ROWS_B[name] + i + 1]

        def job_bank(name):
            return bank[JOB[name] % 4]

        def job_wide(name):
            return job_bank(name)[:, :].rearrange("p (a t) -> p a t", a=2)

        SET = {"n1": 0, "c1": 1, "n2": 0, "ffn1": 1, "mix": 2, "ffn2": 0}

        def gain(key, k):
            return gains[:, SET[key] * KD + k:SET[key] * KD + k + 1]

        def attention_1():
            for h in range(8):
                g = 64 * (h // 4)
                for qb in range(2):
                    yield dict(job=f"attn_o{h // 2}", last=(h % 2 == 1 and qb == 1), col=64 * (h % 2), qb=qb, keys=512,
                               q=[qk[g:g + 64, h % 4, qb * P:qb * P + P]],
                               k=[qk[g:g + 64, 4:6, :].rearrange("p a t -> p (a t)")],
                               v=[v1[:, b, g:g + 64] for b in range(4)], mask=False)

        def attention_mla():
            for h in range(8):
                for qb in range(2):
                    n = (qb + 1) * P
                    yield dict(job=f"mla_o{h // 2}", last=(h % 2 == 1 and qb == 1), col=64 * (h % 2), qb=qb, keys=n,
                               q=[mla_q[0:96, h, qb * P:qb * P + P]], k=[mla_k[0:96, h, 0:n]],
                               v=[mla_v[:, b, 64 * h:64 * h + 64] for b in range(qb + 1)], mask=True)

        def attention_ca():
            for h in range(8):
                p = 64 * (h % 2)
                for qb in range(2):
                    n = (qb + 1) * P
                    bias = bias_late[:, h, :] if qb else bias_early[:, h, :]
                    yield dict(job=f"ca_o{h // 2}", last=(h % 2 == 1 and qb == 1), col=p, qb=qb, keys=n,
                               q=[ca_q[p:p + 64, h // 2, qb * P:qb * P + P], K("reverse")],
                               k=[ca_k[p:p + 64, h // 2, 0:n], bias],
                               v=[ca_v[:, b, 64 * h:64 * h + 64] for b in range(qb + 1)], mask=True)

        ATTENTIONS = {"at1": (0, list(attention_1()), 0.125), "mla": (1, list(attention_mla()), ROPE_SCALE_2),
                      "ca": (2, list(attention_ca()), 1.0)}
        ATT_OUT = {"at1": lambda c: mixT[:, c, :], "mla": lambda c: squares[:, c, :], "ca": lambda c: squares[:, 4 + c, :]}

        block = ctx.enter_context(nc.Block())

        def wait_item_read(eng, reader):
            if isinstance(reader, int):
                eng.wait_ge(sem("mod_acc_step"), 8 * (reader + 1))
            else:
                eng.wait_ge(sem("job_ready"), JOB[reader] + 1)

        def chunked(ap, lo, hi):
            return ap[:, lo:hi].rearrange("(k p) n -> p k n", p=P)

        @block.sync
        def _(sp):
            readers = {}

            def load(part, name, src, reader, width=512, k=KD):
                slot, use = PLACE[(part, name)]
                if slot in readers:
                    wait_item_read(sp, readers[slot])
                dst = ring(slot).rearrange("p (k n) -> p k n", k=k)[:, :, 0:width]
                sp.dma_start(dst, src).then_inc(sem(f"ring_full{slot}"), 16)
                readers[slot] = reader

            sp.dma_start(x_rows, ins["x"][0].rearrange("(b p) d -> p b d", p=P)).then_inc(sem("x_loaded"), 16)
            sp.dma_start(ctx_rows, ins["ctx"][0].rearrange("(b p) d -> p b d", p=P)).then_inc(sem("ctx_loaded"), 16)
            w_mod, w_in, w_out = ins["w_mod"][0], ins["w_in"][0], ins["w_out"][0]
            seg = {"gt1a": 2048, "gt1b": 2560, "sh2a": 3072, "sh2b": 3584, "sc2a": 4096, "sc2b": 4608, "gt2a": 5120, "gt2b": 5632}
            win = {"w_q": (0, 512), "w_kv": (512, 256), "w_gb": (768, 512), "w_gc": (1280, 512), "w_u": (1792, 512)}
            for name, reader in PRE:
                if name in win:
                    at, width = win[name]
                    load("pre", name, chunked(w_in, at, at + width), reader, width)
                elif name.startswith("w_out"):
                    at = 512 * int(name[-1])
                    load("pre", name, chunked(w_out, at, at + 512), reader)
                else:
                    at = seg[name] if name in seg else 512 * int(name[-1])
                    load("pre", name, chunked(w_mod, at, at + 512), reader)

            w_gate, w_up, w_down = ins["w_gate"][0], ins["w_up"][0], ins["w_down"][0]

            def load_gate_up(u, e):
                gate, up, _ = expert_w(u)
                sp.dma_start(gate, w_gate[bass.ds(e, 1)].rearrange("a (k p) n -> p (a k) n", p=P))\
                  .then_inc(sem(f"gate_full{u}"), 16)
                sp.dma_start(up, w_up[bass.ds(e, 1)].rearrange("a (k p) n -> p (a k) n", p=P))\
                  .then_inc(sem(f"up_full{u}"), 16)

            def load_down(u, e):
                _, _, down = expert_w(u)
                sp.dma_start(down, w_down[bass.ds(e, 1)].rearrange("a (k p) n -> p (a k) n", p=P))\
                  .then_inc(sem(f"down_full{u}"), 16)

            def load_expert(u, e, done):
                sp.wait_ge(sem("gate_up_done"), done)
                load_gate_up(u, e)
                sp.wait_ge(sem("down_done"), done)
                load_down(u, e)

            for s in range(3):
                wait_item_read(sp, readers[s])
            load_gate_up(0, 0)
            for s in range(3, RING):
                wait_item_read(sp, readers[s])
            readers.clear()
            load_down(0, 0)
            sp.wait_ge(sem("mg_ready"), KD)
            load_gate_up(1, 1)
            load_down(1, 1)
            with sp.Fori(1, N_EXPERTS // 2) as it:
                for u in range(2):
                    load_expert(u, it * 2 + u, it * 2 + u - 1)
            sp.wait_ge(sem("busiest_ready"), 1)
            most = sp.value_load(busiest[0:1, 0:1], min_val=0, max_val=T)
            with sp.If(most > SLOTS):
                with sp.Fori(1, PASSES) as ps:
                    with sp.Fori(0, N_EXPERTS // 2) as it:
                        for u in range(2):
                            load_expert(u, it * 2 + u, ps * N_EXPERTS + it * 2 + u - 1)
                sp.wait_ge(sem("gate_up_done"), PASSES * N_EXPERTS)
                sp.wait_ge(sem("down_done"), PASSES * N_EXPERTS)

            w_ada = ins["w_ada_2"][0]
            sp.wait_ge(sem("gate_up_done"), N_EXPERTS - 1)
            sp.wait_ge(sem("down_done"), N_EXPERTS - 1)
            for i in range(4):
                if i == 3:
                    sp.wait_ge(sem("experts_done"), 1)
                load("ada", f"ada{i}", chunked(w_ada, 512 * i, 512 * i + 512), f"row_ada{i}")

            def load_ff_in(slot, w, c, key):
                dst = ring(slot).rearrange("p (k g n) -> p k g n", k=KD, g=2)
                for g in range(2):
                    sp.dma_start(dst[:, :, g, :], w[:, bass.ds(c * FF_CHUNK + g * D_FF, FF_CHUNK)]
                                 .rearrange("(k p) n -> p k n", p=P)).then_inc(sem(f"{key}_in_full{slot}"), 16)

            def load_ff_out(slot, w, c, key):
                dst = ring(slot)[:, 0:2 * D].rearrange("p (k n) -> p k n", k=2)
                sp.dma_start(dst, w[bass.ds(c * FF_CHUNK, FF_CHUNK), :].rearrange("(k p) n -> p k n", p=P))\
                  .then_inc(sem(f"{key}_out_full{slot}"), 16)

            def load_ada(it, u, two_before=True):
                if two_before:
                    sp.wait_ge(sem("mod_acc_step"), it * 16 + 8 * (4 + u))
                sp.dma_start(ring(4 + u).rearrange("p (k n) -> p k n", k=KD),
                             w_ada[:, bass.ds(it * 1024 + (4 + u) * 512, 512)]
                             .rearrange("(k p) n -> p k n", p=P)).then_inc(sem(f"ada_full{4 + u}"), 16)

            def feed_forward(key, w_in_ff, w_out_ff, with_ada):
                if 2 in readers:
                    wait_item_read(sp, readers[2])
                load_ff_in(2, w_in_ff, 0, key)
                wait_item_read(sp, readers[3])
                load_ff_out(3, w_out_ff, 0, key)
                for s in (0, 1):
                    wait_item_read(sp, readers[s])
                load_ff_in(0, w_in_ff, 1, key)
                if with_ada:
                    wait_item_read(sp, readers[4])
                    load_ada(0, 0, two_before=False)
                load_ff_out(1, w_out_ff, 1, key)

                def load_even(it):
                    sp.wait_ge(sem(f"{key}_gate_up_done"), it * 4 + 2)
                    load_ff_in(2, w_in_ff, it * 2 + 2, key)
                    if with_ada:
                        load_ada(it, 1)
                    sp.wait_ge(sem(f"{key}_down_done"), it * 4 + 2)
                    load_ff_out(3, w_out_ff, it * 2 + 2, key)

                with sp.Fori(0, FF_LOOPS - 1) as it:
                    load_even(it)
                    sp.wait_ge(sem(f"{key}_gate_up_done"), it * 4 + 4)
                    load_ff_in(0, w_in_ff, it * 2 + 3, key)
                    if with_ada:
                        load_ada(it + 1, 0)
                    sp.wait_ge(sem(f"{key}_down_done"), it * 4 + 4)
                    load_ff_out(1, w_out_ff, it * 2 + 3, key)
                load_even(FF_LOOPS - 1)
                sp.wait_ge(sem(f"{key}_sum_done"), 1)
                readers.clear()

            feed_forward("ffn1", ins["ffn1_w_in_2"][0], ins["ffn1_w_out_2"][0], True)
            w_in2 = ins["w_in_2"][0]
            w2 = {"w2_lat": (0, 416), "w2_caq": (416, 512), "w2_cak": (928, 512), "w2_cav": (1440, 512),
                  "w2_ga0": (1952, 512), "w2_ga1": (2464, 512), "w2_gb0": (2976, 512), "w2_gb1": (3488, 512)}
            sp.wait_ge(sem("mod_acc_step"), 8 * 15)
            for name, reader in MID:
                if name.startswith("ada"):
                    i = int(name[3:])
                    load("mid", name, chunked(w_ada, 512 * i, 512 * i + 512), reader)
                elif name == "mla_up":
                    slot, _ = PLACE[("mid", name)]
                    wait_item_read(sp, readers[slot])
                    sp.dma_start(ring(slot)[:, 0:1536].rearrange("p (k n) -> p k n", k=2),
                                 ins["mla_w_uq_2"][0].rearrange("(k p) n -> p k n", p=P)).then_inc(sem("w_uq_full"), 16)
                    sp.dma_start(ring(slot)[:, 1536:2560], ins["mla_w_ukv_2"][0]).then_inc(sem("w_ukv_full"), 16)
                    readers[slot] = reader
                elif name.startswith("w_branch"):
                    load("mid", name, chunked(ins[name + "_2"][0], 0, D), reader, D, 4)
                elif name.startswith("w_out2"):
                    at = 512 * int(name[-1])
                    load("mid", name, chunked(ins["w_out_2"][0], at, at + 512), reader)
                else:
                    at, width = w2[name]
                    load("mid", name, chunked(w_in2, at, at + width), reader, width)
            feed_forward("ffn2", ins["ffn2_w_in_2"][0], ins["ffn2_w_out_2"][0], False)
            sp.wait_ge(sem("job_emptied"), len(JOBS))
            sp.dma_start(out[0].rearrange("(b p) d -> p b d", p=P), h_rows[:, :, :]).then_inc(sem("stored"), 16)
            sp.wait_ge(sem("stored"), 16)

        @block.gpsimd
        def _(pool):
            n_step = [0]

            def step(instruction):
                n_step[0] += 1
                instruction.then_inc(sem("pool_step"), 1)
                pool.wait_ge(sem("pool_step"), n_step[0])

            pool.wait_ge(sem("job_emptied"), JOB["z_u1"] + 1)
            for tap in range(3):
                for c in range(4):
                    w = col_a("conv_w", 4 * tap + c)
                    dst = conv_out[:, c, :] if tap == 0 else mixT[:, 4 + c, :]
                    i = nc.gpsimd.tensor_scalar(dst, conv_in[:, c, tap:tap + T], w, 0.0, ALU.mult, ALU.add)
                step(i)
                if tap:
                    step(nc.gpsimd.tensor_tensor(conv_out, conv_out, mixT[:, 4:8, :], ALU.add))
            nc.gpsimd.tensor_tensor(mixT[:, 4:8, :], conv_out, gate_b, ALU.mult).then_inc(sem("conv_done"), 1)
            pool.wait_ge(sem("job_emptied"), JOB["bias_turn"] + 1)
            pool.dma_start(bias_scratch, bias_rows).then_inc(sem("bias_stored"), 16)
            pool.wait_ge(sem("bias_stored"), 16)
            pool.wait_ge(sem("ffn1_sum_done"), 1)
            for tile, first in ((bias_early, 129), (bias_late, 1)):
                src = bass.AP(bias_scratch.tensor, first, [[1, P], [512, 8], [1, tile.shape[2]]])
                pool.dma_start(tile, src).then_inc(sem("bias_loaded"), 16)


        @block.scalar
        def _(act):
            n_step = [0]

            def step(instruction):
                n_step[0] += 1
                instruction.then_inc(sem("act_step"), 1)
                act.wait_ge(sem("act_step"), n_step[0])

            n_warm = [0]

            def warm(function):
                act.wait_ge(sem("consts_loaded"), 16)
                nc.scalar.activation(warmed[0:1, n_warm[0]:n_warm[0] + 1], K("eps")[0:1, :], function)
                n_warm[0] += 1

            act.dma_start(consts[:, :], ins["shape_constants"]).then_inc(sem("consts_loaded"), 16)
            act.dma_start(rows_a[:, :], ins["vectors_a"]).then_inc(sem("rows_a_loaded"), 16)
            act.dma_start(rows_b[:, :], ins["vectors_b"]).then_inc(sem("rows_b_loaded"), 16)
            act.dma_start(turns[64:96, :], ins["positions_2"][0].partition_broadcast(32)).then_inc(sem("positions_loaded"), 16)
            act.dma_start(router[:, :, 0:4], ins["w_group"][0].rearrange("(k p) n -> p k n", p=P))\
               .then_inc(sem("router_loaded"), 16)
            act.dma_start(router[:, :, 4:36], ins["w_router"][0].rearrange("(k p) n -> p k n", p=P))\
               .then_inc(sem("router_loaded"), 16)
            for b in range(4):
                act.dma_start(rel_bias_rows[:, b, :], ins["rel_bias_2"][0][385 - P * b:513 - P * b, :])\
                   .then_inc(sem("rel_bias_loaded"), 16)

            act.wait_ge(sem("cond_zeroed"), 1)
            act.wait_ge(sem("job_emptied"), 1)
            for i, name in enumerate(("c", "c_ctx")):
                r = ROWS_A[name]
                ins_ = nc.scalar.activation(cond[:, :, i], cols_a[:, r:r + KD], ACT.Silu)
                ins_.then_inc(sem("cond_ready"), 1)
            act.wait_ge(sem("job_emptied"), 2)
            c2 = cols_b[:, ROWS_B["c"]:ROWS_B["c"] + KD]
            nc.scalar.activation(cond2[:, :], c2, ACT.Silu).then_inc(sem("cond_ready"), 1)
            nc.scalar.activation(cond_ada[:, :, 0], c2, ACT.Silu).then_inc(sem("cond_ready"), 1)

            def head_squares(key, src, dst, source, value=1):
                act.wait_ge(sem(source), value)
                nc.scalar.activation(dst, src, ACT.Square).then_inc(sem(f"{key}_squares"), 1)
                warm(ACT.Sqrt)

            def norm_squares(key, src, dst, source, first, by):
                for i in range(KD // 2):
                    act.wait_ge(sem(source), first + by * i)
                    nc.scalar.activation(dst[:, 2 * i:2 * i + 2, :], src[:, 2 * i:2 * i + 2, :], ACT.Square)\
                      .then_inc(sem(f"{key}_squares"), 1)

            def norm_root(key, job, dst):
                act.wait_ge(sem("job_ready"), JOB[job] + 1)
                nc.scalar.activation(dst, job_bank(job)[:, 0:T], ACT.Sqrt, bias=K("eps")).then_inc(sem(f"{key}_root"), 1)

            def head_root(key, jobs, dst):
                for i, job in enumerate(jobs):
                    act.wait_ge(sem("job_ready"), JOB[job] + 1)
                    nc.scalar.activation(dst[:, 2 * i:2 * i + 2, :], job_wide(job), ACT.Sqrt, bias=K("eps"))\
                      .then_inc(sem(f"{key}_root"), 1)

            def norm_shift(key, dst, shifts, shift_at, src=None):
                for k in range(KD):
                    act.wait_ge(sem(f"{key}_scaled"), k + 1)
                    nc.scalar.activation(dst[:, k, :], (dst if src is None else src)[:, k, :], ACT.Identity,
                                         bias=shifts[:, shift_at + k:shift_at + k + 1]).then_inc(sem(f"{key}_ready"), 1)

            def attention(key):
                index, instances, scale = ATTENTIONS[key]
                n = len(instances)
                for i in range(n + 2):
                    if i < n:
                        it = instances[i]
                        act.wait_ge(sem(f"{key}_negmax"), i + 1)
                        if i >= 2:
                            act.wait_ge(sem(f"{key}_turned"), i - 1)
                        nc.scalar.activation(probs[:, i % 2, 0:it["keys"]], bank[4 + i % 2][:, 0:it["keys"]], ACT.Exp,
                                             bias=stats[:, index, 0, i:i + 1], scale=scale,
                                             accum_out=stats[:, index, 1, i:i + 1]).then_inc(sem(f"{key}_exp"), 1)
                    if i >= 2:
                        j = i - 2
                        act.wait_ge(sem(f"{key}_turned"), j + 1)
                        w = instances[j]["keys"]
                        nc.scalar.activation(probsT[:, j % 2, 0:w], bank[6 + j % 2][:, 0:w], ACT.Copy)\
                          .then_inc(sem(f"{key}_probsT"), 1)

            norm_squares("n1", xT, squares, "job_emptied", JOB["x_turn0"] + 1, 1)
            act.wait_ge(sem("job_ready"), JOB["x_turn3"] + 1)
            norm_squares("c1", ctxT, ctx_squares, "job_emptied", JOB["ctx_turn0"] + 1, 1)
            warm(ACT.Sqrt)
            norm_root("n1", "sum_x", rstd[:, 0:T])
            norm_root("c1", "sum_ctx", rstd[:, T:2 * T])
            norm_shift("c1", mixT, mod_ctx, 0)
            norm_shift("n1", hT, mod, 0)
            act.wait_ge(sem("angles_ready"), 1)
            nc.scalar.activation(rope_cs[64:96, :, :], angle[64:96, 2:4, :], ACT.Sin).then_inc(sem("rope_ready"), 1)
            head_squares("qk", qk, squares[:, 0:6, :], "job_emptied", JOB["z_q1"] + 1)
            head_root("qk", [f"qk_sum{i}" for i in range(3)], qk_tmp)
            warm(ACT.Exp)
            attention("at1")
            act.wait_ge(sem("conv_done"), 1)
            head_squares("mg", mixT[:, :, :], squares[:, :, :], "job_emptied", JOB["attn_o3"] + 1)
            head_root("mg", [f"head_sum{i}" for i in range(4)], h_rows[:, :, :].rearrange("p b (k t) -> p (b k) t", t=T))
            norm_squares("n2", xT, squares, "job_emptied", JOB["merge0"] + 1, 1)
            norm_root("n2", "sum_n2", rstd[:, 0:T])
            norm_shift("n2", hT, mod, 24)
            warm(ACT.Exp)
            act.wait_ge(sem("router_max"), 2)
            for b in range(2):
                nc.scalar.activation(picked[:, b, 4:8], route[:, b, 0:4], ACT.Exp, bias=picked[:, b, 0:1],
                                     accum_out=picked[:, b, 1:2]).then_inc(sem("group_exp"), 1)
            act.wait_ge(sem("router_top"), 2)
            for b in range(2):
                nc.scalar.activation(picked[:, b, 2:3], picked[:, b, 17:18], ACT.Exp, bias=picked[:, b, 3:4])\
                  .then_inc(sem("second_exp"), 1)

            def expert_in(count):
                act.wait_ge(sem("gathered"), count)
                nc.scalar.activation(xeT, bank[4][:, :].rearrange("p (k s) -> p k s", k=KD), ACT.Copy)\
                  .then_inc(sem("xe_ready"), 1)

            def expert_steps(n, prep):
                act.wait_ge(sem("gate_up_done"), n)
                nc.scalar.activation(gate_act, bank[4][:, 0:HALF_E], ACT.Silu).then_inc(sem("gate_act_ready"), 1)
                act.wait_ge(sem("hidden_turned"), n)
                nc.scalar.activation(hiddenT, bank[5][:, 0:HALF_E].rearrange("p (c s) -> p c s", c=3), ACT.Copy)\
                  .then_inc(sem("hiddenT_ready"), 1)
                expert_in(prep)
                act.wait_ge(sem("down_done"), n)
                nc.scalar.activation(y_e, bank[6][:, :], ACT.Copy).then_inc(sem("y_ready"), 1)

            expert_in(1)
            with act.Fori(0, N_EXPERTS // 2) as it:
                for u in range(2):
                    expert_steps(it * 2 + u + 1, it * 2 + u + 2)
            act.wait_ge(sem("busiest_ready"), 1)
            most = act.value_load(busiest[0:1, 0:1], min_val=0, max_val=T)
            with act.If(most > SLOTS):
                with act.Fori(1, PASSES) as ps:
                    expert_in(ps * (N_EXPERTS + 1) + 1)
                    with act.Fori(0, N_EXPERTS // 2) as it:
                        for u in range(2):
                            expert_steps(ps * N_EXPERTS + it * 2 + u + 1, ps * (N_EXPERTS + 1) + it * 2 + u + 2)

            warm(ACT.Sqrt)
            norm_squares("fin1", xT, squares, "y_moe_read", 1, 1)
            norm_root("fin1", "sum_final", rstd[:, 0:T])

            def ff_round(key, slot, half, arrivals):
                act.wait_ge(sem(f"{key}_in_full{slot}"), arrivals)
                nc.scalar.activation(ff_half(ff_w_hi[slot], half), ff_half(ring(slot), half), ACT.Copy)\
                  .then_inc(sem(f"{key}_w_hi"), 1)

            def ff_round_out(key, slot, half, arrivals):
                act.wait_ge(sem(f"{key}_out_full{slot}"), arrivals)
                nc.scalar.activation(ff_out_hi[slot][:, half * D:(half + 1) * D], ring(slot)[:, half * D:(half + 1) * D],
                                     ACT.Copy).then_inc(sem(f"{key}_out_hi"), 1)

            def feed_forward(key, split_out):
                def silu(s, parity):
                    act.wait_ge(sem(f"{key}_gate_up_done"), s)
                    nc.scalar.activation(silu_g[:, parity, :], bank[4 + parity][:, 0:T], ACT.Silu)\
                      .then_inc(sem(f"{key}_silu"), 1)

                def round_act(s, parity):
                    act.wait_ge(sem(f"{key}_act"), s)
                    nc.scalar.activation(ff_act_hi[:, parity, :], ff_act[:, parity, :], ACT.Copy)\
                      .then_inc(sem(f"{key}_act_hi"), 1)

                if split_out:
                    ff_round_out(key, 3, 0, 16)
                silu(1, 0)
                if split_out:
                    round_act(1, 0)
                    ff_round_out(key, 3, 1, 16)
                with act.Fori(0, FF_LOOPS) as it:
                    for j in range(4):
                        slot = 2 * (j // 2)
                        ff_round(key, slot, j % 2, it * 32 + 32 * (1 + j // 2))
                        silu(it * 4 + j + 2, (j + 1) % 2)
                        if split_out:
                            round_act(it * 4 + j + 2, (j + 1) % 2)
                            ff_round_out(key, slot + 1, j % 2, it * 16 + 16 * (1 + j // 2))
                silu(4 * FF_LOOPS + 2, 1)
                if split_out:
                    round_act(4 * FF_LOOPS + 2, 1)

            norm_squares("ffn1", xT, squares, "fin1_ready", 2, 2)
            ff_round("ffn1", 2, 0, 32)
            norm_root("ffn1", "sum_ffn1", rstd[:, 0:T])
            norm_shift("ffn1", ff_x_hi, ada, 0, hT)
            ff_round("ffn1", 2, 1, 32)
            warm(ACT.Silu)
            feed_forward("ffn1", False)
            warm(ACT.Sqrt)
            norm_squares("mix", xT, squares, "ffn1_sum_read", 1, 1)
            norm_root("mix", "sum_mix", rstd[:, 0:T])
            norm_shift("mix", hT, ada, 24)
            head_squares("lat", latT, squares[:, 0:3, :], "job_emptied", JOB["z_kv"] + 1)
            act.wait_ge(sem("job_emptied"), JOB["lat_sum"] + 1)
            nc.scalar.activation(rstd[:, :], rstd[:, :], ACT.Sqrt, bias=K("eps")).then_inc(sem("lat_root"), 1)
            for gate, job in ((gate_aT, "z_ga3"), (gate_bT, "z_gb3_2")):
                act.wait_ge(sem("job_emptied"), JOB[job] + 1)
                nc.scalar.activation(gate, gate, ACT.Sigmoid).then_inc(sem("gates_ready"), 1)
            warm(ACT.Exp)
            attention("mla")
            attention("ca")
            warm(ACT.Sqrt)
            norm_squares("ffn2", xT, squares, "job_emptied", JOB["out2_0"] + 1, 1)
            ff_round("ffn2", 2, 0, 32)
            norm_root("ffn2", "sum_ffn2", rstd[:, 0:T])
            norm_shift("ffn2", ff_x_hi, ada, 48, hT)
            ff_round("ffn2", 2, 1, 32)
            warm(ACT.Silu)
            feed_forward("ffn2", True)
            warm(ACT.Sqrt)
            norm_squares("last", xT, squares, "ffn2_sum_read", 1, 1)
            norm_root("last", "sum_last", rstd[:, 0:T])

        @block.tensor
        def _(pe):
            ident = K("ident")
            done_jobs = [0]

            def ring_arrived(part, name):
                slot, loads = PLACE[(part, name)]
                pe.wait_ge(sem(f"ring_full{slot}"), 16 * loads)

            def open_job(name):
                j = JOB[name]
                assert j == done_jobs[0], (name, JOBS[done_jobs[0]])
                if j >= 4:
                    pe.wait_ge(sem("job_emptied"), j - 3)
                return bank[j % 4]

            def close_job(last):
                last.then_inc(sem("job_ready"), 1)
                done_jobs[0] += 1

            def product(dst, lhs, rhs, by_chunk=None):
                n = len(lhs)
                for i in range(n):
                    if by_chunk is not None:
                        pe.wait_ge(sem(by_chunk), i + 1)
                    last = pe.matmul(dst, lhsT=lhs[i], rhs=rhs[i], start=(i == 0), stop=(i == n - 1))
                return last

            def turn_job(name, pieces):
                b = open_job(name)
                for i, piece in enumerate(pieces):
                    last = pe.transpose(b[:, i * P:(i + 1) * P], piece, ident)
                close_job(last)

            def sum_job(name, key, src):
                b = open_job(name)
                for k in range(KD):
                    if k % 2 == 0:
                        pe.wait_ge(sem(f"{key}_squares"), k // 2 + 1)
                    last = pe.matmul(b[:, 0:T], lhsT=K("mean"), rhs=src[:, k, :], start=(k == 0), stop=(k == KD - 1))
                close_job(last)

            def row_job(part, name, item, condition):
                b = open_job(name)
                ring_arrived(part, item)
                w = ring_w(part, item)
                for k in range(KD):
                    last = pe.matmul(b[32 * (k % 4):32 * (k % 4) + 32, :], lhsT=condition[:, k, :], rhs=w[:, k, :],
                                     start=(k < 4), stop=(k >= 4))
                close_job(last)

            def turn_row_job(name, u, row_name):
                b = open_job(name)
                pe.wait_ge(sem("job_emptied"), JOB[row_name] + 1)
                for m in range(4):
                    last = pe.matmul(b[:, 2 * m:2 * m + 2], lhsT=mod_acc[:, u, m * P:(m + 1) * P], rhs=K("select"),
                                     start=True, stop=True)
                close_job(last)

            def col_job(name, item):
                b = open_job(name)
                pe.wait_ge(sem("mod_acc_step"), 8 * (item + 1))
                for m in range(4):
                    last = pe.matmul(b[:, m:m + 1], lhsT=mod_acc[:, item % 2, m * P:(m + 1) * P],
                                     rhs=K("ones")[:, 0:1], start=True, stop=True)
                close_job(last)

            def linear_job(name, w, cols, src, by_chunk=None):
                b = open_job(name)
                for i, (lo, n) in enumerate(cols):
                    last = product(b[0:n, i * T:(i + 1) * T], [w[:, k, lo:lo + n] for k in range(w.shape[1])],
                                   [src[:, k, :] for k in range(w.shape[1])], by_chunk if i == 0 else None)
                close_job(last)

            pe.wait_ge(sem("consts_loaded"), 16)
            for name, rows in (("rows_a", rows_a), ("rows_b", rows_b)):
                b = open_job(name)
                pe.wait_ge(sem(f"{name}_loaded"), 16)
                n = rows.shape[0]
                close_job(pe.transpose(b[:, 0:n], rows[:, :], ident[0:n, 0:n]))
            for what, rows in (("x", x_rows), ("ctx", ctx_rows)):
                pe.wait_ge(sem(f"{what}_loaded"), 16)
                for i in range(4):
                    turn_job(f"{what}_turn{i}", [rows[:, b, (2 * i + c) * P:(2 * i + c + 1) * P]
                                                 for c in range(2) for b in range(2)])
            sum_job("sum_x", "n1", squares)
            sum_job("sum_ctx", "c1", ctx_squares)
            pe.wait_ge(sem("cond_ready"), 2)
            for i in range(4):
                row_job("pre", f"modrow{i}", f"mod{i}", cond)
                if i >= 1:
                    turn_row_job(f"mod{i - 1}", (i - 1) % 2, f"modrow{i - 1}")
            turn_row_job("mod3", 1, "modrow3")
            ring_arrived("pre", "w_kv")
            w = ring_w("pre", "w_kv")
            b = open_job("z_k")
            product(b[:, 0:T], [w[:, k, 0:P] for k in range(KD)], [mixT[:, k, :] for k in range(KD)], "c1_ready")
            close_job(product(b[:, T:2 * T], [w[:, k, 0:P] for k in range(KD)], [hT[:, k, :] for k in range(KD)], "n1_ready"))
            b = open_job("z_v")
            for kb in range(4):
                src = mixT if kb < 2 else hT
                last = product(b[:, kb * P:(kb + 1) * P], [src[:, k, (kb % 2) * P:(kb % 2) * P + P] for k in range(KD)],
                               [w[:, k, P:2 * P] for k in range(KD)])
            close_job(last)
            col_job("col_gt1a", 0)
            ring_arrived("pre", "w_q")
            w = ring_w("pre", "w_q")
            for i in range(2):
                b = open_job(f"z_q{i}")
                for c in range(2):
                    for k in range(KD):
                        for a in range(2):
                            head = 2 * i + c + 4 * a
                            last = pe.matmul(b[64 * a:64 * a + 64, c * T:(c + 1) * T], lhsT=w[:, k, 64 * head:64 * head + 64],
                                             rhs=hT[:, k, :], start=(k == 0), stop=(k == KD - 1))
                close_job(last)
            col_job("col_gt1b", 1)
            for item, (name, col) in enumerate((("gb", "col_sh2a"), ("gc", "col_sh2b"), ("u", "col_sc2a"))):
                ring_arrived("pre", f"w_{name}")
                for i in range(2):
                    linear_job(f"z_{name}{i}", ring_w("pre", f"w_{name}"), [(256 * i, P), (256 * i + P, P)], hT)
                col_job(col, 2 + item)
            pe.wait_ge(sem("qk_squares"), 1)
            for i in range(3):
                b = open_job(f"qk_sum{i}")
                close_job(pe.matmul(b[:, :], lhsT=K("heads64"), rhs=squares[:, 2 * i:2 * i + 2, :], start=True, stop=True))
            row_job("pre", "row_sc2b", "sc2b", cond)
            row_job("pre", "row_gt2a", "gt2a", cond)
            turn_row_job("col_sc2b", 0, "row_sc2b")
            turn_row_job("col_gt2a", 1, "row_gt2a")
            pe.wait_ge(sem("qk_ready"), 1)
            for i, chunks in enumerate(((0, 2), (2, 4), (5, 6))):
                b = open_job(f"qk_rot{i}")
                w = (chunks[1] - chunks[0]) * T
                close_job(pe.matmul(b[:, 0:w], lhsT=K("rot_axial"), rhs=qk[:, chunks[0]:chunks[1], :], start=True, stop=True))

            def attention(key):
                _, instances, _ = ATTENTIONS[key]
                n = len(instances)
                job = None
                for i in range(n + 3):
                    if i < n:
                        it = instances[i]
                        if i >= 2:
                            pe.wait_ge(sem(f"{key}_exp"), i - 1)
                        product(bank[4 + i % 2][:, 0:it["keys"]], it["q"], it["k"]).then_inc(sem(f"{key}_scores"), 1)
                    if 2 <= i <= n + 1:
                        j = i - 2
                        pe.wait_ge(sem(f"{key}_probs"), j + 1)
                        if j >= 2:
                            pe.wait_ge(sem(f"{key}_probsT"), j - 1)
                        for b in range(instances[j]["keys"] // P):
                            last = pe.transpose(bank[6 + j % 2][:, b * P:(b + 1) * P], probs[:, j % 2, b * P:(b + 1) * P], ident)
                        last.then_inc(sem(f"{key}_turned"), 1)
                    if i >= 3:
                        j = i - 3
                        it = instances[j]
                        if it["job"] != job:
                            job = it["job"]
                            open_job(job)
                        pe.wait_ge(sem(f"{key}_probsT"), j + 1)
                        nk = it["keys"] // P
                        last = product(job_bank(job)[it["col"]:it["col"] + 64, it["qb"] * P:(it["qb"] + 1) * P], it["v"],
                                       [probsT[:, j % 2, b * P:(b + 1) * P] for b in range(nk)])
                        if it["last"]:
                            close_job(last)

            pe.wait_ge(sem("rope1_ready"), 1)
            attention("at1")
            pe.wait_ge(sem("mg_squares"), 1)
            for i in range(4):
                b = open_job(f"head_sum{i}")
                close_job(pe.matmul(b[:, :], lhsT=K("heads64"), rhs=squares[:, 2 * i:2 * i + 2, :], start=True, stop=True))
            row_job("pre", "row_gt2b", "gt2b", cond)
            turn_row_job("col_gt2b", 0, "row_gt2b")
            for i in range(4):
                if i % 2 == 0:
                    ring_arrived("pre", f"w_out{i // 2}")
                linear_job(f"merge{i}", ring_w("pre", f"w_out{i // 2}"), [(256 * (i % 2), P), (256 * (i % 2) + P, P)], mixT,
                           "mg_ready" if i == 0 else None)
            sum_job("sum_n2", "n2", squares)
            pe.wait_ge(sem("router_loaded"), 32)
            b = open_job("logits")
            for tb in range(2):
                last = product(b[:, 64 * tb:64 * tb + 36], [hT[:, k, tb * P:(tb + 1) * P] for k in range(KD)],
                               [router[:, k, :] for k in range(KD)], "n2_ready" if tb == 0 else None)
            close_job(last)
            for i in range(4):
                turn_job(f"h2_turn{i}", [hT[:, 4 * (i % 2) + c, (i // 2) * P:(i // 2 + 1) * P] for c in range(4)])
            b = open_job("positions")
            pe.wait_ge(sem("assigned"), 2)
            a0, a1 = assigned[:, 0, :], assigned[:, 1, :]
            product(b[:, 0:32], [K("before")], [a0])
            product(b[:, 32:64], [K("ones"), K("before")], [a0, a1])
            close_job(product(b[:, 64:96], [K("ones"), K("ones")], [a0, a1]))
            b = open_job("bias_turn")
            pe.wait_ge(sem("rel_bias_loaded"), 64)
            for i in range(4):
                last = pe.matmul(b[0:8, i * P:(i + 1) * P], lhsT=rel_bias_rows[:, i, :], rhs=K("reverse"),
                                 start=True, stop=True)
            close_job(last)

            pe.wait_ge(sem("job_emptied"), done_jobs[0])
            pe.wait_ge(sem("zeros_ready"), 1)
            for i in range(4):
                pe.matmul(bank[i][:, :], lhsT=zeros[:, 0:P], rhs=zeros[:, :], start=True, stop=False, skip_group_check=True)

            def prepare(count, selected):
                pe.wait_ge(sem("selected"), count)
                if selected is not None:
                    pe.wait_ge(sem("pick_wT_ready"), selected)
                for k in range(KD):
                    for tb in range(2):
                        pe.matmul(bank[4][:, k * SLOTS:(k + 1) * SLOTS], lhsT=h_rows[:, tb, k * P:(k + 1) * P],
                                  rhs=pick[:, tb, :], start=(tb == 0), stop=(tb == 1))
                for tb in range(2):
                    last = pe.transpose(bank[7][:, tb * P:(tb + 1) * P], pick_w[:, tb, :], ident)
                last.then_inc(sem("gathered"), 1)

            def combine(u):
                for c in range(4):
                    for half in range(2):
                        m = 4 * half + c
                        pe.matmul(bank[m // 2][:, (m % 2) * T:(m % 2 + 1) * T],
                                  lhsT=y_e[64 * half:64 * half + 64, c * P:(c + 1) * P],
                                  rhs=pick_wT[64 * half:64 * half + 64, u, :],
                                  start=False, stop=False, skip_group_check=True)

            def expert(u, n, prep, arrivals):
                gate, up, down = expert_w(u)
                pe.wait_ge(sem("xe_ready"), prep - 1)
                pe.wait_ge(sem(f"gate_full{u}"), arrivals)
                for w, b in ((gate, bank[4]), (up, bank[5])):
                    if b is bank[5]:
                        pe.wait_ge(sem(f"up_full{u}"), arrivals)
                    for k in range(KD):
                        for half in range(2):
                            last = pe.matmul(b[64 * half:64 * half + 64, 0:HALF_E], lhsT=xeT[:, k, :],
                                             rhs=w[:, k, half * HALF_E:(half + 1) * HALF_E],
                                             start=(k == 0), stop=(k == KD - 1))
                last.then_inc(sem("gate_up_done"), 1)
                pe.wait_ge(sem("y_ready"), n)
                combine(1 - u)
                pe.wait_ge(sem("hidden_ready"), n)
                for c in range(3):
                    last = pe.transpose(bank[5][:, c * P:(c + 1) * P], hidden[:, c * P:(c + 1) * P], ident)
                last.then_inc(sem("hidden_turned"), 1)
                prepare(prep, prep - 1)
                pe.wait_ge(sem("hiddenT_ready"), n)
                pe.wait_ge(sem(f"down_full{u}"), arrivals)
                for f in range(6):
                    for half in range(2):
                        last = pe.matmul(bank[6][64 * half:64 * half + 64, :],
                                         lhsT=hiddenT[:, f % 3, 64 * (f // 3):64 * (f // 3) + 64],
                                         rhs=down[:, f, half * 512:(half + 1) * 512], start=(f == 0), stop=(f == 5))
                last.then_inc(sem("down_done"), 1)

            prepare(1, None)
            with pe.Fori(0, N_EXPERTS // 2) as it:
                for u in range(2):
                    expert(u, it * 2 + u + 1, it * 2 + u + 2, it * 16 + 16)
            pe.wait_ge(sem("busiest_ready"), 1)
            most = pe.value_load(busiest[0:1, 0:1], min_val=0, max_val=T)
            with pe.If(most > SLOTS):
                with pe.Fori(1, PASSES) as ps:
                    pe.wait_ge(sem("xe_ready"), ps * (N_EXPERTS + 1))
                    prepare(ps * (N_EXPERTS + 1) + 1, ps * (N_EXPERTS + 1))
                    with pe.Fori(0, N_EXPERTS // 2) as it:
                        for u in range(2):
                            expert(u, ps * N_EXPERTS + it * 2 + u + 1, ps * (N_EXPERTS + 1) + it * 2 + u + 2,
                                   ps * (8 * N_EXPERTS) + it * 16 + 16)
                pe.wait_ge(sem("y_ready"), PASSES * N_EXPERTS + 1)
            pe.wait_ge(sem("y_ready"), N_EXPERTS + 1)
            combine(1)
            for i in range(4):
                last = pe.matmul(bank[i][:, :], lhsT=zeros[:, 0:P], rhs=zeros[:, :], start=False, stop=True, skip_group_check=True)
            last.then_inc(sem("experts_done"), 1)

            pe.wait_ge(sem("y_moe_read"), 4)
            pe.wait_ge(sem("cond_ready"), 4)
            row_job("ada", "row_ada0", "ada0", cond_ada)
            sum_job("sum_final", "fin1", squares)
            for i in range(1, 4):
                row_job("ada", f"row_ada{i}", f"ada{i}", cond_ada)
                turn_row_job(f"col_ada{i - 1}", (i - 1) % 2, f"row_ada{i - 1}")
            turn_row_job("col_ada3", 1, "row_ada3")

            def feed_forward(key, ada_items):
                pe.wait_ge(sem("job_emptied"), done_jobs[0])

                def gate_up(s, slot, half, parity, act_read, first=False):
                    w_hi, w_lo = ff_half(ff_w_hi[slot], half), ff_half(ff_w_lo[slot], half)
                    pe.wait_ge(sem(f"{key}_w_lo"), s)
                    if act_read is not None:
                        pe.wait_ge(sem(f"{key}_act"), act_read)
                    for g in range(2):
                        for n, (w, x) in enumerate(((w_hi, "ready"), (w_lo, "ready"), (w_hi, "x_lo"))):
                            for k in range(KD):
                                if first and g == 0 and n != 1:
                                    pe.wait_ge(sem(f"{key}_{x}"), k + 1)
                                last = pe.matmul(bank[4 + parity][:, g * T:(g + 1) * T], lhsT=w[:, k, g, :],
                                                 rhs=(ff_x_hi if x == "ready" else ff_x_lo)[:, k, :],
                                                 start=(n == 0 and k == 0), stop=(n == 2 and k == KD - 1))
                    last.then_inc(sem(f"{key}_gate_up_done"), 1)

                def down(s, slot, half, parity, arrivals, first=False):
                    if ada_items:
                        if half == 0:
                            pe.wait_ge(sem(f"{key}_out_full{slot}"), arrivals)
                        pe.wait_ge(sem(f"{key}_act"), s)
                        parts = (({slot: ring(slot)[:, 0:2 * D]}, ff_act),)
                    else:
                        pe.wait_ge(sem(f"{key}_out_lo"), s)
                        parts = ((ff_out_hi, ff_act_hi), (ff_out_lo, ff_act_hi), (ff_out_hi, ff_act_lo))
                    for n, (w, x) in enumerate(parts):
                        if n == 0 and not ada_items:
                            pe.wait_ge(sem(f"{key}_act_hi"), s)
                        elif n == 2:
                            pe.wait_ge(sem(f"{key}_act_lo"), s)
                        for m in range(KD):
                            last = pe.matmul(bank[m // 2][:, (m % 2) * T:(m % 2 + 1) * T],
                                             lhsT=w[slot][:, half * D + m * P:half * D + (m + 1) * P],
                                             rhs=x[:, parity, :], start=(first and n == 0 and m % 2 == 0), stop=False,
                                             skip_group_check=True)
                    last.then_inc(sem(f"{key}_down_done"), 1)
                    return last

                def ada_columns(it, u):
                    pe.wait_ge(sem("mod_acc_step"), it * 16 + 8 * (5 + u + 1))
                    for m in range(4):
                        last = pe.matmul(bank[6 + u][:, m:m + 1], lhsT=mod_acc[:, u, m * P:(m + 1) * P],
                                         rhs=K("ones")[:, 0:1], start=True, stop=True)
                    last.then_inc(sem("ada_col_ready"), 1)

                gate_up(1, 2, 0, 0, None, first=True)
                gate_up(2, 2, 1, 1, None)
                down(1, 3, 0, 0, 16, first=True)
                with pe.Fori(0, FF_LOOPS) as it:
                    for j in range(4):
                        s = it * 4 + j + 3
                        slot = 2 * (j // 2)
                        if j == 0:
                            gate_up(s, 0, 0, 0, s - 2)
                            down(s - 1, 3, 1, 1, None)
                        elif j == 1:
                            gate_up(s, 0, 1, 1, s - 2)
                            if ada_items:
                                ada_columns(it, 0)
                            down(s - 1, 1, 0, 0, it * 16 + 16)
                        elif j == 2:
                            gate_up(s, 2, 0, 0, s - 2)
                            down(s - 1, 1, 1, 1, None)
                        else:
                            gate_up(s, 2, 1, 1, s - 2)
                            if ada_items:
                                ada_columns(it, 1)
                            down(s - 1, 3, 0, 0, it * 16 + 32)
                down(4 * FF_LOOPS + 2, 3, 1, 1, None)
                for i in range(4):
                    last = pe.matmul(bank[i][:, :], lhsT=zeros[:, 0:P], rhs=zeros[:, :], start=False, stop=True,
                                     skip_group_check=True)
                last.then_inc(sem(f"{key}_sum_done"), 1)
                pe.wait_ge(sem(f"{key}_sum_read"), 4)

            sum_job("sum_ffn1", "ffn1", squares)
            feed_forward("ffn1", True)
            sum_job("sum_mix", "mix", squares)
            ring_arrived("mid", "w2_lat")
            w = ring_w("mid", "w2_lat")
            linear_job("z_lat", w, [(0, P), (P, P)], hT, "mix_ready")
            linear_job("z_kv", w, [(256, P), (320, 96)], hT)
            for name, col, item in (("caq", "col_ada14", 15), ("cak", "col_ada15", 16)):
                ring_arrived("mid", f"w2_{name}")
                for i in range(2):
                    linear_job(f"z_{name}{i}", ring_w("mid", f"w2_{name}"), [(256 * i, P), (256 * i + P, P)], hT)
                col_job(col, item)
            ring_arrived("mid", "w2_cav")
            w = ring_w("mid", "w2_cav")
            for tb in range(2):
                b = open_job(f"z_cav{tb}")
                close_job(product(b[:, :], [hT[:, k, tb * P:(tb + 1) * P] for k in range(KD)], [w[:, k, :] for k in range(KD)]))
            b = open_job("lat_sum")
            pe.wait_ge(sem("lat_squares"), 1)
            product(b[:, 0:T], [K("ones")] * 2, [squares[:, 0, :], squares[:, 1, :]])
            close_job(product(b[:, T:2 * T], [K("ones")], [squares[:, 2, :]]))
            col_job("col_ada16", 17)
            def gate_job(gate, i):
                name = f"w2_{gate}{i // 2}"
                if i % 2 == 0:
                    ring_arrived("mid", name)
                linear_job(f"z_{gate}{i}" + ("_2" if gate == "gb" else ""), ring_w("mid", name),
                           [(256 * (i % 2), P), (256 * (i % 2) + P, P)], hT)

            for i in range(4):
                gate_job("ga", i)
            col_job("col_ada17", 18)
            pe.wait_ge(sem("w_uq_full"), 16)
            pe.wait_ge(sem("w_ukv_full"), 16)
            pe.wait_ge(sem("lat_ready"), 1)
            both = ring(PLACE[("mid", "mla_up")][0])
            uq = both[:, 0:1536].rearrange("p (k n) -> p k n", k=2)
            ukv = both[:, 1536:2560].rearrange("p (k h n) -> p k h n", k=1, h=8)
            for i in range(4):
                linear_job(f"mla_q{i}", uq, [(192 * i, 96), (192 * i + 96, 96)], latT)
            for i in range(4):
                linear_job(f"mla_k{i}", both[:, 1536:2560].rearrange("p (k n) -> p k n", k=1),
                           [(256 * i, 64), (256 * i + P, 64)], latT[:, 2:3, :])
            for tb in range(2):
                b = open_job(f"mla_v{tb}")
                close_job(product(b[:, :], [latT[:, 2, tb * P:(tb + 1) * P]], [ukv[:, 0, :, 64:128]]))
            gate_job("gb", 0)
            gate_job("gb", 1)
            pe.wait_ge(sem("job_emptied"), JOB["mla_q3"] + 1)
            for i in range(4):
                b = open_job(f"pe_rot{i}")
                close_job(pe.matmul(b[0:96, :], lhsT=K("rot_half")[0:96, 0:96], rhs=mla_q[0:96, 2 * i:2 * i + 2, :],
                                    start=True, stop=True))
            b = open_job("kpe_rot")
            close_job(pe.matmul(b[0:96, 0:T], lhsT=K("rot_half")[0:96, 0:96], rhs=squares[0:96, 3, :], start=True, stop=True))
            gate_job("gb", 2)
            gate_job("gb", 3)
            pe.wait_ge(sem("mla_ready"), 1)
            attention("mla")
            pe.wait_ge(sem("bias_loaded"), 32)
            attention("ca")
            ring_arrived("mid", "w_branch_a")
            ring_arrived("mid", "w_branch_b")
            pe.wait_ge(sem("job_emptied"), done_jobs[0])
            for i in range(4):
                for ab, at in (("a", 0), ("b", 4)):
                    w = ring(PLACE[("mid", f"w_branch_{ab}")][0]).rearrange("p (k n) -> p k n", k=4)
                    linear_job(f"branch_{ab}{i}", w, [(256 * i, P), (256 * i + P, P)], squares[:, at:at + 4, :])
            pe.wait_ge(sem("merged_ready"), 4)
            for i in range(4):
                if i % 2 == 0:
                    ring_arrived("mid", f"w_out2_{i // 2}")
                linear_job(f"out2_{i}", ring_w("mid", f"w_out2_{i // 2}"), [(256 * (i % 2), P), (256 * (i % 2) + P, P)], hT)
            sum_job("sum_ffn2", "ffn2", squares)
            feed_forward("ffn2", False)
            sum_job("sum_last", "last", squares)
            for i in range(4):
                pe.wait_ge(sem("last_ready"), 4 * min(i, 1) + 4)
                turn_job(f"y_turn{i}", [xT[:, 4 * (i % 2) + c, (i // 2) * P:(i // 2 + 1) * P] for c in range(4)])
            assert done_jobs[0] == len(JOBS)

        @block.vector
        def _(dve):
            n_step, emptied, n_item = [0], [0], [0]

            def step(instruction):
                n_step[0] += 1
                instruction.then_inc(sem("dve_step"), 1)
                dve.wait_ge(sem("dve_step"), n_step[0])

            def ring_arrived(part, name):
                slot, loads = PLACE[(part, name)]
                dve.wait_ge(sem(f"ring_full{slot}"), 16 * loads)

            def take_job(name):
                assert JOB[name] == emptied[0], (name, JOBS[emptied[0]])
                dve.wait_ge(sem("job_ready"), JOB[name] + 1)
                return job_bank(name)

            def empty_job(instruction):
                instruction.then_inc(sem("job_emptied"), 1)
                emptied[0] += 1

            def job_done_here():
                dve.wait_ge(sem("job_emptied"), emptied[0])

            def mod_item(w, scalars, u, first):
                for k in range(KD):
                    if k == 0:
                        i = nc.vector.tensor_scalar(mod_acc[:, u, :], w[:, k, :], scalars[k], None, ALU.mult)
                    else:
                        dve.wait_ge(sem("mod_acc_step"), first + k)
                        i = nc.vector.scalar_tensor_tensor(out=mod_acc[:, u, :], in0=w[:, k, :], scalar=scalars[k],
                                                           in1=mod_acc[:, u, :], op0=ALU.mult, op1=ALU.add)
                    i.then_inc(sem("mod_acc_step"), 1)

            cond_1 = [cond[:, k, 0:1] for k in range(KD)]
            cond_2 = [cond2[:, k:k + 1] for k in range(KD)]

            def item(part, name):
                n = n_item[0]
                n_item[0] += 1
                ring_arrived(part, name)
                mod_item(ring_w(part, name), cond_1 if part == "pre" else cond_2, n % 2, 8 * n)

            def col_job(name, dst, bias):
                b = take_job(name)
                empty_job(nc.vector.tensor_tensor(dst, b[:, 0:4], bias, ALU.add))

            def mod_col(name, n):
                col_job(name, mod[:, 16 + 4 * n:20 + 4 * n], cols_a[:, 16 + 4 * n:20 + 4 * n])

            def ada_col(name, n):
                col_job(name, ada[:, 4 * n:4 * n + 4], cols_b[:, 4 * n:4 * n + 4])

            def make_gain(key, g, scale):
                s = SET[key]
                step(nc.vector.scalar_tensor_tensor(out=gains[:, s * KD:(s + 1) * KD], in0=scale, scalar=1.0, in1=g,
                                                    op0=ALU.add, op1=ALU.mult))

            def norm_root(key, job, stat):
                take_job(job)
                dve.wait_ge(sem(f"{key}_root"), 1)
                empty_job(nc.vector.reciprocal(stat, stat))
                job_done_here()

            def norm_scale(key, src, dst, stat):
                for k in range(KD):
                    nc.vector.scalar_tensor_tensor(out=dst[:, k, :], in0=src[:, k, :], scalar=gain(key, k), in1=stat,
                                                   op0=ALU.mult, op1=ALU.mult).then_inc(sem(f"{key}_scaled"), 1)

            def norm_gain(key, name, col, stat):
                for k in range(KD):
                    nc.vector.scalar_tensor_tensor(out=xT[:, k, :], in0=xT[:, k, :], scalar=col(name, k), in1=stat,
                                                   op0=ALU.mult, op1=ALU.mult).then_inc(sem(f"{key}_ready"), 1)

            def copy_rows(job, u):
                take_job(job)
                empty_job(nc.vector.tensor_copy(mod_acc[:, u, :], job_bank(job)[:, :]))

            def row_col(name, dst, bias):
                b = take_job(name)[:, 0:8].rearrange("p (m c) -> p m c", c=2)
                empty_job(nc.vector.tensor_tensor(dst, b[:, :, 0], bias, ALU.add))

            nc.vector.memset(zeros[:, :], 0.0).then_inc(sem("zeros_ready"), 1)
            nc.vector.memset(cond[:, :, :], 0.0)
            nc.vector.memset(cond_ada[:, :, :], 0.0).then_inc(sem("cond_zeroed"), 1)
            for c in (0, T + 1):
                nc.vector.memset(conv_in[:, :, c:c + 1], 0.0)
            nc.vector.memset(weights[:, :, 32:33], 0.0)
            step(nc.vector.memset(places[:, :, 32:33], -1.0))
            for name, cols in (("rows_a", cols_a), ("rows_b", cols_b)):
                b = take_job(name)
                empty_job(nc.vector.tensor_copy(cols[:, :], b[:, 0:cols.shape[1]]))
            for what, dst in (("x", xT[:, :, :]), ("ctx", ctxT)):
                for i in range(4):
                    take_job(f"{what}_turn{i}")
                    empty_job(nc.vector.tensor_copy(dst[:, 2 * i:2 * i + 2, :], job_wide(f"{what}_turn{i}")))
            norm_root("n1", "sum_x", rstd[:, 0:T])
            norm_root("c1", "sum_ctx", rstd[:, T:2 * T])
            copy_rows("modrow0", 0)
            for i in range(4):
                if i < 3:
                    copy_rows(f"modrow{i + 1}", (i + 1) % 2)
                b = take_job(f"mod{i}")[:, 0:8].rearrange("p (m c) -> p m c", c=2)
                bias = cols_a[:, 4 * i:4 * i + 4]
                nc.vector.tensor_tensor(mod[:, 4 * i:4 * i + 4], b[:, :, 0], bias, ALU.add)
                empty_job(nc.vector.tensor_tensor(mod_ctx[:, 4 * i:4 * i + 4], b[:, :, 1], bias, ALU.add))
            job_done_here()
            g1 = cols_a[:, 48:56]
            make_gain("n1", g1, mod[:, 8:16])
            make_gain("c1", g1, mod_ctx[:, 8:16])
            norm_scale("c1", ctxT, mixT, rstd[:, T:2 * T])
            norm_scale("n1", xT, hT, rstd[:, 0:T])

            dve.wait_ge(sem("positions_loaded"), 16)
            dve.wait_ge(sem("consts_loaded"), 16)
            pos, near, arg, arg_cos, wrap = (angle[64:96, i, :] for i in range(5))
            step(nc.vector.tensor_copy(pos, turns[64:96, :]))
            step(nc.vector.tensor_scalar(pos, pos, K("inv_freq")[64:96, :], None, ALU.mult))
            step(nc.vector.tensor_scalar(turns[64:96, :], pos, 1.0 / TWO_PI, None, ALU.mult))
            step(nc.vector.tensor_copy(near, turns[64:96, :]))
            for i, part in enumerate((PI_A, PI_B, PI_C)):
                step(nc.vector.scalar_tensor_tensor(out=arg, in0=near, scalar=-part, in1=pos if i == 0 else arg,
                                                    op0=ALU.mult, op1=ALU.add))
            step(nc.vector.tensor_scalar(arg_cos, arg, TWO_PI / 4, None, ALU.add))
            for a in (arg, arg_cos):
                for op, turn in ((ALU.is_gt, -TWO_PI), (ALU.is_lt, TWO_PI)):
                    limit = TWO_PI / 2 if turn < 0 else -TWO_PI / 2
                    step(nc.vector.tensor_scalar(wrap, a, limit, turn, op, ALU.mult))
                    step(nc.vector.tensor_tensor(a, a, wrap, ALU.add))
                i = nc.vector.tensor_scalar(a, a, 3.1415925, -3.1415925, ALU.min, ALU.max)
            i.then_inc(sem("angles_ready"), 1)


            item("pre", "gt1a")
            take_job("z_k")
            empty_job(nc.vector.tensor_copy(qk[:, 4:6, :], job_wide("z_k")))
            take_job("z_v")
            empty_job(nc.vector.tensor_copy(v1, job_bank("z_v")[:, :].rearrange("p (b n) -> p b n", b=4)))
            mod_col("col_gt1a", 0)
            item("pre", "gt1b")
            for i in range(2):
                take_job(f"z_q{i}")
                empty_job(nc.vector.tensor_copy(qk[:, 2 * i:2 * i + 2, :], job_wide(f"z_q{i}")))
            mod_col("col_gt1b", 1)
            item("pre", "sh2a")
            for i in range(2):
                take_job(f"z_gb{i}")
                empty_job(nc.vector.tensor_copy(gate_b[:, 2 * i:2 * i + 2, :], job_wide(f"z_gb{i}")))
            mod_col("col_sh2a", 2)
            item("pre", "sh2b")
            for i in range(2):
                take_job(f"z_gc{i}")
                empty_job(nc.vector.tensor_copy(conv_out[:, 2 * i:2 * i + 2, :], job_wide(f"z_gc{i}")))
            mod_col("col_sh2b", 3)
            item("pre", "sc2a")
            for i in range(2):
                take_job(f"z_u{i}")
                empty_job(nc.vector.tensor_tensor(conv_in[:, 2 * i:2 * i + 2, 1:T + 1], job_wide(f"z_u{i}"),
                                                  conv_out[:, 2 * i:2 * i + 2, :], ALU.mult))
            col_job("col_sc2a", mod[:, 32:36], cols_a[:, 32:36])
            for i in range(3):
                take_job(f"qk_sum{i}")
                dve.wait_ge(sem("qk_root"), i + 1)
                tmp = qk_tmp[:, 2 * i:2 * i + 2, :]
                empty_job(nc.vector.reciprocal(tmp, tmp))
            copy_rows("row_sc2b", 0)
            copy_rows("row_gt2a", 1)
            job_done_here()
            for lo, hi, name in ((0, 4, "q_norm_g"), (4, 6, "k_norm_g")):
                i = nc.vector.scalar_tensor_tensor(out=qk[:, lo:hi, :], in0=qk[:, lo:hi, :], scalar=col_a(name),
                                                   in1=qk_tmp[:, lo:hi, :], op0=ALU.mult, op1=ALU.mult)
            i.then_inc(sem("qk_ready"), 1)
            dve.wait_ge(sem("qk_ready"), 1)
            row_col("col_sc2b", mod[:, 36:40], cols_a[:, 36:40])
            row_col("col_gt2a", mod[:, 40:44], cols_a[:, 40:44])

            def tables(cos, sin, n):
                return [t.rearrange("p (a t) -> p a t", a=1).broadcast_to((t.shape[0], n, T)) for t in (cos, sin)]

            for i, (lo, hi) in enumerate(((0, 2), (2, 4), (5, 6))):
                b = take_job(f"qk_rot{i}")[:, 0:(hi - lo) * T].rearrange("p (a t) -> p a t", t=T)
                cos, sin = tables(K("axial_cos"), K("axial_sin"), hi - lo)
                empty_job(nc.vector.tensor_tensor(qk_tmp[:, lo:hi, :], b, sin, ALU.mult))
                step(nc.vector.tensor_tensor(qk[:, lo:hi, :], qk[:, lo:hi, :], cos, ALU.mult))
                i = nc.vector.tensor_tensor(qk[:, lo:hi, :], qk[:, lo:hi, :], qk_tmp[:, lo:hi, :], ALU.add)
            i.then_inc(sem("rope1_ready"), 1)

            def attention(key):
                index, instances, scale = ATTENTIONS[key]
                n = len(instances)
                for i in range(n + 4):
                    if i < n:
                        w = instances[i]["keys"]
                        scores = bank[4 + i % 2]
                        dve.wait_ge(sem(f"{key}_scores"), i + 1)
                        if instances[i]["mask"]:
                            late = scores[0:64, w - 64:w]
                            step(nc.vector.tensor_scalar(late, late, NEG, None, ALU.add))
                        step(nc.vector.reduce_max(stats[:, index, 2, i:i + 1], scores[:, 0:w], AX_X))
                        nc.vector.tensor_scalar(stats[:, index, 0, i:i + 1], stats[:, index, 2, i:i + 1], -scale, None,
                                                ALU.mult).then_inc(sem(f"{key}_negmax"), 1)
                    if 1 <= i <= n:
                        j = i - 1
                        w = instances[j]["keys"]
                        dve.wait_ge(sem(f"{key}_exp"), j + 1)
                        step(nc.vector.reciprocal(stats[:, index, 2, j:j + 1], stats[:, index, 1, j:j + 1]))
                        nc.vector.tensor_scalar(probs[:, j % 2, 0:w], probs[:, j % 2, 0:w], stats[:, index, 2, j:j + 1],
                                                None, ALU.mult).then_inc(sem(f"{key}_probs"), 1)
                    if i >= 4 and instances[i - 4]["last"]:
                        job = instances[i - 4]["job"]
                        take_job(job)
                        empty_job(nc.vector.tensor_copy(ATT_OUT[key](int(job[-1])), job_bank(job)[:, 0:T]))

            attention("at1")
            mg = h_rows[:, :, :].rearrange("p b (k t) -> p (b k) t", t=T)
            for i in range(4):
                take_job(f"head_sum{i}")
                dve.wait_ge(sem("mg_root"), i + 1)
                empty_job(nc.vector.reciprocal(mg[:, 2 * i:2 * i + 2, :], mg[:, 2 * i:2 * i + 2, :]))
            copy_rows("row_gt2b", 0)
            job_done_here()
            for k in range(KD):
                nc.vector.scalar_tensor_tensor(out=mixT[:, k, :], in0=mixT[:, k, :],
                                               scalar=cols_a[:, ROWS_A["attn_out_g"] + k:ROWS_A["attn_out_g"] + k + 1],
                                               in1=mg[:, k, :], op0=ALU.mult, op1=ALU.mult).then_inc(sem("mg_ready"), 1)
            row_col("col_gt2b", mod[:, 44:48], cols_a[:, 44:48])
            job_done_here()

            def residual_job(name, i, gate, at):
                take_job(name)
                for c in range(2):
                    k = 2 * i + c
                    ins_ = nc.vector.scalar_tensor_tensor(out=xT[:, k, :], in0=job_wide(name)[:, c, :],
                                                          scalar=gate[:, at + k:at + k + 1], in1=xT[:, k, :],
                                                          op0=ALU.mult, op1=ALU.add)
                empty_job(ins_)

            for i in range(4):
                residual_job(f"merge{i}", i, mod, 16)
            make_gain("n2", cols_a[:, 56:64], mod[:, 32:40])
            norm_root("n2", "sum_n2", rstd[:, 0:T])
            norm_scale("n2", xT, hT, rstd[:, 0:T])

            b = take_job("logits")
            for tb in range(2):
                i = nc.vector.tensor_copy(logits[:, tb, :], b[:, 64 * tb:64 * tb + 36])
            empty_job(i)
            job_done_here()

            def both(operation):
                operation(0)
                step(operation(1))

            both(lambda tb: nc.vector.reduce_max(picked[:, tb, 28:29], logits[:, tb, 0:4], AX_X))
            for tb in range(2):
                nc.vector.tensor_scalar(picked[:, tb, 0:1], picked[:, tb, 28:29], -1.0, None, ALU.mult)\
                  .then_inc(sem("router_max"), 1)
            both(lambda tb: nc.vector.scalar_tensor_tensor(out=picked[:, tb, 24:28], in0=logits[:, tb, 0:4],
                                                           scalar=picked[:, tb, 28:29], in1=K("group_rank"),
                                                           op0=ALU.is_equal, op1=ALU.mult))
            both(lambda tb: nc.vector.reduce_max(picked[:, tb, 29:30], picked[:, tb, 24:28], AX_X))
            both(lambda tb: nc.vector.tensor_scalar(picked[:, tb, 24:28], picked[:, tb, 24:28], picked[:, tb, 29:30], None,
                                                    ALU.is_equal))
            both(lambda tb: nc.vector.tensor_scalar(picked[:, tb, 30:31], picked[:, tb, 29:30], -float(GROUP_SIZE),
                                                    float(GROUP_SIZE * N_GROUPS), ALU.mult, ALU.add))
            both(lambda tb: nc.vector.tensor_scalar(picked[:, tb, 8:16], logits[:, tb, 4:12], picked[:, tb, 24:25], None,
                                                    ALU.mult))
            for g in range(1, N_GROUPS):
                both(lambda tb: nc.vector.scalar_tensor_tensor(out=picked[:, tb, 8:16], in0=logits[:, tb, 4 + 8 * g:12 + 8 * g],
                                                               scalar=picked[:, tb, 24 + g:25 + g], in1=picked[:, tb, 8:16],
                                                               op0=ALU.mult, op1=ALU.add))
            both(lambda tb: nc.vector.max(out=picked[:, tb, 16:24], in_=picked[:, tb, 8:16]))
            both(lambda tb: nc.vector.max_index(out=picked_i[:, tb, :], in_max=picked[:, tb, 16:24],
                                                in_values=picked[:, tb, 8:16]))
            both(lambda tb: nc.vector.tensor_copy(picked[:, tb, 31:33], picked_i[:, tb, 0:2]))
            both(lambda tb: nc.vector.tensor_scalar(picked[:, tb, 31:33], picked[:, tb, 31:33], picked[:, tb, 30:31], None,
                                                    ALU.add))
            for tb in range(2):
                nc.vector.tensor_scalar(picked[:, tb, 3:4], picked[:, tb, 16:17], -1.0, None, ALU.mult)\
                  .then_inc(sem("router_top"), 1)
            both(lambda tb: nc.vector.tensor_scalar(route_tmp[:, tb, :], K("expert_id"), picked[:, tb, 31:32], None,
                                                    ALU.is_equal))
            for tb in range(2):
                nc.vector.scalar_tensor_tensor(out=assigned[:, tb, :], in0=K("expert_id"), scalar=picked[:, tb, 32:33],
                                               in1=route_tmp[:, tb, :], op0=ALU.is_equal, op1=ALU.add)\
                  .then_inc(sem("assigned"), 1)
            for i in range(4):
                take_job(f"h2_turn{i}")
                empty_job(nc.vector.tensor_copy(h_rows[:, i // 2, 512 * (i % 2):512 * (i % 2) + 512], job_bank(f"h2_turn{i}")[:, :]))
            dve.wait_ge(sem("group_exp"), 2)
            dve.wait_ge(sem("second_exp"), 2)
            both(lambda tb: nc.vector.tensor_scalar(picked[:, tb, 33:34], picked[:, tb, 2:3], 1.0, None, ALU.add))
            both(lambda tb: nc.vector.tensor_tensor(picked[:, tb, 33:34], picked[:, tb, 33:34], picked[:, tb, 1:2], ALU.mult))
            both(lambda tb: nc.vector.reciprocal(picked[:, tb, 34:35], picked[:, tb, 33:34]))
            both(lambda tb: nc.vector.tensor_tensor(picked[:, tb, 35:36], picked[:, tb, 34:35], picked[:, tb, 2:3], ALU.mult))
            dve.wait_ge(sem("assigned"), 2)
            both(lambda tb: nc.vector.tensor_scalar(weights[:, tb, 0:32], K("expert_id"), picked[:, tb, 31:32],
                                                    picked[:, tb, 34:35], ALU.is_equal, ALU.mult))
            both(lambda tb: nc.vector.tensor_scalar(route_tmp[:, tb, :], K("expert_id"), picked[:, tb, 32:33],
                                                    picked[:, tb, 35:36], ALU.is_equal, ALU.mult))
            both(lambda tb: nc.vector.tensor_tensor(weights[:, tb, 0:32], weights[:, tb, 0:32], route_tmp[:, tb, :], ALU.add))
            b = take_job("positions")
            both(lambda tb: nc.vector.tensor_scalar(route_tmp[:, tb, :], assigned[:, tb, :], -NO_SLOT, NO_SLOT, ALU.mult,
                                                    ALU.add))
            both(lambda tb: nc.vector.tensor_tensor(places[:, tb, 0:32], b[:, 32 * tb:32 * tb + 32], route_tmp[:, tb, :],
                                                    ALU.add))
            empty_job(nc.vector.reduce_max(picked[0:1, 0, 37:38], b[0:1, 64:96], AX_X))
            job_done_here()
            nc.vector.tensor_copy(busiest[0:1, 0:1], picked[0:1, 0, 37:38]).then_inc(sem("busiest_ready"), 1)
            take_job("bias_turn")
            empty_job(nc.vector.tensor_copy(bias_rows, job_bank("bias_turn")[0:8, :]))
            job_done_here()

            def select(e, count, gathered):
                if gathered is not None:
                    dve.wait_ge(sem("gathered"), gathered)
                for tb in range(2):
                    place = places[:, tb, bass.ds(e, 1)]
                    nc.vector.tensor_scalar(pick[:, tb, :], K("slot")[:, 0:SLOTS], place, None, ALU.is_equal)
                    i = nc.vector.tensor_scalar(pick_w[:, tb, :], K("slot"), place, weights[:, tb, bass.ds(e, 1)],
                                                ALU.is_equal, ALU.mult)
                i.then_inc(sem("selected"), 1)

            def take_turned(u, count):
                dve.wait_ge(sem("gathered"), count)
                nc.vector.tensor_copy(pick_wT[:, u, :], bank[7][:, 0:T]).then_inc(sem("pick_wT_ready"), 1)

            def expert(u, e, n, prep):
                select(e + 1, prep, prep - 1)
                dve.wait_ge(sem("gate_act_ready"), n)
                nc.vector.tensor_tensor(hidden, gate_act, bank[5][:, 0:HALF_E], ALU.mult).then_inc(sem("hidden_ready"), 1)
                take_turned(1 - u, prep)

            nc.vector.memset(pick_wT[:, 1, :], 0.0)
            nc.vector.memset(y_e, 0.0).then_inc(sem("y_ready"), 1)
            select(0, 1, None)
            take_turned(0, 1)
            with dve.Fori(0, N_EXPERTS // 2) as it:
                for u in range(2):
                    expert(u, it * 2 + u, it * 2 + u + 1, it * 2 + u + 2)
            most = dve.value_load(busiest[0:1, 0:1], min_val=0, max_val=T)
            with dve.If(most > SLOTS):
                with dve.Fori(1, PASSES) as ps:
                    nc.vector.tensor_scalar(places, places, -float(SLOTS), None, ALU.add).then_inc(sem("places_moved"), 1)
                    dve.wait_ge(sem("places_moved"), ps)
                    select(0, None, ps * (N_EXPERTS + 1))
                    take_turned(0, ps * (N_EXPERTS + 1) + 1)
                    with dve.Fori(0, N_EXPERTS // 2) as it:
                        for u in range(2):
                            expert(u, it * 2 + u, ps * N_EXPERTS + it * 2 + u + 1, ps * (N_EXPERTS + 1) + it * 2 + u + 2)

            def residual_sum(done, read, gate, at):
                dve.wait_ge(sem(done), 1)
                for k in range(KD):
                    i = nc.vector.scalar_tensor_tensor(out=xT[:, k, :], in0=bank[k // 2][:, (k % 2) * T:(k % 2 + 1) * T],
                                                       scalar=gate[:, at + k:at + k + 1], in1=xT[:, k, :],
                                                       op0=ALU.mult, op1=ALU.add)
                    if k % 2 == 1:
                        i.then_inc(sem(read), 1)
                dve.wait_ge(sem(read), 4)

            residual_sum("experts_done", "y_moe_read", mod, 40)

            def ff_rest(key, s, slot, half):
                dve.wait_ge(sem(f"{key}_w_hi"), s)
                nc.vector.tensor_tensor(ff_half(ff_w_lo[slot], half), ff_half(ring(slot), half), ff_half(ff_w_hi[slot], half),
                                        ALU.subtract).then_inc(sem(f"{key}_w_lo"), 1)

            def ff_out_rest(key, s, slot, half):
                dve.wait_ge(sem(f"{key}_out_hi"), s)
                part = slice(half * D, (half + 1) * D)
                nc.vector.tensor_tensor(ff_out_lo[slot][:, part], ring(slot)[:, part], ff_out_hi[slot][:, part], ALU.subtract)\
                  .then_inc(sem(f"{key}_out_lo"), 1)

            def ff_x_rest(key, shift_at):
                for k in range(KD):
                    dve.wait_ge(sem(f"{key}_ready"), k + 1)
                    nc.vector.scalar_tensor_tensor(out=ff_x_lo[:, k, :], in0=hT[:, k, :],
                                                   scalar=ada[:, shift_at + k:shift_at + k + 1], in1=ff_x_hi[:, k, :],
                                                   op0=ALU.add, op1=ALU.subtract).then_inc(sem(f"{key}_x_lo"), 1)

            copy_rows("row_ada0", 0)
            norm_root("fin1", "sum_final", rstd[:, 0:T])
            norm_gain("fin1", "final_g", col_a, rstd[:, 0:T])
            for i in range(4):
                if i < 3:
                    copy_rows(f"row_ada{i + 1}", (i + 1) % 2)
                row_col(f"col_ada{i}", ada[:, 4 * i:4 * i + 4], cols_b[:, 4 * i:4 * i + 4])
            job_done_here()
            make_gain("ffn1", cols_b[:, 72:80], ada[:, 8:16])
            dve.wait_ge(sem("fin1_ready"), KD)
            ff_rest("ffn1", 1, 2, 0)
            norm_root("ffn1", "sum_ffn1", rstd[:, 0:T])
            norm_scale("ffn1", xT, hT, rstd[:, 0:T])
            ff_x_rest("ffn1", 0)
            ff_rest("ffn1", 2, 2, 1)

            def feed_forward(key, with_ada, gate_at):
                split_out = not with_ada

                def act(s, parity):
                    dve.wait_ge(sem(f"{key}_silu"), s)
                    nc.vector.tensor_tensor(ff_act[:, parity, :], silu_g[:, parity, :], bank[4 + parity][:, T:2 * T],
                                            ALU.mult).then_inc(sem(f"{key}_act"), 1)

                def act_rest(s, parity):
                    dve.wait_ge(sem(f"{key}_act_hi"), s)
                    nc.vector.tensor_tensor(ff_act_lo[:, parity, :], ff_act[:, parity, :], ff_act_hi[:, parity, :],
                                            ALU.subtract).then_inc(sem(f"{key}_act_lo"), 1)

                if split_out:
                    ff_out_rest(key, 1, 3, 0)
                act(1, 0)
                if split_out:
                    act_rest(1, 0)
                    ff_out_rest(key, 2, 3, 1)
                with dve.Fori(0, FF_LOOPS) as it:
                    for j in range(4):
                        ff_rest(key, it * 4 + j + 3, 2 * (j // 2), j % 2)
                        act(it * 4 + j + 2, (j + 1) % 2)
                        if split_out:
                            act_rest(it * 4 + j + 2, (j + 1) % 2)
                            ff_out_rest(key, it * 4 + j + 3, 2 * (j // 2) + 1, j % 2)
                        if with_ada and j % 2 == 0:
                            u = j // 2
                            dve.wait_ge(sem(f"ada_full{4 + u}"), it * 16 + 16)
                            mod_item(ring(4 + u).rearrange("p (k n) -> p k n", k=KD), cond_2, u, it * 16 + 8 * (5 + u))
                        elif with_ada:
                            u = j // 2
                            dve.wait_ge(sem("ada_col_ready"), it * 2 + u + 1)
                            at = it * 8 + 16 + 4 * u
                            nc.vector.tensor_tensor(ada[:, bass.ds(at, 4)], bank[6 + u][:, 0:4], cols_b[:, bass.ds(at, 4)],
                                                    ALU.add).then_inc(sem("ada_col_read"), 1)
                act(4 * FF_LOOPS + 2, 1)
                if split_out:
                    act_rest(4 * FF_LOOPS + 2, 1)
                if with_ada:
                    n_item[0] += 2 * FF_LOOPS
                    dve.wait_ge(sem("ada_col_read"), 2 * FF_LOOPS)
                step(nc.vector.tensor_scalar(half_gate[:, :], ada[:, gate_at:gate_at + KD], 0.5, None, ALU.mult))
                residual_sum(f"{key}_sum_done", f"{key}_sum_read", half_gate, 0)

            dve.wait_ge(sem("bias_stored"), 16)
            feed_forward("ffn1", True, 16)
            make_gain("mix", cols_b[:, 80:88], ada[:, 32:40])
            norm_root("mix", "sum_mix", rstd[:, 0:T])
            norm_scale("mix", xT, hT, rstd[:, 0:T])
            take_job("z_lat")
            empty_job(nc.vector.tensor_copy(latT[:, 0:2, :], job_wide("z_lat")))
            b = take_job("z_kv")
            nc.vector.tensor_copy(latT[:, 2, :], b[:, 0:T])
            empty_job(nc.vector.tensor_copy(squares[0:96, 3, :], b[0:96, T:2 * T]))
            item("mid", "ada14")
            for i in range(2):
                take_job(f"z_caq{i}")
                empty_job(nc.vector.tensor_scalar(ca_q[:, 2 * i:2 * i + 2, :], job_wide(f"z_caq{i}"), 0.125, None, ALU.mult))
            ada_col("col_ada14", 14)
            item("mid", "ada15")
            for i in range(2):
                take_job(f"z_cak{i}")
                empty_job(nc.vector.tensor_copy(ca_k[:, 2 * i:2 * i + 2, :], job_wide(f"z_cak{i}")))
            ada_col("col_ada15", 15)
            item("mid", "ada16")
            for i in range(2):
                take_job(f"z_cav{i}")
                empty_job(nc.vector.tensor_copy(ca_v[:, i, :], job_bank(f"z_cav{i}")[:, :]))
            b = take_job("lat_sum")
            nc.vector.tensor_scalar(rstd[:, 0:T], b[:, 0:T], 1.0 / 256, None, ALU.mult)
            empty_job(nc.vector.tensor_scalar(rstd[:, T:2 * T], b[:, T:2 * T], 1.0 / P, None, ALU.mult))
            ada_col("col_ada16", 16)
            item("mid", "ada17")
            dve.wait_ge(sem("lat_root"), 1)
            step(nc.vector.reciprocal(rstd[:, :], rstd[:, :]))
            for c in range(3):
                i = nc.vector.scalar_tensor_tensor(out=latT[:, c, :], in0=latT[:, c, :],
                                                   scalar=cols_b[:, ROWS_B["mla_q_norm"] + c:ROWS_B["mla_q_norm"] + c + 1],
                                                   in1=rstd[:, (c // 2) * T:(c // 2 + 1) * T], op0=ALU.mult, op1=ALU.mult)
            i.then_inc(sem("lat_ready"), 1)
            for i in range(4):
                take_job(f"z_ga{i}")
                empty_job(nc.vector.tensor_copy(gate_aT[:, 2 * i:2 * i + 2, :], job_wide(f"z_ga{i}")))
            ada_col("col_ada17", 17)

            def take_gate_b(i):
                take_job(f"z_gb{i}_2")
                empty_job(nc.vector.tensor_copy(gate_bT[:, 2 * i:2 * i + 2, :], job_wide(f"z_gb{i}_2")))

            for i in range(4):
                take_job(f"mla_q{i}")
                empty_job(nc.vector.tensor_copy(mla_q[0:96, 2 * i:2 * i + 2, :], job_wide(f"mla_q{i}")[0:96, :, :]))
            for i in range(4):
                take_job(f"mla_k{i}")
                empty_job(nc.vector.tensor_copy(mla_k[0:64, 2 * i:2 * i + 2, :], job_wide(f"mla_k{i}")[0:64, :, :]))
            for i in range(2):
                take_job(f"mla_v{i}")
                empty_job(nc.vector.tensor_copy(mla_v[:, i, :], job_bank(f"mla_v{i}")[:, :]))
            take_gate_b(0)
            take_gate_b(1)
            dve.wait_ge(sem("rope_ready"), 1)
            pe3 = pe_tmp.rearrange("p (a t) -> p a t", a=2)[64:96, :, :]
            cos, sin = tables(rope_cs[64:96, 1, :], rope_cs[64:96, 0, :], 2)
            for i in range(4):
                take_job(f"pe_rot{i}")
                q = mla_q[64:96, 2 * i:2 * i + 2, :]
                empty_job(nc.vector.tensor_tensor(pe3, job_wide(f"pe_rot{i}")[64:96, :, :], sin, ALU.mult))
                step(nc.vector.tensor_tensor(q, q, cos, ALU.mult))
                step(nc.vector.tensor_tensor(q, q, pe3, ALU.add))
            b = take_job("kpe_rot")
            kpe = squares[64:96, 3, :]
            empty_job(nc.vector.tensor_tensor(pe_tmp[64:96, 0:T], b[64:96, 0:T], rope_cs[64:96, 0, :], ALU.mult))
            step(nc.vector.tensor_tensor(kpe, kpe, rope_cs[64:96, 1, :], ALU.mult))
            step(nc.vector.tensor_tensor(kpe, kpe, pe_tmp[64:96, 0:T], ALU.add))
            nc.vector.tensor_copy(mla_k[64:96, :, :], squares[64:96, 3:4, :].broadcast_to((32, 8, T)))\
              .then_inc(sem("mla_ready"), 1)
            take_gate_b(2)
            take_gate_b(3)
            attention("mla")
            attention("ca")
            dve.wait_ge(sem("gates_ready"), 2)
            for i in range(4):
                pair = slice(2 * i, 2 * i + 2)
                take_job(f"branch_a{i}")
                empty_job(nc.vector.tensor_tensor(hT[:, pair, :], gate_aT[:, pair, :], job_wide(f"branch_a{i}"), ALU.mult))
                take_job(f"branch_b{i}")
                empty_job(nc.vector.tensor_tensor(gate_bT[:, pair, :], gate_bT[:, pair, :], job_wide(f"branch_b{i}"), ALU.mult))
                job_done_here()
                nc.vector.tensor_tensor(hT[:, pair, :], hT[:, pair, :], gate_bT[:, pair, :], ALU.add)\
                  .then_inc(sem("merged_ready"), 1)
            for i in range(4):
                residual_job(f"out2_{i}", i, ada, 40)
            make_gain("ffn2", cols_b[:, 88:96], ada[:, 56:64])
            ff_rest("ffn2", 1, 2, 0)
            norm_root("ffn2", "sum_ffn2", rstd[:, 0:T])
            norm_scale("ffn2", xT, hT, rstd[:, 0:T])
            ff_x_rest("ffn2", 48)
            ff_rest("ffn2", 2, 2, 1)
            feed_forward("ffn2", False, 64)
            norm_root("last", "sum_last", rstd[:, 0:T])
            norm_gain("last", "final_norm", col_b, rstd[:, 0:T])
            for i in range(4):
                take_job(f"y_turn{i}")
                empty_job(nc.vector.tensor_copy(h_rows[:, i // 2, 512 * (i % 2):512 * (i % 2) + 512], job_bank(f"y_turn{i}")[:, :]))
            assert emptied[0] == len(JOBS)


_INS = ["x", "c", "ctx", "c_ctx", "w_mod", "b_mod", "norm1_g", "w_in", "q_norm_g", "k_norm_g", "conv_w", "attn_out_g",
        "conv_out_g", "w_out", "norm2_g", "w_group", "w_router", "w_gate", "w_up", "w_down", "final_g", "c_2",
        "positions_2", "w_ada_2", "b_ada_2", "ffn1_norm_2", "ffn1_w_in_2", "ffn1_w_out_2", "mix_norm_2", "w_in_2",
        "mla_q_norm_2", "mla_w_uq_2", "mla_kv_norm_2", "mla_w_ukv_2", "rel_bias_2", "w_branch_a_2",
        "w_branch_b_2", "w_out_2", "ffn2_norm_2", "ffn2_w_in_2", "ffn2_w_out_2", "final_norm_2"]


def shape_constants():
    import numpy as np

    offsets, width = const_offsets()
    out = np.zeros((P, width), np.float32)

    def put(name, value):
        at, n = offsets[name]
        out[:, at:at + n] = value

    i = np.arange(P)
    put("ident", np.eye(P))
    put("ones", 1.0)
    put("mean", 1.0 / D)
    put("heads64", (i[:, None] // 64 == i[None, :] // 64) / 64.0)
    put("select", i[:, None] % 32 == np.arange(2)[None, :])
    put("reverse", i[:, None] + i[None, :] == P - 1)
    put("before", i[:, None] < i[None, :])
    first = (i % 32) < 16
    rot = np.zeros((P, P))
    rot[i[first] + 16, i[first]] = -1.0
    rot[i[~first] - 16, i[~first]] = 1.0
    put("rot_axial", rot)
    half = np.zeros((P, P))
    half[64:96, 64:96] = rot[64:96, 64:96]
    put("rot_half", half)
    put("slot", np.tile(np.arange(SLOTS), 2)[None, :])
    put("expert_id", np.arange(N_EXPERTS)[None, :])
    put("group_rank", (N_GROUPS - np.arange(N_GROUPS))[None, :])
    put("eps", EPS)
    inv_freq = (np.float32(10000.0) ** (-np.arange(0, 32, 2, dtype=np.float32) / np.float32(32))).astype(np.float32)
    put("inv_freq", inv_freq[i % 16][:, None])
    t = np.arange(T)
    where = np.where((i[:, None] % 64) < 32, (t // 64)[None, :], (t % 64)[None, :]).astype(np.float32)
    angle = (where * inv_freq[i % 16][:, None]).astype(np.float32)
    put("axial_cos", np.cos(angle))
    put("axial_sin", np.sin(angle))
    return out


def kernel(**inputs):
    import numpy as _np
    import concourse.bacc as _bacc
    from concourse import mybir as _mybir
    from concourse.bass_utils import run_bass_kernel_spmd as _run

    nc = _bacc.Bacc("TRN2", target_bir_lowering=False, num_devices=1, dynamic_dma_scratch_size=4096)
    arrays, aps = {}, {}
    given = {name: _np.ascontiguousarray(inputs[name]) for name in _INS}
    given["shape_constants"] = shape_constants()

    def rows(*names):
        return _np.ascontiguousarray(_np.concatenate([_np.ravel(given[name]) for name in names]).reshape(-1, P))

    given["vectors_a"] = rows("b_mod", "norm1_g", "norm2_g", "final_g", "c", "c_ctx", "q_norm_g", "q_norm_g",
                              "k_norm_g", "k_norm_g", "attn_out_g", "conv_out_g", "conv_w")
    given["vectors_b"] = rows("b_ada_2", "ffn1_norm_2", "mix_norm_2", "ffn2_norm_2", "final_norm_2", "c_2",
                              "mla_q_norm_2", "mla_kv_norm_2")
    for name in ("b_mod", "norm1_g", "norm2_g", "final_g", "c", "c_ctx", "q_norm_g", "k_norm_g", "attn_out_g",
                 "conv_out_g", "conv_w", "b_ada_2", "ffn1_norm_2", "mix_norm_2", "ffn2_norm_2", "final_norm_2", "c_2",
                 "mla_q_norm_2", "mla_kv_norm_2"):
        del given[name]
    for name, a in given.items():
        arrays[f"in_{name}_dram"] = a
        aps[name] = nc.dram_tensor(f"in_{name}_dram", a.shape, _mybir.dt.from_np(a.dtype), kind="ExternalInput").ap()
    out = nc.dram_tensor("out_0_dram", (1, T, D), _mybir.dt.float32, kind="ExternalOutput").ap()
    mixed_blocks_kernel(nc, aps, out)
    r = _run(nc, [arrays], core_ids=[0])
    return r.results[0]["out_0_dram"]
```
